# Optimizing a Trainium2 kernel written in Bass

```python
import jax, jax.numpy as jnp
from jax import lax
import numpy as np
import math

D_MODEL = 1024
BATCH = 1
SEQ = 256
DEPTH = 2

GRID_W = 64
CTX_LEN = 256
GROUP_W = D_MODEL // 4
HEAD_DIM = 64
N_HEADS_GROUP = GROUP_W // HEAD_DIM
SC_KERNEL = 3
MLA_Q_RANK = 256
MLA_KV_RANK = 128
MLA_NOPE = 64
MLA_ROPE = 32
MLA_V = 64
MLA_SCALE = (MLA_NOPE + MLA_ROPE) ** -0.5
Q_BLOCK = 128
CF_KERNEL = 31
NA_ROWS = 8
NA_COLS = 16
NA_SCALE = HEAD_DIM ** -0.5
ROPE_BASE = 10000.0
MLP_HIDDEN = 4 * D_MODEL
N_MOD = 6
EPS = 1e-6

SC_END = 3 * GROUP_W
MLA_Q_END = SC_END + MLA_Q_RANK
MLA_KV_END = MLA_Q_END + MLA_KV_RANK + MLA_ROPE
CF_END = MLA_KV_END + 2 * GROUP_W
NA_Q_END = CF_END + GROUP_W
P_IN = NA_Q_END + 2 * GROUP_W


def rmsnorm(x, g):
    xf = x.astype(jnp.float32)
    y = xf * lax.rsqrt(jnp.mean(xf * xf, axis=-1, keepdims=True) + EPS)
    return y.astype(x.dtype) * g

def layernorm(x, g, b):
    xf = x.astype(jnp.float32)
    mu = jnp.mean(xf, axis=-1, keepdims=True)
    var = jnp.mean(jnp.square(xf - mu), axis=-1, keepdims=True)
    return ((xf - mu) * lax.rsqrt(var + EPS)).astype(x.dtype) * g + b

def dwconv(x, w):
    k = w.shape[0]
    return lax.conv_general_dilated(
        x, w[:, None, :], window_strides=(1,), padding=[(k // 2, k // 2)],
        dimension_numbers=("NWC", "WIO", "NWC"), feature_group_count=x.shape[-1])

def heads(t):
    return t.reshape(*t.shape[:-1], N_HEADS_GROUP, -1)

def rope_rotate(x, ang):
    x1, x2 = jnp.split(x, 2, axis=-1)
    cos, sin = jnp.cos(ang).astype(x.dtype), jnp.sin(ang).astype(x.dtype)
    return jnp.concatenate([x1 * cos - x2 * sin, x1 * sin + x2 * cos], axis=-1)

def axial_rope(x, ang_row, ang_col):
    xr, xc = jnp.split(x, 2, axis=-1)
    return jnp.concatenate([rope_rotate(xr, ang_row), rope_rotate(xc, ang_col)], axis=-1)

def short_conv_mixer(u_sc, w_sc):
    x_in, b_gate, c_gate = jnp.split(u_sc, 3, axis=-1)
    return b_gate * dwconv(c_gate * x_in, w_sc)

def conformer_conv_mixer(u_cf, w_dw, b_dw, ln_g, ln_b, w_pw):
    a, g = jnp.split(u_cf, 2, axis=-1)
    y = dwconv(a * jax.nn.sigmoid(g), w_dw) + b_dw
    return jax.nn.silu(layernorm(y, ln_g, ln_b)) @ w_pw

def mla_queries(cq, g_q, w_uq):
    q = heads(rmsnorm(cq, g_q) @ w_uq)
    return q[..., :MLA_NOPE], q[..., MLA_NOPE:]

def mla_keys_values(u_kv, g_kv, w_ukv):
    ckv, k_rope = u_kv[..., :MLA_KV_RANK], u_kv[..., MLA_KV_RANK:]
    kv = heads(rmsnorm(ckv, g_kv) @ w_ukv)
    return kv[..., :MLA_NOPE], k_rope, kv[..., MLA_NOPE:]

def mla_attend(qn, qr, kn, kr, v):
    s = (jnp.einsum("bqhd,bkhd->bhqk", qn, kn)
         + jnp.einsum("bqhr,bkr->bhqk", qr, kr)) * MLA_SCALE
    p = jax.nn.softmax(s.astype(jnp.float32), axis=-1).astype(v.dtype)
    return jnp.einsum("bhqk,bkhd->bqhd", p, v)

def mla_latent(qn, qr, kn, kr, v):
    b, l = qn.shape[:2]
    nb = l // Q_BLOCK

    def to_blocks(t):
        return jnp.moveaxis(t.reshape(b, nb, Q_BLOCK, *t.shape[2:]), 1, 0)

    out = lax.map(lambda qs: mla_attend(qs[0], qs[1], kn, kr, v), (to_blocks(qn), to_blocks(qr)))
    return jnp.moveaxis(out, 0, 1).reshape(b, l, -1)

def dense_attend(q, k, v):
    s = jnp.einsum("bqhd,bkhd->bhqk", q, k) * NA_SCALE
    p = jax.nn.softmax(s.astype(jnp.float32), axis=-1).astype(v.dtype)
    o = jnp.einsum("bhqk,bkhd->bqhd", p, v)
    return o.reshape(*o.shape[:2], -1)

def neighbourhood_attend(q, k, v, k_c, v_c, rpb):
    b, l, h, dh = q.shape
    rows = l // GRID_W
    wh = min(NA_ROWS, rows)
    r = jnp.arange(rows)
    row_idx = jnp.clip(r - wh // 2, 0, rows - wh)[:, None] + jnp.arange(wh)[None, :]
    col = jnp.arange(GRID_W)
    col_start = jnp.clip(col - NA_COLS // 2, 0, GRID_W - NA_COLS)
    in_win = (col[None, :] >= col_start[:, None]) & (col[None, :] < col_start[:, None] + NA_COLS)
    off_r = row_idx - r[:, None] + (NA_ROWS - 1)
    off_c = jnp.clip(col[None, :] - col[:, None] + (NA_COLS - 1), 0, 2 * NA_COLS - 2)
    bias = rpb[:, off_r[:, None, :, None], off_c[None, :, None, :]]

    qg = q.reshape(b, rows, GRID_W, h, dh)
    kw = k.reshape(b, rows, GRID_W, h, dh)[:, row_idx]
    vw = v.reshape(b, rows, GRID_W, h, dh)[:, row_idx]
    s_loc = (jnp.einsum("brqhd,brikhd->bhrqik", qg, kw).astype(jnp.float32) * NA_SCALE
             + bias.astype(jnp.float32)[None])
    s_loc = jnp.where(in_win[:, None, :], s_loc, -jnp.inf)
    s_ctx = jnp.einsum("brqhd,bchd->bhrqc", qg, k_c).astype(jnp.float32) * NA_SCALE
    n_loc = wh * GRID_W
    p = jax.nn.softmax(
        jnp.concatenate([s_loc.reshape(b, h, rows, GRID_W, n_loc), s_ctx], axis=-1),
        axis=-1).astype(v.dtype)
    out = (jnp.einsum("bhrqik,brikhd->brqhd",
                      p[..., :n_loc].reshape(b, h, rows, GRID_W, wh, GRID_W), vw)
           + jnp.einsum("bhrqc,bchd->brqhd", p[..., n_loc:], v_c))
    return out.reshape(b, l, h * dh)

def sq_relu_mlp(h, w1, w2):
    return jnp.square(jax.nn.relu(h @ w1)) @ w2

def trunk_layer(x, xc, mod, mod_c, p, ang_row, ang_col, last):
    sh1, sc1, ga1, sh2, sc2, ga2 = mod
    sh1c, sc1c, ga1c, sh2c, sc2c, ga2c = mod_c
    w_in = p["w_in"]

    h = rmsnorm(x, p["g_pre_mix"]) * (1 + sc1) + sh1
    hc = rmsnorm(xc, p["g_pre_mix"]) * (1 + sc1c) + sh1c
    u = h @ w_in
    if last:
        uc_mla_kv = hc @ w_in[:, MLA_Q_END:MLA_KV_END]
        uc_na_kv = hc @ w_in[:, NA_Q_END:]
    else:
        uc = hc @ w_in
        uc_mla_kv, uc_na_kv = uc[..., MLA_Q_END:MLA_KV_END], uc[..., NA_Q_END:]

    kn_c, kr_c, v_c = mla_keys_values(uc_mla_kv, p["g_kv"], p["w_ukv"])
    nk_c, nv_c = (heads(t) for t in jnp.split(uc_na_kv, 2, axis=-1))

    y_sc = short_conv_mixer(u[..., :SC_END], p["w_sc"])
    qn, qr = mla_queries(u[..., SC_END:MLA_Q_END], p["g_q"], p["w_uq"])
    qr = axial_rope(qr, ang_row[:, None], ang_col[:, None])
    kn, kr, v = mla_keys_values(u[..., MLA_Q_END:MLA_KV_END], p["g_kv"], p["w_ukv"])
    kr = axial_rope(kr, ang_row, ang_col)
    y_mla = mla_latent(qn, qr, jnp.concatenate([kn, kn_c], axis=1),
                       jnp.concatenate([kr, kr_c], axis=1), jnp.concatenate([v, v_c], axis=1))
    y_cf = conformer_conv_mixer(u[..., MLA_KV_END:CF_END], p["cf_w_dw"], p["cf_b_dw"],
                                p["cf_ln_g"], p["cf_ln_b"], p["cf_w_pw"])
    nq, nk, nv = (heads(t) for t in jnp.split(u[..., CF_END:], 3, axis=-1))
    y_na = neighbourhood_attend(nq, nk, nv, nk_c, nv_c, p["na_rpb"])
    y = jnp.concatenate([y_sc, y_mla, y_cf, y_na], axis=-1) @ p["w_out"]
    x = x + ga1 * rmsnorm(y, p["g_post_mix"])

    if not last:
        yc_sc = short_conv_mixer(uc[..., :SC_END], p["w_sc"])
        qn_c, qr_c = mla_queries(uc[..., SC_END:MLA_Q_END], p["g_q"], p["w_uq"])
        yc_mla = mla_attend(qn_c, qr_c, kn_c, kr_c, v_c)
        yc_mla = yc_mla.reshape(*yc_mla.shape[:2], -1)
        yc_cf = conformer_conv_mixer(uc[..., MLA_KV_END:CF_END], p["cf_w_dw"], p["cf_b_dw"],
                                     p["cf_ln_g"], p["cf_ln_b"], p["cf_w_pw"])
        yc_na = dense_attend(heads(uc[..., CF_END:NA_Q_END]), nk_c, nv_c)
        yc = jnp.concatenate([yc_sc, yc_mla, yc_cf, yc_na], axis=-1) @ p["w_out"]
        xc = xc + ga1c * rmsnorm(yc, p["g_post_mix"])

    hm = rmsnorm(x, p["g_pre_mlp"]) * (1 + sc2) + sh2
    x = x + ga2 * rmsnorm(sq_relu_mlp(hm, p["w_mlp1"], p["w_mlp2"]), p["g_post_mlp"])
    if not last:
        hmc = rmsnorm(xc, p["g_pre_mlp"]) * (1 + sc2c) + sh2c
        xc = xc + ga2c * rmsnorm(sq_relu_mlp(hmc, p["w_mlp1"], p["w_mlp2"]), p["g_post_mlp"])
    return x, xc

def first_inputs(seed: int = 0) -> dict:
    key = jax.random.key(seed)
    ks = jax.random.split(key, 25)
    f32 = jnp.float32

    def nrm(k, shape, s):
        return jax.random.normal(k, shape, f32) * s

    def gain(k, shape):
        return 1.0 + 0.1 * jax.random.normal(k, shape, f32)

    L, H = DEPTH, N_HEADS_GROUP
    return {
        "x": nrm(ks[0], (BATCH, SEQ, D_MODEL), 1.0),
        "c": nrm(ks[1], (BATCH, D_MODEL), 1.0),
        "ctx": nrm(ks[2], (BATCH, CTX_LEN, D_MODEL), 1.0),
        "c_ctx": nrm(ks[3], (D_MODEL,), 1.0),
        "w_mod": nrm(ks[4], (L, D_MODEL, N_MOD * D_MODEL), 0.5 * D_MODEL ** -0.5),
        "b_mod": nrm(ks[5], (L, N_MOD * D_MODEL), 0.02),
        "g_pre_mix": gain(ks[6], (L, D_MODEL)),
        "w_in": nrm(ks[7], (L, D_MODEL, P_IN), D_MODEL ** -0.5),
        "w_sc": nrm(ks[8], (L, SC_KERNEL, GROUP_W), SC_KERNEL ** -0.5),
        "g_q": gain(ks[9], (L, MLA_Q_RANK)),
        "w_uq": nrm(ks[10], (L, MLA_Q_RANK, H * (MLA_NOPE + MLA_ROPE)), MLA_Q_RANK ** -0.5),
        "g_kv": gain(ks[11], (L, MLA_KV_RANK)),
        "w_ukv": nrm(ks[12], (L, MLA_KV_RANK, H * (MLA_NOPE + MLA_V)), MLA_KV_RANK ** -0.5),
        "cf_w_dw": nrm(ks[13], (L, CF_KERNEL, GROUP_W), CF_KERNEL ** -0.5),
        "cf_b_dw": nrm(ks[14], (L, GROUP_W), 0.02),
        "cf_ln_g": gain(ks[15], (L, GROUP_W)),
        "cf_ln_b": nrm(ks[16], (L, GROUP_W), 0.02),
        "cf_w_pw": nrm(ks[17], (L, GROUP_W, GROUP_W), GROUP_W ** -0.5),
        "na_rpb": nrm(ks[18], (L, H, 2 * NA_ROWS - 1, 2 * NA_COLS - 1), 0.1),
        "w_out": nrm(ks[19], (L, D_MODEL, D_MODEL), D_MODEL ** -0.5),
        "g_post_mix": gain(ks[20], (L, D_MODEL)),
        "g_pre_mlp": gain(ks[21], (L, D_MODEL)),
        "w_mlp1": nrm(ks[22], (L, D_MODEL, MLP_HIDDEN), D_MODEL ** -0.5),
        "w_mlp2": nrm(ks[23], (L, MLP_HIDDEN, D_MODEL), MLP_HIDDEN ** -0.5),
        "g_post_mlp": gain(ks[24], (L, D_MODEL)),
    }

def first_block(x, c, ctx, c_ctx, w_mod, b_mod, g_pre_mix, w_in, w_sc, g_q, w_uq, g_kv, w_ukv,
              cf_w_dw, cf_b_dw, cf_ln_g, cf_ln_b, cf_w_pw, na_rpb, w_out, g_post_mix,
              g_pre_mlp, w_mlp1, w_mlp2, g_post_mlp):
    l = x.shape[1]
    pos = jnp.arange(l)
    n_freq = MLA_ROPE // 4
    inv_freq = ROPE_BASE ** (-jnp.arange(n_freq, dtype=jnp.float32) / n_freq)
    ang_row = (pos // GRID_W).astype(jnp.float32)[:, None] * inv_freq
    ang_col = (pos % GRID_W).astype(jnp.float32)[:, None] * inv_freq

    xc = ctx
    for i in range(DEPTH):
        mod = [m[:, None, :] for m in jnp.split(jax.nn.silu(c) @ w_mod[i] + b_mod[i], N_MOD, axis=-1)]
        mod_c = jnp.split(jax.nn.silu(c_ctx) @ w_mod[i] + b_mod[i], N_MOD, axis=-1)
        p = {
            "g_pre_mix": g_pre_mix[i], "w_in": w_in[i], "w_sc": w_sc[i],
            "g_q": g_q[i], "w_uq": w_uq[i], "g_kv": g_kv[i], "w_ukv": w_ukv[i],
            "cf_w_dw": cf_w_dw[i], "cf_b_dw": cf_b_dw[i], "cf_ln_g": cf_ln_g[i],
            "cf_ln_b": cf_ln_b[i], "cf_w_pw": cf_w_pw[i], "na_rpb": na_rpb[i],
            "w_out": w_out[i], "g_post_mix": g_post_mix[i], "g_pre_mlp": g_pre_mlp[i],
            "w_mlp1": w_mlp1[i], "w_mlp2": w_mlp2[i], "g_post_mlp": g_post_mlp[i],
        }
        x, xc = trunk_layer(x, xc, mod, mod_c, p, ang_row, ang_col, last=(i == DEPTH - 1))
    return x


DEPTH_2 = 1

A_HEADS = 4
A_QK_DIM = 64
A_V_DIM = 2 * A_QK_DIM
A_WIDTH = A_HEADS * A_V_DIM
B_PAIRS = ((128, 1), (512, 4), (2048, 16))
B_GROUPS = len(B_PAIRS)
B_HEADS = 4
B_HEAD_DIM = 128
B_WIDTH = B_HEADS * B_HEAD_DIM
B_BLOCK = 128
A_Q_COLS = A_HEADS * 2 * A_QK_DIM
A_K_COLS = A_HEADS * 2 * A_QK_DIM
A_V_COLS = A_HEADS * A_V_DIM
B_COLS = B_GROUPS * B_WIDTH
GATE_COLS = 2 * D_MODEL
IN_COLS = A_Q_COLS + A_K_COLS + A_V_COLS + 3 * B_COLS + GATE_COLS
D_FF = 2816
CONV_WIDTH = 3
ROPE_THETA = 10000.0
NORM_EPS = 1e-6


def rms_norm(x, g):
    xf = x.astype(jnp.float32)
    y = xf * lax.rsqrt(jnp.mean(xf * xf, axis=-1, keepdims=True) + NORM_EPS)
    return (y * g.astype(jnp.float32)).astype(x.dtype)

def rope_tables(positions, dim):
    inv = ROPE_THETA ** (-jnp.arange(0, dim, 2, dtype=jnp.float32) / dim)
    ang = positions.astype(jnp.float32)[..., None] * inv
    return jnp.cos(ang)[:, :, None, None, :], jnp.sin(ang)[:, :, None, None, :]

def apply_rope(t, cos, sin):
    tf = t.astype(jnp.float32)
    t1, t2 = jnp.split(tf, 2, axis=-1)
    return jnp.concatenate([t1 * cos - t2 * sin, t2 * cos + t1 * sin], axis=-1).astype(t.dtype)

def diff_attention(q, k, v, lam):
    b, s, h, _, dqk = q.shape
    nq = s // Q_BLOCK
    scale = dqk ** -0.5
    qb = q.reshape(b, nq, Q_BLOCK, h, 2, dqk).transpose(1, 0, 2, 3, 4, 5)
    kpos = jnp.arange(s)

    def one_block(args):
        qi, i = args
        sc = jnp.einsum('bqhcd,bkhcd->bchqk', qi, k).astype(jnp.float32) * scale
        qpos = i * Q_BLOCK + jnp.arange(Q_BLOCK)
        causal = kpos[None, :] <= qpos[:, None]
        p = jax.nn.softmax(jnp.where(causal, sc, -jnp.inf), axis=-1)
        a = p[:, 0] - lam * p[:, 1]
        return jnp.einsum('bhqk,bkhd->bqhd', a.astype(v.dtype), v)

    o = lax.map(one_block, (qb, jnp.arange(nq)))
    return o.transpose(1, 0, 2, 3, 4).reshape(b, s, h, v.shape[-1])

def dilated_group(q, k, v, window, dil):
    b, s, h, d = q.shape
    L = s // dil
    nwin = window // dil
    nb = -(-L // B_BLOCK)
    Lp = nb * B_BLOCK

    def to_blocks(t):
        t = t.reshape(b, L, dil, h, d).transpose(0, 2, 1, 3, 4)
        t = jnp.pad(t, ((0, 0), (0, 0), (0, Lp - L), (0, 0), (0, 0)))
        return t.reshape(b, dil, nb, B_BLOCK, h, d)

    def with_prev(t):
        prev = jnp.pad(t[:, :, :-1], ((0, 0), (0, 0), (1, 0), (0, 0), (0, 0), (0, 0)))
        return jnp.concatenate([prev, t], axis=3)

    qb, kb, vb = to_blocks(q), to_blocks(k), to_blocks(v)
    kk, vv = with_prev(kb), with_prev(vb)
    sc = jnp.einsum('brnqhd,brnkhd->brnhqk', qb, kk).astype(jnp.float32) * (d ** -0.5)
    qi = jnp.arange(B_BLOCK)[:, None]
    kj = jnp.arange(2 * B_BLOCK)[None, :]
    rel = qi - kj + B_BLOCK
    kabs = jnp.arange(nb)[:, None, None] * B_BLOCK + kj - B_BLOCK
    valid = (rel >= 0) & (rel <= nwin) & (kabs >= 0)
    sc = jnp.where(valid[None, None, :, None], sc, -jnp.inf)
    m = jnp.max(sc, axis=-1, keepdims=True)
    p = jnp.exp(sc - m)
    den = jnp.sum(p, axis=-1, keepdims=True)
    o = jnp.einsum('brnhqk,brnkhd->brnqhd', (p / den).astype(v.dtype), vv)
    lse = (m + jnp.log(den))[..., 0].transpose(0, 1, 2, 4, 3)

    def from_blocks(t):
        t = t.reshape((b, dil, Lp) + t.shape[4:])[:, :, :L]
        t = jnp.moveaxis(t, 1, 2)
        return t.reshape((b, s) + t.shape[3:])

    return from_blocks(o), from_blocks(lse)

def causal_depthwise_conv(u, w, bias):
    s = u.shape[1]
    up = jnp.pad(u, ((0, 0), (CONV_WIDTH - 1, 0), (0, 0)))
    out = sum(up[:, j:j + s] * w[j] for j in range(CONV_WIDTH))
    return out + bias

def second_inputs(seed: int = 0) -> dict:
    key = jax.random.key(seed)
    ks = jax.random.split(key, 20)
    f32 = jnp.float32

    def nrm(k, shape, scale):
        return jax.random.normal(k, shape, f32) * scale

    def gain(k, shape):
        return 1.0 + 0.05 * jax.random.normal(k, shape, f32)

    x = jax.random.normal(ks[0], (BATCH, SEQ, D_MODEL), f32)
    offset = jax.random.randint(ks[1], (BATCH, 1), 0, 1024, dtype=jnp.int32)
    positions = (offset + jnp.arange(SEQ, dtype=jnp.int32)[None, :]).astype(jnp.int32)
    return {
        "x": x,
        "positions": positions,
        "pre_mix_g": gain(ks[2], (DEPTH_2, D_MODEL)),
        "w_in": nrm(ks[3], (DEPTH_2, D_MODEL, IN_COLS), D_MODEL ** -0.5),
        "diff_lambda": nrm(ks[4], (DEPTH_2, 4, A_QK_DIM), 0.1),
        "diff_head_g": gain(ks[5], (DEPTH_2, A_V_DIM)),
        "w_a_out": nrm(ks[6], (DEPTH_2, A_WIDTH, D_MODEL), A_WIDTH ** -0.5),
        "w_b_out": nrm(ks[7], (DEPTH_2, B_WIDTH, D_MODEL), B_WIDTH ** -0.5),
        "w_mix_out": nrm(ks[8], (DEPTH_2, D_MODEL, D_MODEL), D_MODEL ** -0.5),
        "post_mix_g": gain(ks[9], (DEPTH_2, D_MODEL)),
        "pre_ffn_g": gain(ks[10], (DEPTH_2, D_MODEL)),
        "w_up": nrm(ks[11], (DEPTH_2, D_MODEL, 2 * D_FF), D_MODEL ** -0.5),
        "conv_w": nrm(ks[12], (DEPTH_2, CONV_WIDTH, 2 * D_FF), CONV_WIDTH ** -0.5),
        "conv_b": nrm(ks[13], (DEPTH_2, 2 * D_FF), 0.01),
        "w_down": nrm(ks[14], (DEPTH_2, D_FF, D_MODEL), D_FF ** -0.5),
        "post_ffn_g": gain(ks[15], (DEPTH_2, D_MODEL)),
    }

def second_block(x, positions, pre_mix_g, w_in, diff_lambda, diff_head_g, w_a_out, w_b_out,
              w_mix_out, post_mix_g, pre_ffn_g, w_up, conv_w, conv_b, w_down, post_ffn_g):
    b, s, _ = x.shape
    cos_a, sin_a = rope_tables(positions, A_QK_DIM)
    cos_b, sin_b = rope_tables(positions, B_HEAD_DIM)
    split_at = np.cumsum([A_Q_COLS, A_K_COLS, A_V_COLS, B_COLS, B_COLS, B_COLS]).tolist()

    for l in range(DEPTH_2):
        h = rms_norm(x, pre_mix_g[l])
        proj = h @ w_in[l]
        qa, ka, va, qb, kb, vb, gates = jnp.split(proj, split_at, axis=-1)

        qa = apply_rope(qa.reshape(b, s, A_HEADS, 2, A_QK_DIM), cos_a, sin_a)
        ka = apply_rope(ka.reshape(b, s, A_HEADS, 2, A_QK_DIM), cos_a, sin_a)
        va = va.reshape(b, s, A_HEADS, A_V_DIM)
        lam_init = 0.8 - 0.6 * math.exp(-0.3 * l)
        lv = diff_lambda[l].astype(jnp.float32)
        lam = jnp.exp(jnp.sum(lv[0] * lv[1])) - jnp.exp(jnp.sum(lv[2] * lv[3])) + lam_init
        oa = diff_attention(qa, ka, va, lam)
        oa = rms_norm(oa, diff_head_g[l]) * (1.0 - lam_init)
        ya = oa.reshape(b, s, A_WIDTH) @ w_a_out[l]

        qb = apply_rope(qb.reshape(b, s, B_GROUPS, B_HEADS, B_HEAD_DIM), cos_b, sin_b)
        kb = apply_rope(kb.reshape(b, s, B_GROUPS, B_HEADS, B_HEAD_DIM), cos_b, sin_b)
        vb = vb.reshape(b, s, B_GROUPS, B_HEADS, B_HEAD_DIM)
        outs, lses = [], []
        for g, (window, dil) in enumerate(B_PAIRS):
            o_g, lse_g = dilated_group(qb[:, :, g], kb[:, :, g], vb[:, :, g], window, dil)
            outs.append(o_g)
            lses.append(lse_g)
        wts = jax.nn.softmax(jnp.stack(lses, axis=0), axis=0)
        ob = jnp.einsum('gbsh,gbshd->bshd', wts.astype(x.dtype), jnp.stack(outs, axis=0))
        yb = ob.reshape(b, s, B_WIDTH) @ w_b_out[l]

        g_a, g_b = jnp.split(jax.nn.sigmoid(gates), 2, axis=-1)
        mix = (g_a * ya + g_b * yb) @ w_mix_out[l]
        x = x + rms_norm(mix, post_mix_g[l])

        h = rms_norm(x, pre_ffn_g[l])
        u = causal_depthwise_conv(h @ w_up[l], conv_w[l], conv_b[l])
        gate, val = jnp.split(u, 2, axis=-1)
        y = (jax.nn.gelu(gate, approximate=True) * val) @ w_down[l]
        x = x + rms_norm(y, post_ffn_g[l])
    return x


def setup_inputs(seed=0):
    out = dict(first_inputs(seed))
    for name, value in second_inputs(seed + 1).items():
        if name != "x":
            out[name + "_2"] = value
    return out


def reference(
    x, c, ctx, c_ctx, w_mod, b_mod, g_pre_mix, w_in, w_sc, g_q, w_uq, g_kv, w_ukv, cf_w_dw,
    cf_b_dw, cf_ln_g, cf_ln_b, cf_w_pw, na_rpb, w_out, g_post_mix, g_pre_mlp, w_mlp1, w_mlp2,
    g_post_mlp, positions_2, pre_mix_g_2, w_in_2, diff_lambda_2, diff_head_g_2, w_a_out_2,
    w_b_out_2, w_mix_out_2, post_mix_g_2, pre_ffn_g_2, w_up_2, conv_w_2, conv_b_2, w_down_2,
    post_ffn_g_2,
):
    x = first_block(
        x, c, ctx, c_ctx, w_mod, b_mod, g_pre_mix, w_in, w_sc, g_q, w_uq, g_kv, w_ukv, cf_w_dw,
        cf_b_dw, cf_ln_g, cf_ln_b, cf_w_pw, na_rpb, w_out, g_post_mix, g_pre_mlp, w_mlp1,
        w_mlp2, g_post_mlp,
    )
    return second_block(
        x, positions_2, pre_mix_g_2, w_in_2, diff_lambda_2, diff_head_g_2, w_a_out_2, w_b_out_2,
        w_mix_out_2, post_mix_g_2, pre_ffn_g_2, w_up_2, conv_w_2, conv_b_2, w_down_2,
        post_ffn_g_2,
    )


_drawn_inputs = setup_inputs


def setup_inputs(seed=0):
    import zlib

    import numpy as np

    out = dict(_drawn_inputs(seed))
    spreads = {}
    factors = {'g_q': 8.0,
     'g_kv': 3.326,
     'cf_b_dw': 3.828,
     'cf_ln_b': 5.745,
     'na_rpb': 38.264,
     'conv_b_2': 7.253,
     'cf_ln_g': 2.827}
    for name, (base, spread) in spreads.items():
        noise = np.random.default_rng([zlib.crc32(name.encode()), seed]).standard_normal(out[name].shape)
        drawn = base * np.exp(spread * noise) if base else spread * noise
        out[name] = __import__('jax').numpy.asarray(drawn.astype(out[name].dtype))
    for name, factor in factors.items():
        out[name] = (out[name] * factor).astype(out[name].dtype)
    return out
```

```python
import numpy as np
from contextlib import ExitStack

import concourse.bass as bass
from concourse import mybir

D = 1024
SEQ = 256
CTX = 256
NT_ALL = SEQ + CTX
DEPTH = 2
KT = D // 128
GRID = 64
RPB = 15 * 31
HEADS = 4
MLA_SCALE = 96 ** -0.5
NA_SCALE = 64 ** -0.5
CF_K = 31
EPS = 1e-6
MASKED = -1e30
FF2 = 2816
LAM_INIT = 0.2
CHUNK = 2048
HALF = CHUNK // 2
SLOTS = 4

WIN = ["cf_a", "cf_g", "kv", "q", "nk", "nq", "nv", "sc_x", "sc_c", "sc_b"]
WIN_ALL_TOKENS = ("kv", "nk", "nv")
GROUPS1 = 4
GROUPS2 = [4, 4, 3]


def chunk_kinds():
    kinds, first = [], {}

    def add(key, names):
        first[key] = len(kinds)
        kinds.extend(names)

    for l in range(DEPTH):
        add(("mod", l), ["mod"] * 24)
        add(("win", l), WIN)
        add(("out", l), ["out"] * 4)
        add(("mlp", l), (["up"] * 4 + ["down"] * 4) * GROUPS1)
    add("proj2", ["qa", "qa", "ka", "ka", "va", "va"] + ["qb"] * 6 + ["kb"] * 6 + ["vb"] * 6)
    add("gates2", ["gate"] * 8)
    add("mix2", ["a_out"] * 2 + ["b_out"] * 2 + ["mix"] * 4)
    for g, steps in enumerate(GROUPS2):
        add(("ffn", g), ["up_gate", "up_val"] * steps + ["down2"] * 4)
    return kinds, first


KINDS, FIRST = chunk_kinds()
N_CHUNKS = len(KINDS)
ACT_READS = {"cf_a", "cf_g", "kv", "q", "nk", "nq", "nv", "sc_x", "sc_b", "out", "up", "va", "vb", "gate",
             "mix", "up_gate", "up_val"}
DVE_READS = {"mod", "cf_a", "kv", "q", "nk", "nq", "nv", "sc_x", "sc_c", "sc_b", "out", "down", "qa", "ka",
             "va", "qb", "kb", "vb", "a_out", "b_out", "mix", "up_gate", "up_val", "down2"}


def running(of):
    total, out = 0, []
    for k in KINDS:
        total += k in of
        out.append(total)
    return out + [total] * 2


ACT_READ_COUNT = running(ACT_READS)
DVE_READ_COUNT = running(DVE_READS)


class At:

    def __init__(self, first, per=0, i=0):
        self.first, self.per, self.i = first, per, i

    def __add__(self, n):
        return At(self.first + n, self.per, self.i)

    def value(self, count):
        if not self.per:
            return count(self.first)
        step = count(self.first + self.per + 2) - count(self.first + 2)
        return self.i * step + (count(self.first + self.per) - step)

    @property
    def slot(self):
        return self.first % SLOTS

    @property
    def pair(self):
        return self.first % 2


def feature_columns():
    cols, at = {}, 0

    def add(key, n):
        nonlocal at
        cols[key] = at
        at += n

    add("c", 16)
    for l in range(DEPTH):
        for key, n in (("g_pre_mix", 8), ("g_pre_mlp", 8), ("w_sc", 6), ("g_q", 2), ("g_kv", 1),
                       ("cf_w", 62), ("cf_b", 2), ("ln_g", 2), ("ln_b", 2)):
            add((key, l), n)
    for key, n in (("pre_mix2", 8), ("pre_ffn2", 8), ("conv_w2", 132), ("conv_b2", 44), ("head_g2", 1)):
        add(key, n)
    cols["n"] = at
    return cols


FC = feature_columns()
C_IDENT, C_ONES, C_SWAP, C_COS, C_SIN, C_INV, C_EPS, C_ZERO, C_SIGN = 0, 128, 256, 384, 640, 896, 898, 899, 900
C_N = 902

f32, f32r, i32 = mybir.dt.float32, mybir.dt.float32r, mybir.dt.int32
ALU, ACT, AX = mybir.AluOpType, mybir.ActivationFunctionType, mybir.AxisListType
SMALL_N = 2 * 384 + 512 + 512



FIRST_LAYER = {"rows_in": 64, "small_in": 16, "bias_in": 17 * 16, "gate_rows": 2, "gates": 4, "latent_sq": 2,
               "mla_in": 2, "cf_y": 2, "sc_y": 2, "hidden": 16, "squared": 16}
FIRST_LAYER.update({step: 16 for step in ("scores", "nmax", "exp", "p", "pt_mm", "pt_act", "pt_dve", "o_mm", "o_hi",
                                          "o_lo")})


class Core:

    def __init__(self, nc, stack):
        def sb(name, shape, dt=f32, to=stack):
            return to.enter_context(nc.sbuf_tensor(name, shape, dt))

        def sem(name):
            return stack.enter_context(nc.semaphore(name))

        self.nc = nc
        loaded = ExitStack()
        self.w = sb("w", [128, SLOTS, CHUNK], f32, loaded)
        loaded.close()
        self.w_lo = sb("w_lo", [128, SLOTS, CHUNK], f32r)
        self.w_hi = sb("w_hi", [128, SLOTS, CHUNK], f32r)
        self.X = sb("X", [128, 4, D])
        self.Y = sb("Y", [128, 4, D])
        self.h_hi = sb("h_hi", [128, KT * NT_ALL], f32r)
        self.h_lo = sb("h_lo", [128, KT * NT_ALL], f32r)
        self.GA = sb("GA", [128, 4, D])
        self.F = sb("F", [128, FC["n"]])
        self.C = sb("C", [128, C_N])
        self.SW = sb("SW", [128, SMALL_N])
        self.tiny = sb("tiny", [128, 128])
        self.cs_hi = sb("cs_hi", [128, 16], f32r)
        self.cs_lo = sb("cs_lo", [128, 16], f32r)
        self.mod_feat = sb("mod_feat", [128, 64])
        self.mod_gain = sb("mod_gain", [128, 32])
        attention = ExitStack()
        self.U = sb("U", [128, 12416], f32, attention)
        attention.close()
        self.g_hi = sb("g_hi", [128, KT * NT_ALL], f32r)
        self.g_lo = sb("g_lo", [128, KT * NT_ALL], f32r)
        self.R = sb("R", [128, 2, 1024])
        self.hf = sb("hf", [128, 2, 1024])
        self.ps = stack.enter_context(nc.psum_tensor("ps", [128, 8, 512], f32))

        self.w_loaded = [sem(f"w_loaded{r}") for r in range(SLOTS)]
        self.hi_done = sem("hi_done")
        self.lo_done = sem("lo_done")
        self.chunk_mm = sem("chunk_mm")
        self.act_read = sem("act_read")
        self.dve_read = sem("dve_read")
        self.act_order, self.dve_order, self.pool_order = sem("act_order"), sem("dve_order"), sem("pool_order")
        self.sems = {}
        self.make = sem

    def s(self, *name):
        name = "_".join(str(n) for n in name)
        if name not in self.sems:
            self.sems[name] = self.make(name)
        return self.sems[name]

    def wait(self, eng, name, l, value):
        eng.wait_ge(self.s(name), value + l * FIRST_LAYER.get(name, 1))

    def banks(self, b, n, at=0, parts=slice(0, 128)):
        flat = self.ps[:, :, :].rearrange("p b n -> p (b n)")
        return flat[parts, b * 512 + at:b * 512 + at + n]

    def two(self, c, n, parts=slice(0, 128)):
        return self.ps[parts, 2 * c.pair:2 * c.pair + 2, 0:n]


class Order:

    def __init__(self, eng, sem):
        self.eng, self.sem, self.n, self.base = eng, sem, 0, 0

    def then(self, ins):
        ins.then_inc(self.sem, 1)
        self.n += 1
        return self.n

    def wait(self, n=None):
        self.eng.wait_ge(self.sem, self.base + (self.n if n is None else n))

    def link(self, ins):
        self.wait(self.then(ins))

    def enter(self, i, per):
        self.base, self.per, self.start = i * per, per, self.n

    def leave(self, times):
        assert self.n - self.start == self.per, (self.n - self.start)
        self.n, self.base = self.start + self.per * times, 0


def run_loop(eng, times):
    return eng.Fori(0, times)


def feed_hi(k, act, c):
    if c.first >= N_CHUNKS:
        return
    act.wait_ge(k.w_loaded[c.slot], c.value(lambda n: 16 * (n // SLOTS + 1)))
    for half in (slice(0, HALF), slice(HALF, CHUNK)):
        act.activation(k.w_hi[:, c.slot, half], k.w[:, c.slot, half], ACT.Copy).then_inc(k.hi_done, 1)


def feed_lo(k, dve, c):
    if c.first >= N_CHUNKS:
        return
    for n_half, half in enumerate((slice(0, HALF), slice(HALF, CHUNK))):
        dve.wait_ge(k.hi_done, c.value(lambda n: 2 * n + n_half + 1))
        dve.tensor_tensor(k.w_lo[:, c.slot, half], k.w[:, c.slot, half], k.w_hi[:, c.slot, half].bitcast(f32),
                          ALU.subtract).then_inc(k.lo_done, 1)


def sync_program(k, sp, t):
    def load(c, c_dyn=None):
        src = t["stream"][bass.ds(c.value(lambda n: n), 1)].rearrange("o p n -> (o p) n")
        if c.first >= SLOTS:
            sp.wait_ge(k.chunk_mm, c.value(lambda n: n - SLOTS + 1))
        sp.dma_start(k.w[:, c.slot, :], src).then_inc(k.w_loaded[c.slot], 16)

    sp.dma_start(k.F[:, :], t["feats"]).then_inc(k.s("feats_in"), 16)
    for r in range(SLOTS):
        load(At(r))
    sp.dma_start(k.X[:, 0:2, :], t["x"].rearrange("o (t p) d -> p (o t) d", p=128)).then_inc(k.s("x_in"), 16)
    sp.dma_start(k.X[:, 2:4, :], t["ctx"].rearrange("o (t p) d -> p (o t) d", p=128)).then_inc(k.s("x_in"), 16)
    sp.dma_start(k.C[:, :], t["consts"]).then_inc(k.s("consts_in"), 16)
    whole = N_CHUNKS // SLOTS
    with sp.Fori(0, whole - 1) as i:
        for r in range(SLOTS):
            load(At(SLOTS + r, SLOTS, i))
    for n in range(whole * SLOTS, N_CHUNKS):
        load(At(n))
    sp.wait_ge(k.s("res", "ffn"), 2)
    sp.dma_start(t["out"].rearrange("o (t p) d -> p (o t) d", p=128), k.X[:, 0:2, :]).then_inc(k.s("out_done"), 16)
    sp.wait_ge(k.s("out_done"), 16)


def mixer_buffers(k):
    U, Yf = k.U, k.Y[:, :, :].rearrange("p t d -> p (t d)")
    b = {}
    for name, at, n in (("bias", 0, 2048), ("cf_a", 2048, 1024), ("cf_g", 3072, 1024), ("cf_in", 4096, 1144),
                        ("cf_acc", 5240, 1024), ("ckv", 6264, 512), ("ckv_sq", 6776, 512), ("kr", 7288, 512),
                        ("cq", 7800, 1024), ("sc_x", 8824, 1024), ("sc_in", 9848, 1032), ("sc_b", 10880, 1024),
                        ("qr", 11904, 512), ("sq", 2048, 1024), ("std", 3072, 1024), ("p", 2048, 2048),
                        ("pt", 4096, 2048), ("qn", 7800, 1024), ("kn", 6264, 1024), ("rope", 10880, 256),
                        ("window", 11904, 256)):
        b[name] = U[:, at:at + n]
    for name, at in (("na_q", 0), ("na_k", 1024), ("na_v", 2048), ("v", 3072)):
        b[name] = Yf[:, at:at + 1024]
    return b


def attention_items(l):
    items = [("mla", h, 0, 512, 2) for h in range(HEADS)] + [("na", h, 0, 512, 6) for h in range(HEADS)]
    if l == 0:
        items += [("mla", h, 256, 256, 2) for h in range(HEADS)] + [("na", h, 256, 256, 6) for h in range(HEADS)]
    return items


PASSES = (("hi", "hi"), ("hi", "lo"), ("lo", "hi"))


def chunk_waits(k, pe, c):
    for sem, count in ((k.act_read, ACT_READ_COUNT), (k.dve_read, DVE_READ_COUNT)):
        if c.first >= 2 and count[c.first - 2]:
            pe.wait_ge(sem, c.value(lambda n: count[n - 2]))


def half_wait(k, pe, c, half):
    pe.wait_ge(k.lo_done, c.value(lambda n: 2 * n + half + 1))


def to_features(k, pe, c, h, kts, width, tiles, n, stride, before_kt=None):
    chunk_waits(k, pe, c)
    w = {"hi": k.w_hi, "lo": k.w_lo}
    for j in range(tiles):
        for kt in range(kts):
            if j == 0 and kt * width in (0, HALF):
                half_wait(k, pe, c, kt * width // HALF)
            if j == 0 and before_kt:
                before_kt(kt)
            for p, (a, b) in enumerate(PASSES):
                at = kt * width + j * 128
                last = pe.matmul(k.banks(2 * c.pair, n, j * (512 if tiles == 2 else n)), w[a][:, c.slot, at:at + 128],
                                 h[b][:, kt * stride:kt * stride + n],
                                 start=kt == 0 and p == 0, stop=kt == kts - 1 and p == 2)
    last.then_inc(k.chunk_mm, 1)


def to_tokens(k, pe, c, h, kts, n_tiles, stride, m=128, late=None):
    chunk_waits(k, pe, c)
    w = {"hi": k.w_hi, "lo": k.w_lo}

    def products(t, kt0, kt1):
        for kt in range(kt0, kt1):
            if t == 0 and kt in (0, 4):
                half_wait(k, pe, c, kt // 4)
            for p, (a, b) in enumerate(PASSES):
                at = kt * stride + t * 128
                last = pe.matmul(k.banks(2 * c.pair, 256, t * (512 if n_tiles == 2 else 256), slice(0, m)),
                                 h[a][:, at:at + m], w[b][:, c.slot, kt * 256:kt * 256 + 256],
                                 start=kt == 0 and p == 0, stop=kt == kts - 1 and p == 2)
        return last

    if late:
        first = range(0, n_tiles, n_tiles // 2)
        for t in first:
            products(t, 0, late[0])
        late[1]()
        for t in first:
            last = products(t, late[0], kts)
        rest = [t for t in range(n_tiles) if t not in first]
    else:
        rest = range(n_tiles)
    for t in rest:
        last = products(t, 0, kts)
    last.then_inc(k.chunk_mm, 1)


def pe_norm(k, pe, name, tiles, stride):
    ident = k.C[:, C_IDENT:C_IDENT + 128]
    pe.wait_ge(k.s("xn", name), tiles)
    for kt in range(KT):
        if kt >= 4:
            pe.wait_ge(k.s("hf", name), kt - 3)
        for t in range(tiles):
            last = pe.transpose(k.banks(4 + kt % 4, 128, t * 128), k.Y[:, t, kt * 128:kt * 128 + 128], ident)
        last.then_inc(k.s("tp", name), 1)


def pe_mod(k, pe, l):
    c0 = FIRST["mod", l]
    if l == 0:
        pe.wait_ge(k.s("cond"), 1)
    cs = {"hi": k.cs_hi, "lo": k.cs_lo}
    for j in range(4):
        to_tokens(k, pe, At(c0 + j), cs, KT, 1, 2, m=2)
    with run_loop(pe, 5) as i:
        for j in range(4, 8):
            to_tokens(k, pe, At(c0 + j, 4, i), cs, KT, 1, 2, m=2)
    mod = k.U[0:2, 0:6144]
    ident = k.C[0:2, C_IDENT:C_IDENT + 2]
    pe.wait_ge(k.dve_read, DVE_READ_COUNT[c0 + 23])
    if l == 0:
        pe.wait_ge(k.s("consts_in"), 16)
    for n, sec in enumerate((0, 1, 3, 4)):
        for kt in range(KT):
            last = pe.transpose(k.banks(0, 2, n * 16 + kt * 2), mod[:, sec * D + kt * 128:sec * D + kt * 128 + 128],
                                ident)
    last.then_inc(k.s("mod_t"), 1)
    sel = k.Y[0:2, 2, 0:256]
    k.wait(pe, "rows_in", l, 64)
    for which, sec in enumerate((2, 5)):
        if which:
            k.wait(pe, "mod_feat", l, 1)
        for v in range(2):
            for half in range(2):
                last = pe.matmul(k.banks((4, 0)[which] + 2 * v + half, 512), sel[:, v * 128:v * 128 + 128],
                                 mod[:, sec * D + half * 512:sec * D + half * 512 + 512], start=True, stop=True)
        last.then_inc(k.s("gate_rows"), 1)


def pe_mixers(k, pe, l):
    b = mixer_buffers(k)
    nq = NT_ALL if l == 0 else SEQ
    ones, swap = k.C[:, C_ONES:C_ONES + 128], k.C[:, C_SWAP:C_SWAP + 128]
    h = {"hi": k.h_hi, "lo": k.h_lo}
    c0 = FIRST["win", l]
    k.wait(pe, "gates", l, 4 if l == 0 else 2)
    for j, kind in enumerate(WIN):
        n = NT_ALL if kind in WIN_ALL_TOKENS else nq
        if kind == "nv":
            to_tokens(k, pe, At(c0 + j), h, KT, 4, NT_ALL)
        else:
            to_features(k, pe, At(c0 + j), h, KT, 256, 2, n, NT_ALL,
                        before_kt=None if j else lambda kt: pe.wait_ge(k.s("h", f"mix{l}"), kt + 1))

    k.wait(pe, "latent_sq", l, 2)
    pe.matmul(k.banks(4, 512), ones, b["ckv_sq"], start=True, stop=True)
    for kt in range(2):
        last = pe.matmul(k.banks(5, nq), ones, b["sq"][:, kt * nq:kt * nq + nq], start=kt == 0, stop=kt == 1)
    last.then_inc(k.s("latent_ssq"), 1)
    pe.wait_ge(k.act_read, ACT_READ_COUNT[c0 + 9])
    pe.wait_ge(k.dve_read, DVE_READ_COUNT[c0 + 9])
    k.wait(pe, "latent", l, 1)
    k.wait(pe, "small_in", l, 16)
    pe.matmul(k.banks(5, 256), swap, b["kr"][:, 0:256], start=True, stop=True)
    for j in range(2):
        pe.matmul(k.banks(6 + j, 512), k.SW[:, 768 + j * 128:768 + j * 128 + 128], b["ckv"], start=True, stop=True)
    for t in range(4):
        pe.matmul(k.banks(2, 256, t * 256), b["ckv"][:, t * 128:t * 128 + 128], k.SW[:, 1024:1280],
                  start=True, stop=True)
    for j, to in ((2, 4), (0, 0), (1, 1)):
        for kt in range(2):
            last = pe.matmul(k.banks(to, nq), k.SW[:, kt * 384 + j * 128:kt * 384 + j * 128 + 128],
                             b["cq"][:, kt * nq:kt * nq + nq], start=kt == 0, stop=kt == 1)
    last.then_inc(k.s("mla_mm"), 1)
    k.wait(pe, "qr", l, 1)
    k.wait(pe, "mla_in", l, 1)
    pe.matmul(k.banks(5, 256, 256), swap, b["qr"][:, 0:256], start=True, stop=True).then_inc(k.s("swap"), 1)
    k.wait(pe, "cf_conv", l, 1)
    for kt in range(2):
        last = pe.matmul(k.banks(4, nq), ones, b["cf_acc"][:, kt * nq:kt * nq + nq], start=kt == 0, stop=kt == 1)
    last.then_inc(k.s("cf_mean"), 1)
    k.wait(pe, "cf_sq", l, 1)
    for kt in range(2):
        last = pe.matmul(k.banks(4, nq), ones, b["sq"][:, kt * nq:kt * nq + nq], start=kt == 0, stop=kt == 1)
    last.then_inc(k.s("cf_var"), 1)
    k.wait(pe, "mla_kv", l, 1)
    k.wait(pe, "cf_act", l, 1)
    for j in range(2):
        for kt in range(2):
            last = pe.matmul(k.banks(6, nq, j * nq), k.SW[:, 1280 + kt * 256 + j * 128:1280 + kt * 256 + j * 128 + 128],
                             b["cf_acc"][:, kt * nq:kt * nq + nq], start=kt == 0, stop=kt == 1)
    last.then_inc(k.s("cf_mm"), 1)

    items = attention_items(l)
    ident = k.C[:, C_IDENT:C_IDENT + 128]
    k.wait(pe, "mla_in", l, 2)
    k.wait(pe, "mla_q", l, 1)

    def scores(i):
        kind, hd, q0, nk, _ = items[i]
        k0 = 0 if nk == 512 else 256
        rows = slice(64 * (hd % 2), 64 * (hd % 2) + 64)
        rot = slice(32 * hd, 32 * hd + 32)
        if i >= 2:
            k.wait(pe, "exp", l, i - 1)
        for qt in range(2):
            q = q0 + qt * 128
            to = k.banks(2 * (i % 2) + qt, nk)
            if kind == "mla":
                qa, ka = (hd // 2) * nq + q, (hd // 2) * 512 + k0
                pe.matmul(to, b["qn"][rows, qa:qa + 128], b["kn"][rows, ka:ka + nk], start=True, stop=False)
                last = pe.matmul(to, b["qr"][rot, q:q + 128], b["kr"][rot, k0:k0 + nk], start=False, stop=True)
            else:
                qa, ka = (hd // 2) * nq + q, (hd // 2) * 512 + k0
                last = pe.matmul(to, b["na_q"][rows, qa:qa + 128], b["na_k"][rows, ka:ka + nk], start=True, stop=True)
        last.then_inc(k.s("scores"), 1)

    def transposes(i):
        nk = items[i][3]
        k.wait(pe, "p", l, i + 1)
        if i == 0:
            k.wait(pe, "cf_y", l, 2)
        if i >= 1:
            k.wait(pe, "pt_act", l, i)
            k.wait(pe, "pt_dve", l, i)
        for kt in range(nk // 128):
            for qt in range(2):
                at = qt * nk + kt * 128
                last = pe.transpose(k.banks(4 + kt // (nk // 256), 128, kt % (nk // 256) * 256 + qt * 128),
                                    b["p"][:, (i % 2) * 1024 + at:(i % 2) * 1024 + at + 128], ident)
        last.then_inc(k.s("pt_mm"), 1)

    def values(i):
        kind, hd, q0, nk, _ = items[i]
        v = b["v"] if kind == "mla" else b["na_v"]
        t0 = 0 if nk == 512 else 2
        k.wait(pe, "pt_act", l, i + 1)
        k.wait(pe, "pt_dve", l, i + 1)
        if i >= 2:
            k.wait(pe, "o_lo", l, i - 1)
        rows = slice(64 * (hd % 2), 64 * (hd % 2) + 64)
        for kt in range(nk // 128):
            at = (t0 + kt) * 256 + hd * 64
            last = pe.matmul(k.banks(6 + i % 2, 256, 0, rows), v[:, at:at + 64],
                             b["pt"][:, (i % 2) * 1024 + kt * 256:(i % 2) * 1024 + kt * 256 + 256],
                             start=kt == 0, stop=kt == nk // 128 - 1)
        last.then_inc(k.s("o_mm"), 1)

    scores(0)
    for i in range(len(items)):
        if i + 1 < len(items):
            scores(i + 1)
        transposes(i)
        values(i)

    k.wait(pe, "o_lo", l, len(items))
    k.wait(pe, "sc_y", l, 2)
    tiles = 4 if l == 0 else 2
    for j in range(4):
        to_tokens(k, pe, At(FIRST["out", l] + j), h, KT, tiles, NT_ALL)


def pe_mlp(k, pe, l):
    tiles = 4 if l == 0 else 2
    n = tiles * 128
    h, g = {"hi": k.h_hi, "lo": k.h_lo}, {"hi": k.g_hi, "lo": k.g_lo}
    pe_norm(k, pe, f"mlp{l}", tiles, n)
    c0 = FIRST["mlp", l]
    with run_loop(pe, GROUPS1) as i:
        for j in range(4):
            to_features(k, pe, At(c0 + j, 8, i), h, KT, 256, 2, n, NT_ALL,
                        before_kt=None if j else lambda kt: pe.wait_ge(k.s("h", f"mlp{l}"), kt + 1))
        k.wait(pe, "hidden", l, i * 4 + 3)
        for j in range(4):
            to_tokens(k, pe, At(c0 + 4 + j, 8, i), g, KT, tiles, n,
                      late=(6, lambda: k.wait(pe, "hidden", l, i * 4 + 4)) if j == 0 else None)


def pe_second(k, pe):
    h, g = {"hi": k.h_hi, "lo": k.h_lo}, {"hi": k.g_hi, "lo": k.g_lo}
    b = second_buffers(k)
    ones, ident = k.C[:, C_ONES:C_ONES + 128], k.C[:, C_IDENT:C_IDENT + 128]
    pe_norm(k, pe, "mix2", 2, SEQ)
    c0 = FIRST["proj2"]
    for j in range(24):
        c = At(c0 + j)
        if KINDS[c.first] in ("va", "vb"):
            to_tokens(k, pe, c, h, KT, 2, SEQ)
        else:
            to_features(k, pe, c, h, KT, 256, 2, SEQ, SEQ,
                        before_kt=None if j else lambda kt: pe.wait_ge(k.s("h", "mix2"), kt + 1))
    pe.wait_ge(k.act_read, ACT_READ_COUNT[c0 + 23])
    pe.wait_ge(k.dve_read, DVE_READ_COUNT[c0 + 23])
    pe.wait_ge(k.s("rope2"), 16)

    def scores_a(hd):
        if hd >= 2:
            pe.wait_ge(k.s("exp_a"), hd - 1)
        for cmp in range(2):
            rows = slice(64 * cmp, 64 * cmp + 64)
            for qt in range(2):
                last = pe.matmul(k.banks(2 * (hd % 2), 256, (cmp * 2 + qt) * 256),
                                 b["qa"][rows, hd * 256 + qt * 128:hd * 256 + qt * 128 + 128],
                                 b["ka"][rows, hd * 256:hd * 256 + 256], start=True, stop=True)
        last.then_inc(k.s("scores_a"), 1)

    scores_a(0)
    for hd in range(HEADS):
        if hd + 1 < HEADS:
            scores_a(hd + 1)
        pe.wait_ge(k.s("p_a"), hd + 1)
        if hd:
            pe.wait_ge(k.s("pt_a"), hd)
        for kt in range(2):
            for qt in range(2):
                at = (hd % 2) * 1024 + qt * 256 + kt * 128
                last = pe.transpose(k.banks(4, 128, kt * 256 + qt * 128), b["pa"][:, at:at + 128], ident)
        last.then_inc(k.s("pt_a_mm"), 1)
        pe.wait_ge(k.s("pt_a"), hd + 1)
        if hd:
            pe.wait_ge(k.s("oa"), hd)
        for kt in range(2):
            last = pe.matmul(k.banks(5, 256), b["va"][:, kt * 512 + hd * 128:kt * 512 + hd * 128 + 128],
                             b["pta"][:, (hd % 2) * 512 + kt * 256:(hd % 2) * 512 + kt * 256 + 256],
                             start=kt == 0, stop=kt == 1)
        last.then_inc(k.s("oa_mm"), 1)
        pe.wait_ge(k.s("oa_sq"), hd + 1)
        pe.matmul(k.banks(6, 256), ones, b["oa_sq"], start=True, stop=True).then_inc(k.s("oa_ssq"), 1)
    pe.wait_ge(k.s("oa"), HEADS)

    def scores_b(hd):
        if hd:
            pe.wait_ge(k.s("exp_b"), hd)
        for qt in range(2):
            for grp in range(3):
                at = (grp * 4 + hd) * 256
                last = pe.matmul(k.banks(0, 256, qt * 768 + grp * 256), b["qb"][:, at + qt * 128:at + qt * 128 + 128],
                                 b["kb"][:, at:at + 256], start=True, stop=True)
        last.then_inc(k.s("scores_b"), 1)

    scores_b(0)
    for hd in range(HEADS):
        pe.wait_ge(k.s("p_b"), hd + 1)
        for grp in range(3):
            for kt in range(2):
                for qt in range(2):
                    at = qt * 768 + grp * 256 + kt * 128
                    last = pe.transpose(k.banks(3, 128, (grp * 2 + kt) * 256 + qt * 128), b["pb"][:, at:at + 128],
                                        ident)
        last.then_inc(k.s("pt_b_mm"), 1)
        if hd + 1 < HEADS:
            scores_b(hd + 1)
        pe.wait_ge(k.s("pt_b_act"), hd + 1)
        pe.wait_ge(k.s("pt_b_dve"), hd + 1)
        if hd >= 2:
            pe.wait_ge(k.s("ob"), hd - 1)
        for n in range(6):
            grp, kt = n // 2, n % 2
            at = kt * 1536 + (grp * 4 + hd) * 128
            last = pe.matmul(k.banks(6 + hd % 2, 256), b["vb"][:, at:at + 128], b["ptb"][:, n * 256:n * 256 + 256],
                             start=n == 0, stop=n == 5)
        last.then_inc(k.s("ob_mm"), 1)

    for j in range(8):
        to_features(k, pe, At(FIRST["gates2"] + j), h, KT, 256, 2, SEQ, SEQ)
    pe.wait_ge(k.s("ob"), HEADS)
    for j in range(4):
        o = {p: h[p][:, 2048 + (j // 2) * 1024:2048 + (j // 2) * 1024 + 1024] for p in h}
        to_features(k, pe, At(FIRST["mix2"] + j), o, 4, 512, 4, SEQ, SEQ)
    pe.wait_ge(k.s("z"), 1)
    for j in range(4):
        to_tokens(k, pe, At(FIRST["mix2"] + 4 + j), h, KT, 2, SEQ)

    pe_norm(k, pe, "ffn", 2, SEQ)

    def group(i, g0, steps):
        c0 = FIRST["ffn", g0]
        per = 12 if steps == 4 else 0
        for j in range(2 * steps):
            to_features(k, pe, At(c0 + j, per, i), h, KT, 256, 2, SEQ, SEQ,
                        before_kt=None if j else lambda kt: pe.wait_ge(k.s("h", "ffn"), kt + 1))
        n = i * 4 + steps if per else 4 * g0 + steps
        pe.wait_ge(k.s("hidden2"), n - 1)
        for j in range(4):
            to_tokens(k, pe, At(c0 + 2 * steps + j, per, i), g, 2 * steps, 2, SEQ,
                      late=(2 * steps - 2, lambda: pe.wait_ge(k.s("hidden2"), n)) if j == 0 else None)

    with run_loop(pe, 2) as i:
        group(i, 0, 4)
    group(0, 2, 3)


def tensor_program(k, pe):
    for l in range(DEPTH):
        pe_mod(k, pe, l)
        pe_norm(k, pe, f"mix{l}", 4, NT_ALL)
        pe_mixers(k, pe, l)
        pe_mlp(k, pe, l)
    pe_second(k, pe)


def second_buffers(k):
    Yf, T = k.Y[:, :, :].rearrange("p t d -> p (t d)"), k.GA[:, 2, :]
    b = {}
    for name, at, n in (("qa", 0, 1024), ("ka", 1024, 1024), ("va", 2048, 1024), ("qb", 3072, 3072),
                        ("kb", 6144, 3072), ("vb", 9216, 3072), ("gate", 0, 4096), ("z", 4096, 2048),
                        ("zb", 6144, 2048)):
        b[name] = k.U[:, at:at + n]
    for name, at, n in (("pa", 0, 2048), ("pta", 2048, 1024), ("pb", 0, 1536), ("ptb", 1536, 1536),
                        ("swapped", 3072, 1024)):
        b[name] = Yf[:, at:at + n]
    for name, at, n in (("oa_sq", 0, 256), ("oa_std", 256, 256), ("oa_f", 512, 256), ("lam", 0, 256),
                        ("pos", 256, 256), ("t0", 512, 256), ("t1", 768, 256)):
        b[name] = T[:, at:at + n]
    for n, name in enumerate(("cos_a", "sin_a", "cos_b", "sin_b")):
        b[name] = k.GA[:, 3, n * 256:n * 256 + 256]
    b["mask_a"] = k.X[:, 2, 0:512]
    b["mask_b"] = k.X[:, 2:4, :].rearrange("p t d -> p (t d)")[:, 512:2048]
    return b


def col(k, at, n=1):
    return k.F[:, at:at + n]


def act_norm(k, act, o, name, tiles, n, x_ready, gain, shift):
    for t in range(tiles):
        x_ready(t)
        o.then(act.activation(k.Y[:, t, :], k.X[:, t, :], ACT.Square, accum_out=k.tiny[:, t:t + 1]))
    o.wait()
    act.activation(k.tiny[:, 4:4 + tiles], k.tiny[:, 0:tiles], ACT.Sqrt, bias=k.C[:, C_EPS:C_EPS + 1],
                   scale=1.0 / D).then_inc(k.s("std", name), 1)
    for kt in range(KT):
        act.wait_ge(k.s("tp", name), kt + 1)
        if kt >= 2:
            act.wait_ge(k.s("h", name), kt - 1)
        for part in range(n // 256):
            last = act.activation(k.hf[:, kt % 2, part * 256:part * 256 + 256],
                                  k.banks(4 + kt % 4, 256, part * 256), ACT.Identity,
                                  bias=shift(kt, part), scale=gain(kt, part))
        last.then_inc(k.s("hf", name), 1)


def act_residual(k, act, o, name, tiles, last_chunk):
    act.wait_ge(k.act_read, ACT_READ_COUNT[last_chunk])
    act.wait_ge(k.dve_read, DVE_READ_COUNT[last_chunk])
    for t in range(tiles):
        o.link(act.activation(k.hf[:, t % 2, :], k.Y[:, t, :], ACT.Square, accum_out=k.tiny[:, t:t + 1]))
    act.activation(k.tiny[:, 4:4 + tiles], k.tiny[:, 0:tiles], ACT.Sqrt, bias=k.C[:, C_EPS:C_EPS + 1],
                   scale=1.0 / D).then_inc(k.s("rstd", name), 1)


def act_take(k, act, c, out, width, at, func=None, scale=1.0):
    act.wait_ge(k.chunk_mm, c.value(lambda n: n + 1))
    return act.activation(out, k.banks(2 * c.pair, width, at), func or ACT.Copy, scale=scale)


def act_mixers(k, act, o, l):
    b = mixer_buffers(k)
    nq = NT_ALL if l == 0 else SEQ
    c0 = FIRST["win", l]
    eps = k.C[:, C_EPS:C_EPS + 1]
    for j, kind in enumerate(WIN):
        c = At(c0 + j)
        feed_hi(k, act, c + 2)
        n = NT_ALL if kind in WIN_ALL_TOKENS else nq
        last = None
        if kind in ("cf_a", "sc_x", "sc_b"):
            last = act_take(k, act, c, b[kind][:, 0:n], n, 0)
        elif kind == "cf_g":
            act.wait_ge(k.chunk_mm, c.first + 1)
            last = act.activation(b["cf_g"][:, 0:2 * n].rearrange("p (t n) -> p t n", t=2), k.two(c, n), ACT.Sigmoid)
        elif kind == "kv":
            last = act_take(k, act, c, b["kr"], 512, 512)
        elif kind == "q":
            last = act_take(k, act, c, b["cq"][:, 0:n], n, 0)
        elif kind == "nk":
            last = act_take(k, act, c, b["na_k"][:, 0:n], n, 0)
        elif kind == "nq":
            last = act_take(k, act, c, b["na_q"][:, 0:n], n, 0, scale=NA_SCALE)
        elif kind == "nv":
            last = act_take(k, act, c, b["na_v"][:, 0:512], 512, 0)
        if last is not None:
            last.then_inc(k.act_read, 1)
        if kind == "q":
            act.wait_ge(k.dve_read, DVE_READ_COUNT[c0 + 2])
            act.activation(b["ckv_sq"], b["ckv"], ACT.Square).then_inc(k.s("latent_sq"), 1)
        if kind == "nk":
            act.wait_ge(k.act_read, ACT_READ_COUNT[c0 + 3])
            act.wait_ge(k.dve_read, DVE_READ_COUNT[c0 + 3])
            act.activation(b["sq"][:, 0:2 * nq], b["cq"][:, 0:2 * nq], ACT.Square).then_inc(k.s("latent_sq"), 1)

    hk = k.h_hi[:, :].rearrange("p (k n) -> p k n", k=KT)
    k.wait(act, "latent_ssq", l, 1)
    act.activation(b["std"][:, 0:512], k.banks(4, 512), ACT.Sqrt, bias=eps, scale=1.0 / 128)
    act.activation(b["std"][:, 512:512 + nq], k.banks(5, nq), ACT.Sqrt, bias=eps,
                   scale=1.0 / 256).then_inc(k.s("latent_std"), 1)
    k.wait(act, "sc_done", l, 1)
    act.activation(hk[:, 0:2, 0:nq], b["sc_x"][:, 0:2 * nq].rearrange("p (k n) -> p k n", k=2),
                   ACT.Copy).then_inc(k.s("sc_y"), 1)
    k.wait(act, "mla_mm", l, 1)
    act.activation(b["kn"], k.banks(6, 1024), ACT.Copy).then_inc(k.s("mla_kv"), 1)
    for j in range(2):
        last = act.activation(b["qn"][:, j * nq:j * nq + nq], k.banks(j, nq), ACT.Copy, scale=MLA_SCALE)
    last.then_inc(k.s("mla_q"), 1)
    k.wait(act, "cf_cent", l, 1)
    act.activation(b["sq"][:, 0:2 * nq], b["cf_acc"][:, 0:2 * nq], ACT.Square).then_inc(k.s("cf_sq"), 1)
    k.wait(act, "cf_var", l, 1)
    act.activation(b["std"][:, 0:nq], k.banks(4, nq), ACT.Sqrt, bias=eps, scale=1.0 / 256).then_inc(k.s("cf_std"), 1)
    k.wait(act, "cf_norm", l, 1)
    for j in range(2):
        last = act.activation(b["cf_acc"][:, j * nq:j * nq + nq], b["cf_acc"][:, j * nq:j * nq + nq], ACT.Silu,
                              bias=col(k, FC["ln_b", l] + j))
    last.then_inc(k.s("cf_act"), 1)
    k.wait(act, "cf_mm", l, 1)
    act.activation(hk[:, 4:6, 0:nq], k.banks(6, 2 * nq).rearrange("p (k n) -> p k n", k=2),
                   ACT.Copy).then_inc(k.s("cf_y"), 1)

    items = attention_items(l)

    def exps(i):
        nk = items[i][3]
        k.wait(act, "nmax", l, i + 1)
        if i >= 2:
            k.wait(act, "pt_mm", l, i - 1)
        for qt in range(2):
            at = (i % 2) * 1024 + qt * nk
            last = act.activation(b["p"][:, at:at + nk], k.banks(2 * (i % 2) + qt, nk), ACT.Exp,
                                  bias=k.tiny[:, 16 + 2 * (i % 2) + qt:17 + 2 * (i % 2) + qt],
                                  accum_out=k.tiny[:, 20 + 2 * (i % 2) + qt:21 + 2 * (i % 2) + qt])
        last.then_inc(k.s("exp"), 1)

    exps(0)
    for i, (kind, hd, q0, nk, kt0) in enumerate(items):
        if i + 1 < len(items):
            exps(i + 1)
        k.wait(act, "pt_mm", l, i + 1)
        if i >= 2:
            k.wait(act, "o_mm", l, i - 1)
        act.activation(b["pt"][:, (i % 2) * 1024:(i % 2) * 1024 + nk], k.banks(4, nk),
                       ACT.Copy).then_inc(k.s("pt_act"), 1)
        k.wait(act, "o_mm", l, i + 1)
        rows, at = slice(64 * (hd % 2), 64 * (hd % 2) + 64), (kt0 + hd // 2) * NT_ALL + q0
        act.activation(k.h_hi[rows, at:at + 256], k.banks(6 + i % 2, 256, 0, rows),
                       ACT.Copy).then_inc(k.s("o_hi"), 1)

    half = 512 if l == 0 else 256
    for j in range(4):
        c = At(FIRST["out", l] + j)
        feed_hi(k, act, c + 2)
        out = k.Y[:, 0:half // 256, j * 256:j * 256 + 256]
        act.wait_ge(k.chunk_mm, c.first + 1)
        act.activation(out, k.banks(2 * c.pair, half).rearrange("p (t n) -> p t n", n=256),
                       ACT.Copy).then_inc(k.act_read, 1)


def act_mlp(k, act, o, l):
    tiles = 4 if l == 0 else 2
    n = tiles * 128
    act_residual(k, act, o, f"mix{l}", tiles, FIRST["out", l] + 3)
    act_norm(k, act, o, f"mlp{l}", tiles, n, lambda t: act.wait_ge(k.s("res", f"mix{l}"), t + 1),
             lambda kt, v: k.mod_gain[:, 16 + v * 8 + kt:17 + v * 8 + kt],
             lambda kt, v: k.mod_feat[:, 32 + kt * 2 + v:33 + kt * 2 + v])
    c0 = FIRST["mlp", l]
    with run_loop(act, GROUPS1) as i:
        for j in range(8):
            c = At(c0 + j, 8, i)
            feed_hi(k, act, c + 2)
            if j >= 4:
                continue
            act.wait_ge(k.chunk_mm, c.value(lambda m: m + 1))
            if j >= 2:
                k.wait(act, "hidden", l, i * 4 + (j - 1))
            act.activation(k.R[:, j % 2, 0:2 * n].rearrange("p (t n) -> p t n", t=2), k.two(c, n),
                           ACT.Relu).then_inc(k.act_read, 1)
            act.wait_ge(k.act_read, c.value(lambda m: ACT_READ_COUNT[m]))
            act.activation(k.R[:, j % 2, 0:2 * n], k.R[:, j % 2, 0:2 * n],
                           ACT.Square).then_inc(k.s("squared"), 1)
    act_residual(k, act, o, f"mlp{l}", tiles, c0 + 31)


def act_second(k, act, o):
    b = second_buffers(k)
    eps = k.C[:, C_EPS:C_EPS + 1]
    act.wait_ge(k.s("angles"), 1)
    act.activation(k.GA[:, 3, :], k.GA[:, 3, :], ACT.Sin).then_inc(k.s("tables"), 1)
    act.activation(k.tiny[:, 66:68], k.tiny[:, 64:66], ACT.Exp).then_inc(k.s("lam_exp"), 1)
    act_norm(k, act, o, "mix2", 2, SEQ, lambda t: act.wait_ge(k.s("res", "mlp1"), t + 1),
             lambda kt, v: col(k, FC["pre_mix2"] + kt), lambda kt, v: k.C[:, C_ZERO:C_ZERO + 1])
    c0 = FIRST["proj2"]
    for j in range(24):
        c = At(c0 + j)
        feed_hi(k, act, c + 2)
        kind = KINDS[c.first]
        if kind in ("va", "vb"):
            at = (j - 4) * 256 if kind == "va" else (j - 18) * 256
            act_take(k, act, c, b[kind][:, at:at + 256], 256, 0).then_inc(k.act_read, 1)

    act.wait_ge(k.s("lam_exp"), 1)

    def exps_a(hd):
        act.wait_ge(k.s("nmax_a"), hd + 1)
        if hd >= 2:
            act.wait_ge(k.s("pt_a_mm"), hd - 1)
        for m in range(4):
            at = (hd % 2) * 1024 + m * 256
            last = act.activation(b["pa"][:, at:at + 256], k.banks(2 * (hd % 2), 256, m * 256), ACT.Exp,
                                  bias=k.tiny[:, 40 + 4 * (hd % 2) + m:41 + 4 * (hd % 2) + m], scale=0.125,
                                  accum_out=k.tiny[:, 48 + 4 * (hd % 2) + m:49 + 4 * (hd % 2) + m])
        last.then_inc(k.s("exp_a"), 1)

    exps_a(0)
    for hd in range(HEADS):
        if hd + 1 < HEADS:
            exps_a(hd + 1)
        act.wait_ge(k.s("pt_a_mm"), hd + 1)
        if hd >= 2:
            act.wait_ge(k.s("oa_mm"), hd - 1)
        act.activation(b["pta"][:, (hd % 2) * 512:(hd % 2) * 512 + 512], k.banks(4, 512),
                       ACT.Copy).then_inc(k.s("pt_a"), 1)
        act.wait_ge(k.s("oa_mm"), hd + 1)
        if hd:
            act.wait_ge(k.s("oa"), hd)
        act.activation(b["oa_sq"], k.banks(5, 256), ACT.Square).then_inc(k.s("oa_sq"), 1)
        act.wait_ge(k.s("oa_ssq"), hd + 1)
        act.activation(b["oa_std"], k.banks(6, 256), ACT.Sqrt, bias=eps, scale=1.0 / 128).then_inc(k.s("oa_std"), 1)

    def exps_b(hd):
        act.wait_ge(k.s("nmax_b"), hd + 1)
        if hd:
            act.wait_ge(k.s("pt_b_mm"), hd)
        for qt in range(2):
            last = act.activation(b["pb"][:, qt * 768:qt * 768 + 768], k.banks(0, 768, qt * 768), ACT.Exp,
                                  bias=k.tiny[:, 74 + qt:75 + qt], scale=128 ** -0.5,
                                  accum_out=k.tiny[:, 76 + qt:77 + qt])
        last.then_inc(k.s("exp_b"), 1)

    exps_b(0)
    for hd in range(HEADS):
        act.wait_ge(k.s("pt_b_mm"), hd + 1)
        if hd:
            act.wait_ge(k.s("ob_mm"), hd)
        act.activation(b["ptb"][:, 0:1024], k.banks(3, 1024), ACT.Copy).then_inc(k.s("pt_b_act"), 1)
        if hd + 1 < HEADS:
            exps_b(hd + 1)
        act.wait_ge(k.s("ob_mm"), hd + 1)
        at = 3072 + hd * 256
        act.activation(k.h_hi[:, at:at + 256], k.banks(6 + hd % 2, 256), ACT.Copy).then_inc(k.s("ob_hi"), 1)

    for j in range(8):
        c = At(FIRST["gates2"] + j)
        feed_hi(k, act, c + 2)
        act.wait_ge(k.chunk_mm, c.first + 1)
        act.activation(b["gate"][:, j * 512:j * 512 + 512].rearrange("p (t n) -> p t n", t=2), k.two(c, 256),
                       ACT.Sigmoid).then_inc(k.act_read, 1)
    for j in range(4):
        feed_hi(k, act, At(FIRST["mix2"] + j + 2))
    act.wait_ge(k.s("z_f"), 1)
    act.activation(k.h_hi[:, 0:2048], b["z"], ACT.Copy).then_inc(k.s("z_hi"), 1)
    for j in range(4):
        c = At(FIRST["mix2"] + 4 + j)
        feed_hi(k, act, c + 2)
        act_take(k, act, c, k.Y[:, 0, j * 256:j * 256 + 256], 256, 0).then_inc(k.act_read, 1)
    act_residual(k, act, o, "mix2", 2, FIRST["mix2"] + 7)
    act_norm(k, act, o, "ffn", 2, SEQ, lambda t: act.wait_ge(k.s("res", "mix2"), t + 1),
             lambda kt, v: col(k, FC["pre_ffn2"] + kt), lambda kt, v: k.C[:, C_ZERO:C_ZERO + 1])

    def group(i, g0, steps):
        per = 12 if steps == 4 else 0
        for st in range(steps):
            for kind in range(2):
                c = At(FIRST["ffn", g0] + 2 * st + kind, per, i)
                feed_hi(k, act, c + 2)
                act.wait_ge(k.chunk_mm, c.value(lambda m: m + 1))
                if st >= 2 and kind == 0:
                    act.wait_ge(k.s("hidden2"), i * 4 + (st - 1) if per else 4 * g0 + st - 1)
                for t in range(2):
                    tile = kind * 22 + (g0 * 4 + st) * 2 + t
                    w = FC["conv_w2"] + 2 * 44 + tile
                    bb = FC["conv_b2"] + tile
                    if per:
                        w, bb = i * 8 + w, i * 8 + bb
                    last = act.activation(k.R[:, st % 2, kind * 512 + t * 256:kind * 512 + t * 256 + 256],
                                          k.banks(2 * c.pair, 256, t * 512), ACT.Identity,
                                          bias=k.F[:, bass.ds(bb, 1)], scale=k.F[:, bass.ds(w, 1)])
                last.then_inc(k.act_read, 1)
            act.wait_ge(k.dve_read, At(FIRST["ffn", g0] + 2 * st, per, i).value(lambda m: DVE_READ_COUNT[m]))
            act.activation(k.R[:, st % 2, 0:512], k.R[:, st % 2, 0:512],
                           ACT.Gelu_apprx_tanh).then_inc(k.s("gelu"), 1)
        for j in range(4):
            feed_hi(k, act, At(FIRST["ffn", g0] + 2 * steps + j + 2, per, i))

    with run_loop(act, 2) as i:
        group(i, 0, 4)
    group(0, 2, 3)
    act_residual(k, act, o, "ffn", 2, N_CHUNKS - 1)


def scalar_program(k, act):
    o = Order(act, k.act_order)
    act.wait_ge(k.s("feats_in"), 16)
    o.link(act.activation(k.tiny[:, 96:112], k.F[:, 0:16], ACT.Silu))
    act.activation(k.cs_hi[:, :], k.tiny[:, 96:112], ACT.Copy).then_inc(k.s("cond_hi"), 1)
    feed_hi(k, act, At(0))
    feed_hi(k, act, At(1))
    for l in range(DEPTH):
        c0 = FIRST["mod", l]
        with run_loop(act, 6) as i:
            for j in range(4):
                feed_hi(k, act, At(c0 + j + 2, 4, i))
        n_gates = 4 if l == 0 else 2

        def x_ready(t):
            if t == 0:
                k.wait(act, "gates", l, n_gates)
                if l == 0:
                    act.wait_ge(k.s("x_in"), 32)
                    act.wait_ge(k.s("consts_in"), 16)
            if l:
                act.wait_ge(k.s("res", "mlp0"), t + 1)

        act_norm(k, act, o, f"mix{l}", 4, NT_ALL, x_ready,
                 lambda kt, v: k.mod_gain[:, v * 8 + kt:v * 8 + kt + 1],
                 lambda kt, v: k.mod_feat[:, kt * 2 + v:kt * 2 + v + 1])
        act_mixers(k, act, o, l)
        act_mlp(k, act, o, l)
    act_second(k, act, o)


def dve_norm(k, dve, o, name, tiles, n, stride):
    dve.wait_ge(k.s("std", name), 1)
    o.link(dve.reciprocal(k.tiny[:, 8:8 + tiles], k.tiny[:, 4:4 + tiles]))
    for t in range(tiles):
        dve.tensor_scalar(k.Y[:, t, :], k.X[:, t, :], k.tiny[:, 8 + t:9 + t], None,
                          ALU.mult).then_inc(k.s("xn", name), 1)
    for kt in range(KT):
        dve.wait_ge(k.s("hf", name), kt + 1)
        hi, lo = k.h_hi[:, kt * stride:kt * stride + n], k.h_lo[:, kt * stride:kt * stride + n]
        o.link(dve.tensor_copy(hi, k.hf[:, kt % 2, 0:n]))
        dve.tensor_tensor(lo, k.hf[:, kt % 2, 0:n], hi.bitcast(f32), ALU.subtract).then_inc(k.s("h", name), 1)


def dve_residual(k, dve, o, name, tiles, ga):
    dve.wait_ge(k.s("rstd", name), 1)
    o.link(dve.reciprocal(k.tiny[:, 8:8 + tiles], k.tiny[:, 4:4 + tiles]))
    for t in range(tiles):
        o.link(dve.scalar_tensor_tensor(k.Y[:, t, :], k.Y[:, t, :], k.tiny[:, 8 + t:9 + t], k.GA[:, ga(t), :],
                                        ALU.mult, ALU.mult))
        dve.tensor_tensor(k.X[:, t, :], k.X[:, t, :], k.Y[:, t, :], ALU.add).then_inc(k.s("res", name), 1)


def dve_take(k, dve, c, out, width, at, scale=None):
    dve.wait_ge(k.chunk_mm, c.value(lambda n: n + 1))
    if scale is None:
        return dve.tensor_copy(out, k.banks(2 * c.pair, width, at))
    return dve.tensor_scalar(out, k.banks(2 * c.pair, width, at), scale, None, ALU.mult)


def dve_mod(k, dve, o, l):
    c0 = FIRST["mod", l]
    k.wait(dve, "rows_in", l, 64)

    def take(c, at):
        dve.wait_ge(k.chunk_mm, c.value(lambda n: n + 1))
        dve.tensor_tensor(k.U[0:2, bass.ds(at, 256)], k.banks(2 * c.pair, 256, 0, slice(0, 2)),
                          k.U[0:2, bass.ds(at + 6144, 256)], ALU.add).then_inc(k.dve_read, 1)
        feed_lo(k, dve, c + 2)

    for j in range(4):
        take(At(c0 + j), j * 256)
    with run_loop(dve, 5) as i:
        for j in range(4, 8):
            take(At(c0 + j, 4, i), i * 1024 + j * 256)
    k.wait(dve, "mod_t", l, 1)
    dve.tensor_copy(k.mod_feat[:, :], k.banks(0, 64)).then_inc(k.s("mod_feat"), 1)
    k.wait(dve, "mod_feat", l, 1)
    mf = k.mod_feat[:, :].rearrange("p (s k v) -> p s v k", s=4, v=2)
    for which, gain in enumerate(("g_pre_mix", "g_pre_mlp")):
        for v in range(2):
            at = (2 * which + v) * 8
            o.then(dve.scalar_tensor_tensor(k.mod_gain[:, at:at + 8], mf[:, 2 * which + 1, v, :], 1.0,
                                            col(k, FC[gain, l], 8), ALU.add, ALU.mult))
    for which in range(2):
        k.wait(dve, "gate_rows", l, which + 1)
        for v in range(2 if l == 0 else 1):
            dve.tensor_tensor(k.GA[:, 2 * which + v, :], k.banks((4, 0)[which] + 2 * v, 1024), k.Y[:, which, :],
                              ALU.mult).then_inc(k.s("gates"), 1)


def dve_mixers(k, dve, o, l):
    b = mixer_buffers(k)
    nq = NT_ALL if l == 0 else SEQ
    seg = nq // 256
    c0 = FIRST["win", l]
    cf_in = b["cf_in"].rearrange("p (k s n) -> p k s n", k=2, s=2)
    sc_in = b["sc_in"].rearrange("p (k s n) -> p k s n", k=2, s=2)
    acc = b["cf_acc"][:, 0:2 * nq].rearrange("p (k s n) -> p k s n", k=2, s=seg)
    scx = b["sc_x"][:, 0:2 * nq].rearrange("p (k s n) -> p k s n", k=2, s=seg)
    o.then(dve.memset(b["cf_in"], 0.0))
    o.link(dve.memset(b["sc_in"], 0.0))

    done = {}
    taps = [(tap, kt) for tap in range(CF_K) for kt in range(2)]

    def conv_taps(n):
        for tap, kt in taps[:n]:
            src, w = cf_in[:, kt, 0:seg, tap:tap + 256], col(k, FC["cf_w", l] + kt * CF_K + tap)
            if tap == 0:
                ins = dve.tensor_scalar(acc[:, kt], src, w, col(k, FC["cf_b", l] + kt), ALU.mult, ALU.add)
            else:
                o.wait(done[kt])
                ins = dve.scalar_tensor_tensor(acc[:, kt], src, w, acc[:, kt], ALU.mult, ALU.add)
            if (tap, kt) == (CF_K - 1, 1):
                ins.then_inc(k.s("cf_conv"), 1)
            else:
                done[kt] = o.then(ins)
        del taps[:n]

    for j, kind in enumerate(WIN):
        c = At(c0 + j)
        feed_lo(k, dve, c + 2)
        n = NT_ALL if kind in WIN_ALL_TOKENS else nq
        if kind in ("cf_a", "sc_x", "sc_b"):
            dve_take(k, dve, c, b[kind][:, n:2 * n], n, 512).then_inc(k.dve_read, 1)
        elif kind == "cf_g":
            dve.wait_ge(k.act_read, ACT_READ_COUNT[c.first])
            dve.wait_ge(k.dve_read, DVE_READ_COUNT[c.first - 1])
            o.link(dve.tensor_tensor(cf_in[:, :, 0:seg, 15:271],
                                     b["cf_a"][:, 0:2 * n].rearrange("p (k s n) -> p k s n", k=2, s=seg),
                                     b["cf_g"][:, 0:2 * n].rearrange("p (k s n) -> p k s n", k=2, s=seg), ALU.mult))
        elif kind == "kv":
            dve_take(k, dve, c, b["ckv"], 512, 0).then_inc(k.dve_read, 1)
        elif kind == "q":
            dve_take(k, dve, c, b["cq"][:, n:2 * n], n, 512).then_inc(k.dve_read, 1)
        elif kind == "nk":
            dve_take(k, dve, c, b["na_k"][:, n:2 * n], n, 512).then_inc(k.dve_read, 1)
        elif kind == "nq":
            dve_take(k, dve, c, b["na_q"][:, n:2 * n], n, 512, NA_SCALE).then_inc(k.dve_read, 1)
        elif kind == "nv":
            dve_take(k, dve, c, b["na_v"][:, 512:1024], 512, 512).then_inc(k.dve_read, 1)
        elif kind == "sc_c":
            dve.wait_ge(k.chunk_mm, c.first + 1)
            dve.wait_ge(k.act_read, ACT_READ_COUNT[c.first])
            dve.wait_ge(k.dve_read, DVE_READ_COUNT[c.first - 1])
            dve.tensor_tensor(sc_in[:, :, 0:seg, 1:257],
                              k.two(c, n).rearrange("p k (s n) -> p k s n", s=seg), scx,
                              ALU.mult).then_inc(k.dve_read, 1)
        if j >= 2:
            conv_taps(8)
    dve.wait_ge(k.dve_read, DVE_READ_COUNT[c0 + 9])
    dve.wait_ge(k.act_read, ACT_READ_COUNT[c0 + 9])
    for kt in range(2):
        w = FC["w_sc", l] + kt * 3
        done[kt] = o.then(dve.tensor_scalar(scx[:, kt], sc_in[:, kt, 0:seg, 0:256], col(k, w), None, ALU.mult))
    for tap in (1, 2):
        for kt in range(2):
            o.wait(done[kt])
            done[kt] = o.then(dve.scalar_tensor_tensor(scx[:, kt], sc_in[:, kt, 0:seg, tap:tap + 256],
                                                       col(k, FC["w_sc", l] + kt * 3 + tap), scx[:, kt],
                                                       ALU.mult, ALU.add))
    o.wait()
    sc = b["sc_x"][:, 0:2 * nq]
    dve.tensor_tensor(sc, sc, b["sc_b"][:, 0:2 * nq], ALU.mult).then_inc(k.s("sc_done"), 1)

    k.wait(dve, "latent_std", l, 1)
    o.link(dve.reciprocal(b["std"][:, 0:512 + nq], b["std"][:, 0:512 + nq]))
    dve.scalar_tensor_tensor(b["ckv"], b["ckv"], col(k, FC["g_kv", l]), b["std"][:, 0:512], ALU.mult, ALU.mult)
    for kt in range(2):
        cq = b["cq"][:, kt * nq:kt * nq + nq]
        last = dve.scalar_tensor_tensor(cq, cq, col(k, FC["g_q", l] + kt), b["std"][:, 512:512 + nq],
                                        ALU.mult, ALU.mult)
    last.then_inc(k.s("latent"), 1)
    hk, lk = (h[:, :].rearrange("p (k n) -> p k n", k=KT) for h in (k.h_hi, k.h_lo))
    k.wait(dve, "sc_y", l, 1)
    dve.tensor_tensor(lk[:, 0:2, 0:nq], sc.rearrange("p (k n) -> p k n", k=2), hk[:, 0:2, 0:nq].bitcast(f32),
                      ALU.subtract).then_inc(k.s("sc_y"), 1)
    k.wait(dve, "mla_mm", l, 1)
    k.wait(dve, "bias", l, 1)
    dve.tensor_scalar(b["qr"][:, 0:nq], k.banks(4, nq), MLA_SCALE, None, ALU.mult).then_inc(k.s("qr"), 1)
    o.then(dve.tensor_copy(b["v"], k.banks(2, 1024)))
    cos, sin = k.C[:, C_COS:C_COS + 256], k.C[:, C_SIN:C_SIN + 256]

    def rotate(x, swapped):
        o.then(dve.tensor_tensor(b["rope"], swapped, sin, ALU.mult))
        o.link(dve.tensor_tensor(x, x, cos, ALU.mult))
        ins = dve.tensor_tensor(x, x, b["rope"], ALU.add)
        ins.then_inc(k.s("mla_in"), 1)

    rotate(b["kr"][:, 0:256], k.banks(5, 256))
    k.wait(dve, "cf_mean", l, 1)
    cf = [b["cf_acc"][:, kt * nq:kt * nq + nq] for kt in range(2)]
    for kt in range(2):
        last = dve.scalar_tensor_tensor(cf[kt], k.banks(4, nq), -1.0 / 256, cf[kt], ALU.mult, ALU.add)
    last.then_inc(k.s("cf_cent"), 1)
    k.wait(dve, "swap", l, 1)
    k.wait(dve, "mla_in", l, 1)
    k.wait(dve, "qr", l, 1)
    rotate(b["qr"][:, 0:256], k.banks(5, 256, 256))
    k.wait(dve, "cf_std", l, 1)
    o.link(dve.reciprocal(b["std"][:, 0:nq], b["std"][:, 0:nq]))
    for kt in range(2):
        last = dve.scalar_tensor_tensor(cf[kt], cf[kt], col(k, FC["ln_g", l] + kt), b["std"][:, 0:nq],
                                        ALU.mult, ALU.mult)
    last.then_inc(k.s("cf_norm"), 1)
    k.wait(dve, "cf_y", l, 1)
    dve.tensor_tensor(lk[:, 4:6, 0:nq], k.banks(6, 2 * nq).rearrange("p (k n) -> p k n", k=2),
                      hk[:, 4:6, 0:nq].bitcast(f32), ALU.subtract).then_inc(k.s("cf_y"), 1)

    items = attention_items(l)

    def maxima(i):
        kind, hd, q0, nk, _ = items[i]
        k.wait(dve, "scores", l, i + 1)
        sc2 = k.ps[:, 2 * (i % 2):2 * (i % 2) + 2, :]
        if kind == "na" and q0 == 0:
            bias = b["bias"][:, hd * 512:hd * 512 + 512].rearrange("p (q n) -> p q n", q=2)
            o.link(dve.tensor_tensor(sc2[:, :, 0:256], sc2[:, :, 0:256], bias, ALU.add))
        dve.tensor_reduce(k.tiny[:, 16 + 2 * (i % 2):18 + 2 * (i % 2)], sc2[:, :, 0:nk], AX.X, ALU.max,
                          negate=True).then_inc(k.s("nmax"), 1)

    maxima(0)
    for i, (kind, hd, q0, nk, kt0) in enumerate(items):
        k.wait(dve, "exp", l, i + 1)
        rc = k.tiny[:, 24 + 2 * (i % 2):26 + 2 * (i % 2)]
        o.link(dve.reciprocal(rc, k.tiny[:, 20 + 2 * (i % 2):22 + 2 * (i % 2)]))
        for qt in range(2):
            at = (i % 2) * 1024 + qt * nk
            last = dve.tensor_scalar(b["p"][:, at:at + nk], b["p"][:, at:at + nk], rc[:, qt:qt + 1], None, ALU.mult)
        last.then_inc(k.s("p"), 1)
        if i + 1 < len(items):
            maxima(i + 1)
        k.wait(dve, "pt_mm", l, i + 1)
        if i >= 2:
            k.wait(dve, "o_mm", l, i - 1)
        at = (i % 2) * 1024 + nk
        dve.tensor_copy(b["pt"][:, at:at + nk], k.banks(5, nk)).then_inc(k.s("pt_dve"), 1)
        k.wait(dve, "o_hi", l, i + 1)
        rows, at = slice(64 * (hd % 2), 64 * (hd % 2) + 64), (kt0 + hd // 2) * NT_ALL + q0
        dve.tensor_tensor(k.h_lo[rows, at:at + 256], k.banks(6 + i % 2, 256, 0, rows),
                          k.h_hi[rows, at:at + 256].bitcast(f32), ALU.subtract).then_inc(k.s("o_lo"), 1)

    half = 512 if l == 0 else 256
    for j in range(4):
        c = At(FIRST["out", l] + j)
        feed_lo(k, dve, c + 2)
        dve.wait_ge(k.chunk_mm, c.first + 1)
        t0 = half // 256
        dve.tensor_copy(k.Y[:, t0:2 * t0, j * 256:j * 256 + 256],
                        k.banks(2 * c.pair, half, 512).rearrange("p (t n) -> p t n", n=256)).then_inc(k.dve_read, 1)


def dve_down(k, dve, c, tiles, j):
    feed_lo(k, dve, c + 2)
    dve.wait_ge(k.chunk_mm, c.value(lambda n: n + 1))
    dve.wait_ge(k.dve_read, c.value(lambda n: DVE_READ_COUNT[n - 1]))
    y = k.Y[:, 0:tiles, j * 256:j * 256 + 256]
    products = k.two(c, 256) if tiles == 2 else k.banks(2 * c.pair, 1024).rearrange("p (t n) -> p t n", n=256)
    dve.tensor_tensor(y, products, y,
                      ALU.add).then_inc(k.dve_read, 1)


def dve_mlp(k, dve, o, l):
    tiles = 4 if l == 0 else 2
    n = tiles * 128
    dve_residual(k, dve, o, f"mix{l}", tiles, lambda t: t // 2)
    dve_norm(k, dve, o, f"mlp{l}", tiles, n, NT_ALL)
    dve.wait_ge(k.s("y0", f"mlp{l}"), 1)
    c0 = FIRST["mlp", l]
    with run_loop(dve, GROUPS1) as i:
        o.enter(i, 4)
        for j in range(4):
            feed_lo(k, dve, At(c0 + j + 2, 8, i))
            k.wait(dve, "squared", l, i * 4 + (j + 1))
            r, at = k.R[:, j % 2, 0:2 * n], 2 * j * n
            o.link(dve.tensor_copy(k.g_hi[:, at:at + 2 * n], r))
            dve.tensor_tensor(k.g_lo[:, at:at + 2 * n], r, k.g_hi[:, at:at + 2 * n].bitcast(f32),
                              ALU.subtract).then_inc(k.s("hidden"), 1)
        for j in range(4):
            dve_down(k, dve, At(c0 + 4 + j, 8, i), tiles, j)
    o.leave(GROUPS1)
    dve_residual(k, dve, o, f"mlp{l}", tiles, lambda t: 2 + t // 2)


TWO_PI = 2 * np.pi
C1 = 6.28125
C2 = float(np.float32(np.round((TWO_PI - C1) * 2 ** 20) / 2 ** 20))
C3 = float(np.float32(TWO_PI - C1 - C2))
ROUND = 1.5 * 2 ** 23
PI_IN = 3.1415925


def dve_tables(k, dve, o):
    b = second_buffers(k)
    dve.wait_ge(k.s("second_in"), 32)
    o.link(dve.tensor_copy(b["t0"], b["pos"].bitcast(i32)))
    for n, (cs, sn) in enumerate((("cos_a", "sin_a"), ("cos_b", "sin_b"))):
        a, turns, cs = b[sn], b["t1"], b[cs]
        o.link(dve.tensor_scalar(a, b["t0"], k.C[:, C_INV + n:C_INV + n + 1], None, ALU.mult))
        o.link(dve.tensor_scalar(turns, a, 1.0 / TWO_PI, ROUND, ALU.mult, ALU.add))
        o.link(dve.tensor_scalar(turns, turns, -ROUND, None, ALU.add))
        for part in (C1, C2, C3):
            o.link(dve.scalar_tensor_tensor(a, turns, -part, a, ALU.mult, ALU.add))
        o.link(dve.tensor_scalar(cs, a, np.pi / 2, None, ALU.add))
        o.link(dve.tensor_scalar(turns, cs, PI_IN, -TWO_PI, ALU.is_gt, ALU.mult))
        o.link(dve.tensor_tensor(cs, cs, turns, ALU.add))
        o.link(dve.tensor_scalar(cs, cs, PI_IN, -PI_IN, ALU.min, ALU.max))
        o.link(dve.tensor_scalar(a, a, PI_IN, -PI_IN, ALU.min, ALU.max))
        o.link(dve.tensor_scalar(a, a, k.C[:, C_SIGN + n:C_SIGN + n + 1], None, ALU.mult))
    lam = b["lam"].rearrange("p (a b n) -> p a b n", a=2, b=2)
    o.link(dve.tensor_tensor(b["t1"][:, 0:128].rearrange("p (a n) -> p a n", a=2), lam[:, :, 0, :], lam[:, :, 1, :],
                             ALU.mult))
    dve.tensor_reduce(k.tiny[:, 64:66], b["t1"][:, 0:128].rearrange("p (a n) -> p a n", a=2), AX.X,
                      ALU.add).then_inc(k.s("angles"), 1)
    dve.wait_ge(k.s("lam_exp"), 1)
    o.link(dve.tensor_tensor(k.tiny[:, 68:69], k.tiny[:, 67:68], k.tiny[:, 66:67], ALU.subtract))
    o.link(dve.tensor_scalar(k.tiny[:, 69:70], k.tiny[:, 68:69], -LAM_INIT, None, ALU.add))
    o.link(dve.tensor_scalar(k.tiny[:, 70:71], col(k, FC["head_g2"]), 1.0 - LAM_INIT, None, ALU.mult))


def dve_second(k, dve, o):
    b = second_buffers(k)
    dve_tables(k, dve, o)
    dve_norm(k, dve, o, "mix2", 2, SEQ, SEQ)
    c0 = FIRST["proj2"]
    dve.wait_ge(k.s("tables"), 1)
    turned = 0
    for j in range(24):
        c = At(c0 + j)
        feed_lo(k, dve, c + 2)
        kind = KINDS[c.first]
        if kind in ("va", "vb"):
            at, width = ((j - 4) * 256, 512) if kind == "va" else ((j - 18) * 256, 1536)
            dve_take(k, dve, c, b[kind][:, width + at:width + at + 256], 256, 512).then_inc(k.dve_read, 1)
            continue
        at = {"qa": j, "ka": j - 2, "qb": j - 6, "kb": j - 12}[kind] * 512
        if turned >= 2:
            dve.wait_ge(k.s("rope2"), turned - 1)
        dve.wait_ge(k.chunk_mm, c.first + 1)
        two = lambda ap: ap.rearrange("p (t n) -> p t n", t=2)
        wide = 32 if kind in ("qa", "ka") else 64
        cos, sin = (b["cos_a"], b["sin_a"]) if wide == 32 else (b["cos_b"], b["sin_b"])
        for q in range(128 // wide):
            src, dst = slice(q * wide, q * wide + wide), slice((q ^ 1) * wide, (q ^ 1) * wide + wide)
            m = b["swapped"][dst, (turned % 2) * 512:(turned % 2) * 512 + 512]
            dve.tensor_tensor(two(m), k.two(c, 256, src),
                              sin[src].unsqueeze(1).broadcast_to([wide, 2, 256]), ALU.mult)
        dve.tensor_tensor(two(b[kind][:, at:at + 512]), k.two(c, 256),
                          cos.unsqueeze(1).broadcast_to([128, 2, 256]), ALU.mult).then_inc(k.dve_read, 1)
        turned += 1

    def maxima_a(hd):
        dve.wait_ge(k.s("scores_a"), hd + 1)
        if hd == 0:
            dve.wait_ge(k.s("masks_in"), 16)
        sc = k.banks(2 * (hd % 2), 1024).rearrange("p (c n) -> p c n", c=2)
        o.link(dve.tensor_tensor(sc, sc, b["mask_a"].unsqueeze(1).broadcast_to([128, 2, 512]), ALU.add))
        nm = k.tiny[:, 32 + 4 * (hd % 2):36 + 4 * (hd % 2)]
        o.link(dve.tensor_reduce(nm, k.banks(2 * (hd % 2), 1024).rearrange("p (m n) -> p m n", m=4), AX.X, ALU.max,
                                 negate=True))
        dve.tensor_scalar(k.tiny[:, 40 + 4 * (hd % 2):44 + 4 * (hd % 2)], nm, 0.125, None,
                          ALU.mult).then_inc(k.s("nmax_a"), 1)

    maxima_a(0)
    for hd in range(HEADS):
        dve.wait_ge(k.s("exp_a"), hd + 1)
        rc = k.tiny[:, 56 + 4 * (hd % 2):60 + 4 * (hd % 2)]
        o.link(dve.reciprocal(rc, k.tiny[:, 48 + 4 * (hd % 2):52 + 4 * (hd % 2)]))
        o.link(dve.tensor_scalar(rc[:, 2:4], rc[:, 2:4], k.tiny[:, 69:70], None, ALU.mult))
        p = b["pa"][:, (hd % 2) * 1024:(hd % 2) * 1024 + 1024]
        for qt in range(2):
            o.then(dve.tensor_scalar(p[:, qt * 256:qt * 256 + 256], p[:, qt * 256:qt * 256 + 256],
                                     rc[:, qt:qt + 1], None, ALU.mult))
        o.wait()
        for qt in range(2):
            last = dve.scalar_tensor_tensor(p[:, qt * 256:qt * 256 + 256], p[:, 512 + qt * 256:768 + qt * 256],
                                            rc[:, 2 + qt:3 + qt], p[:, qt * 256:qt * 256 + 256], ALU.mult, ALU.add)
        last.then_inc(k.s("p_a"), 1)
        if hd + 1 < HEADS:
            maxima_a(hd + 1)
        dve.wait_ge(k.s("oa_std"), hd + 1)
        o.link(dve.reciprocal(b["oa_std"], b["oa_std"]))
        o.link(dve.scalar_tensor_tensor(b["oa_f"], k.banks(5, 256), k.tiny[:, 70:71], b["oa_std"], ALU.mult, ALU.mult))
        at = 2048 + hd * 256
        o.link(dve.tensor_copy(k.h_hi[:, at:at + 256], b["oa_f"]))
        dve.tensor_tensor(k.h_lo[:, at:at + 256], b["oa_f"], k.h_hi[:, at:at + 256].bitcast(f32),
                          ALU.subtract).then_inc(k.s("oa"), 1)

    def maxima_b(hd):
        dve.wait_ge(k.s("scores_b"), hd + 1)
        sc = k.banks(0, 1536)
        o.link(dve.tensor_tensor(sc, sc, b["mask_b"], ALU.add))
        o.link(dve.tensor_reduce(k.tiny[:, 72:74], sc.rearrange("p (q n) -> p q n", q=2), AX.X, ALU.max, negate=True))
        dve.tensor_scalar(k.tiny[:, 74:76], k.tiny[:, 72:74], 128 ** -0.5, None, ALU.mult).then_inc(k.s("nmax_b"), 1)

    maxima_b(0)
    for hd in range(HEADS):
        dve.wait_ge(k.s("exp_b"), hd + 1)
        o.link(dve.reciprocal(k.tiny[:, 78:80], k.tiny[:, 76:78]))
        for qt in range(2):
            p = b["pb"][:, qt * 768:qt * 768 + 768]
            last = dve.tensor_scalar(p, p, k.tiny[:, 78 + qt:79 + qt], None, ALU.mult)
        last.then_inc(k.s("p_b"), 1)
        dve.wait_ge(k.s("pt_b_mm"), hd + 1)
        if hd:
            dve.wait_ge(k.s("ob_mm"), hd)
        dve.tensor_copy(b["ptb"][:, 1024:1536], k.banks(5, 512)).then_inc(k.s("pt_b_dve"), 1)
        if hd + 1 < HEADS:
            maxima_b(hd + 1)
        dve.wait_ge(k.s("ob_hi"), hd + 1)
        at = 3072 + hd * 256
        dve.tensor_tensor(k.h_lo[:, at:at + 256], k.banks(6 + hd % 2, 256), k.h_hi[:, at:at + 256].bitcast(f32),
                          ALU.subtract).then_inc(k.s("ob"), 1)

    for j in range(8):
        feed_lo(k, dve, At(FIRST["gates2"] + j + 2))
    dve.wait_ge(k.act_read, ACT_READ_COUNT[FIRST["gates2"] + 7])
    for j in range(4):
        c = At(FIRST["mix2"] + j)
        feed_lo(k, dve, c + 2)
        dve.wait_ge(k.chunk_mm, c.first + 1)
        to = b[("z", "zb")[j // 2]][:, (j % 2) * 1024:(j % 2) * 1024 + 1024]
        dve.tensor_tensor(to, k.banks(2 * c.pair, 1024), b["gate"][:, j * 1024:j * 1024 + 1024],
                          ALU.mult).then_inc(k.dve_read, 1)
    dve.wait_ge(k.dve_read, DVE_READ_COUNT[FIRST["mix2"] + 3])
    dve.tensor_tensor(b["z"], b["z"], b["zb"], ALU.add).then_inc(k.s("z_f"), 1)
    dve.wait_ge(k.s("z_hi"), 1)
    dve.tensor_tensor(k.h_lo[:, 0:2048], b["z"], k.h_hi[:, 0:2048].bitcast(f32), ALU.subtract).then_inc(k.s("z"), 1)
    for j in range(4):
        c = At(FIRST["mix2"] + 4 + j)
        feed_lo(k, dve, c + 2)
        dve_take(k, dve, c, k.Y[:, 1, j * 256:j * 256 + 256], 256, 512).then_inc(k.dve_read, 1)
    dve.wait_ge(k.s("post_in"), 32)
    dve_residual(k, dve, o, "mix2", 2, lambda t: 1)
    dve_norm(k, dve, o, "ffn", 2, SEQ, SEQ)
    dve.wait_ge(k.s("y0", "ffn"), 1)

    def group(i, g0, steps):
        per = 12 if steps == 4 else 0
        for st in range(steps):
            for kind in range(2):
                c = At(FIRST["ffn", g0] + 2 * st + kind, per, i)
                feed_lo(k, dve, c + 2)
                dve.wait_ge(k.act_read, c.value(lambda m: ACT_READ_COUNT[m]))
                for tap in (0, 1):
                    for t in range(2):
                        tile = FC["conv_w2"] + tap * 44 + kind * 22 + (g0 * 4 + st) * 2 + t
                        if per:
                            tile = i * 8 + tile
                        r = k.R[:, st % 2, kind * 512 + t * 256 + 2 - tap:kind * 512 + t * 256 + 256]
                        if tap:
                            o.wait(first[t])
                        ins = dve.scalar_tensor_tensor(r, k.banks(2 * c.pair, 254 + tap, t * 512),
                                                       k.F[:, bass.ds(tile, 1)], r, ALU.mult, ALU.add)
                        if tap == 0:
                            first = {} if t == 0 else first
                            first[t] = o.then(ins)
                ins.then_inc(k.dve_read, 1)
            dve.wait_ge(k.s("gelu"), i * 4 + (st + 1) if per else 4 * g0 + st + 1)
            dve.wait_ge(k.dve_read, At(FIRST["ffn", g0] + 2 * st + 1, per, i).value(lambda m: DVE_READ_COUNT[m]))
            r = k.R[:, st % 2, 0:512]
            o.link(dve.tensor_tensor(r, r, k.R[:, st % 2, 512:1024], ALU.mult))
            o.link(dve.tensor_copy(k.g_hi[:, st * 512:st * 512 + 512], r))
            dve.tensor_tensor(k.g_lo[:, st * 512:st * 512 + 512], r, k.g_hi[:, st * 512:st * 512 + 512].bitcast(f32),
                              ALU.subtract).then_inc(k.s("hidden2"), 1)
        for j in range(4):
            dve_down(k, dve, At(FIRST["ffn", g0] + 2 * steps + j, per, i), 2, j)

    with run_loop(dve, 2) as i:
        o.enter(i, 4 * 6)
        group(i, 0, 4)
    o.leave(2)
    group(0, 2, 3)
    dve_residual(k, dve, o, "ffn", 2, lambda t: 0)


def vector_program(k, dve):
    o = Order(dve, k.dve_order)
    dve.wait_ge(k.s("cond_hi"), 1)
    dve.tensor_tensor(k.cs_lo[:, :], k.tiny[:, 96:112], k.cs_hi[:, :].bitcast(f32),
                      ALU.subtract).then_inc(k.s("cond"), 1)
    feed_lo(k, dve, At(0))
    feed_lo(k, dve, At(1))
    for l in range(DEPTH):
        dve_mod(k, dve, o, l)
        dve_norm(k, dve, o, f"mix{l}", 4, NT_ALL, NT_ALL)
        dve_mixers(k, dve, o, l)
        dve_mlp(k, dve, o, l)
    dve_second(k, dve, o)


def pool_program(k, pool, t):
    b2 = second_buffers(k)

    def rows(ap, parts):
        return bass.AP(ap.tensor, ap.offset, [[0, parts]] + [list(x) for x in ap.ap])

    for hd in range(DEPTH * HEADS):
        pool.dma_start(t["rpb_rows"][hd], rows(t["rpb"][hd], GRID)).then_inc(k.s("rpb_out"), 16)
    pool.wait_ge(k.s("rpb_out"), 16 * DEPTH * HEADS)
    for l in range(DEPTH):
        b = mixer_buffers(k)
        if l:
            pool.wait_ge(k.s("res", f"mlp{l - 1}"), 4)
        into = k.s("rows_in")
        pool.dma_start(k.U[0:2, 6144:12288], rows(t["b_mod"][l], 2)).then_inc(into, 16)
        pool.dma_start(k.Y[:, 0, :], rows(t["gpost"][2 * l], 128)).then_inc(into, 16)
        pool.dma_start(k.Y[:, 1, :], rows(t["gpost"][2 * l + 1], 128)).then_inc(into, 16)
        pool.dma_start(k.Y[0:2, 2, 0:256], t["sel"]).then_inc(into, 16)
        pool.dma_start(k.SW[:, :], t["small"][l]).then_inc(k.s("small_in"), 16)
        if l:
            pool.dma_start(k.GA[:, 1, :], rows(t["gpost"][4], 128)).then_inc(k.s("post_in"), 16)
        pool.wait_ge(k.s("h", f"mix{l}"), KT)
        for hd in range(HEADS):
            for r in range(4):
                at = ((l * HEADS + hd) * GRID) * RPB + (7 - r) * 31 + 15
                src = bass.AP(t["rpb_rows"].tensor, at, [[RPB - 1, GRID], [31, 4], [1, GRID]])
                dst = b["bias"][64 * (r % 2):64 * (r % 2) + 64, hd * 512 + (r // 2) * 256:hd * 512 + (r // 2) * 256 + 256]
                pool.dma_start(dst.rearrange("p (i n) -> p i n", i=4), src).then_inc(k.s("bias_in"), 16)
        pool.dma_start(b["window"], t["window"]).then_inc(k.s("bias_in"), 16)
        k.wait(pool, "bias_in", l, 17 * 16)
        bias = b["bias"].rearrange("p (m n) -> p m n", m=8)
        pool.tensor_tensor(bias, bias, b["window"].unsqueeze(1).broadcast_to([128, 8, 256]),
                           ALU.add).then_inc(k.s("bias"), 1)
        if l:
            pool.dma_start(k.X[:, 2:4, :].rearrange("p t d -> p (t d)"), t["masks2"]).then_inc(k.s("masks_in"), 16)
        pool.wait_ge(k.s("tp", f"mlp{l}"), KT)
        pool.memset(k.Y[:, :, :], 0.0).then_inc(k.s("y0", f"mlp{l}"), 1)
    pool.dma_start(k.GA[:, 0, :], rows(t["gpost"][5], 128)).then_inc(k.s("post_in"), 16)
    pool.wait_ge(k.s("res", "mlp1"), 2)
    pool.dma_start(b2["lam"], rows(t["lam"], 128)).then_inc(k.s("second_in"), 16)
    pool.dma_start(b2["pos"].bitcast(i32), rows(t["pos"][0], 128)).then_inc(k.s("second_in"), 16)
    turned = 0
    for j in range(24):
        n = FIRST["proj2"] + j
        kind = KINDS[n]
        if kind in ("va", "vb"):
            continue
        at = {"qa": j, "ka": j - 2, "qb": j - 6, "kb": j - 12}[kind] * 512
        pool.wait_ge(k.dve_read, DVE_READ_COUNT[n])
        to = b2[kind][:, at:at + 512]
        pool.tensor_tensor(to, to, b2["swapped"][:, (turned % 2) * 512:(turned % 2) * 512 + 512],
                           ALU.add).then_inc(k.s("rope2"), 1)
        turned += 1
    pool.wait_ge(k.s("tp", "ffn"), KT)
    pool.memset(k.Y[:, 0:2, :], 0.0).then_inc(k.s("y0", "ffn"), 1)


def build(nc, t):
    with ExitStack() as stack:
        k = Core(nc, stack)
        block = stack.enter_context(nc.Block())

        @block.sync
        def _(sp):
            sync_program(k, sp, t)

        @block.gpsimd
        def _(pool):
            pool_program(k, pool, t)

        @block.tensor
        def _(pe):
            tensor_program(k, pe)

        @block.scalar
        def _(act):
            scalar_program(k, act)

        @block.vector
        def _(dve):
            vector_program(k, dve)


def chunked(w, rows, cols):
    kt, n = rows // 128, w.shape[1] // cols
    return w.reshape(kt, 128, n, cols).transpose(2, 1, 0, 3).reshape(n, 128, kt * cols)


def padded(chunks):
    out = np.zeros((chunks.shape[0], 128, CHUNK), np.float32)
    out[:, :, :chunks.shape[2]] = chunks
    return out


def weight_stream(a):
    parts = []
    for l in range(DEPTH):
        parts.append(chunked(a["w_mod"][l], D, 256))
        w = a["w_in"][l]
        kv = np.concatenate([w[:, 1024:1152]] + [w[:, 1152:1184]] * 4, axis=1)
        cols = {"sc_x": w[:, 0:256], "sc_b": w[:, 256:512], "sc_c": w[:, 512:768], "q": w[:, 768:1024], "kv": kv,
                "cf_a": w[:, 1184:1440], "cf_g": w[:, 1440:1696], "nq": w[:, 1696:1952], "nk": w[:, 1952:2208],
                "nv": w[:, 2208:2464]}
        parts.append(chunked(np.concatenate([cols[n] for n in WIN], axis=1), D, 256))
        parts.append(chunked(a["w_out"][l], D, 256))
        up = chunked(a["w_mlp1"][l], D, 256)
        for g in range(GROUPS1):
            parts += [up[4 * g:4 * g + 4], chunked(a["w_mlp2"][l][g * D:g * D + D], D, 256)]
    w = a["w_in_2"][0]
    cols = [w[:, 0:1536]] + [w[:, 1536:6144]] + [w[:, 6144:8192]]
    parts.append(chunked(np.concatenate(cols, axis=1), D, 256))
    parts += [chunked(a["w_a_out_2"][0], 512, 512), chunked(a["w_b_out_2"][0], 512, 512),
              chunked(a["w_mix_out_2"][0], D, 256)]
    up, step = chunked(a["w_up_2"][0], D, 256), 0
    for steps in GROUPS2:
        for s in range(step, step + steps):
            parts += [up[s:s + 1], up[11 + s:12 + s]]
        parts.append(padded(chunked(a["w_down_2"][0][step * 256:(step + steps) * 256], steps * 256, 256)))
        step += steps
    out = np.concatenate(parts)
    assert out.shape == (N_CHUNKS, 128, CHUNK), (out.shape, N_CHUNKS)
    return out


def features(v):
    v = v.reshape(-1, v.shape[-1] // 128, 128)
    return v.transpose(2, 0, 1).reshape(128, -1)


def feature_vectors(a):
    cond = np.stack([a["c"][0], a["c_ctx"]])
    out = {"c": features(cond).reshape(128, 2, 8).transpose(0, 2, 1).reshape(128, 16)}
    by_channel = lambda w: features(w).reshape(128, w.shape[0], -1).transpose(0, 2, 1).reshape(128, -1)
    for l in range(DEPTH):
        out["g_pre_mix", l], out["g_pre_mlp", l] = features(a["g_pre_mix"][l]), features(a["g_pre_mlp"][l])
        out["w_sc", l], out["cf_w", l] = by_channel(a["w_sc"][l]), by_channel(a["cf_w_dw"][l])
        out["g_q", l], out["g_kv", l] = features(a["g_q"][l]), features(a["g_kv"][l])
        out["cf_b", l] = features(a["cf_b_dw"][l])
        out["ln_g", l], out["ln_b", l] = features(a["cf_ln_g"][l]), features(a["cf_ln_b"][l])
    out["pre_mix2"], out["pre_ffn2"] = features(a["pre_mix_g_2"][0]), features(a["pre_ffn_g_2"][0])
    out["conv_w2"], out["conv_b2"] = features(a["conv_w_2"][0]), features(a["conv_b_2"][0])
    out["head_g2"] = features(a["diff_head_g_2"][0])
    return np.concatenate([out[key] for key in FC if key != "n"], axis=1)


def small_weights(a):
    out = []
    for l in range(DEPTH):
        uq = a["w_uq"][l].reshape(256, HEADS, 96)
        uq = np.concatenate([uq[:, :, :64].reshape(256, 256), uq[:, :, 64:].reshape(256, 128)], axis=1)
        ukv = a["w_ukv"][l].reshape(128, HEADS, 2, 64).transpose(0, 2, 1, 3).reshape(128, 512)
        out.append(np.concatenate([chunked(uq, 256, 384)[0], ukv, chunked(a["cf_w_pw"][l], 256, 256)[0]], axis=1))
    return np.stack(out)


def shape_constants():
    c = np.zeros((128, C_N), np.float32)
    p = np.arange(128)
    c[:, C_IDENT:C_IDENT + 128] = np.eye(128)
    c[:, C_ONES:C_ONES + 128] = 1
    c[p ^ 8, C_SWAP + p] = 1
    inv = np.float32(10000.0) ** (-np.arange(8, dtype=np.float32) / np.float32(8))
    tok = np.arange(SEQ)
    grid = np.stack([tok // GRID, tok % GRID]).astype(np.float32)
    ang = grid[(p % 32) // 16] * inv[p % 8][:, None]
    c[:, C_COS:C_COS + 256] = np.cos(ang)
    c[:, C_SIN:C_SIN + 256] = np.sin(ang) * np.where(p % 16 < 8, -1, 1)[:, None]
    inv = lambda dim: np.float32(10000.0) ** (-np.arange(0, dim, 2, dtype=np.float32) / np.float32(dim))
    c[:, C_INV], c[:, C_INV + 1] = inv(64)[p % 32], inv(128)[p % 64]
    c[:, C_EPS] = EPS
    c[:, C_SIGN], c[:, C_SIGN + 1] = np.where(p // 32 % 2, -1, 1), np.where(p // 64, -1, 1)
    qc, kc = p % GRID, np.arange(256) % GRID
    start = np.clip(qc - 8, 0, GRID - 16)[:, None]
    window = np.where((kc >= start) & (kc < start + 16), 0, MASKED).astype(np.float32)
    q = (p[:, None] + np.array([0, 128]))[:, :, None, None]
    rel = q - np.arange(256)
    masks = [rel >= 0, (rel >= 0) & (rel <= 128), (rel >= 0) & (rel % 4 == 0), (rel >= 0) & (rel % 16 == 0)]
    masks = np.where(np.concatenate(masks, axis=2), 0, MASKED).astype(np.float32)
    masks2 = np.concatenate([masks[:, :, 0].reshape(128, 512), masks[:, :, 1:].reshape(128, 1536)], axis=1)
    sel = np.repeat(np.eye(2, dtype=np.float32), 128, axis=1)
    return c, window, masks2, sel


def kernel(**inputs):
    import concourse.bacc as bacc
    from concourse.bass_utils import run_bass_kernel_spmd

    a = {name: np.asarray(v) for name, v in inputs.items()}
    consts, window, masks2, sel = shape_constants()
    arrays = {
        "x": a["x"], "ctx": a["ctx"], "feats": feature_vectors(a), "small": small_weights(a),
        "b_mod": a["b_mod"], "rpb": a["na_rpb"].reshape(DEPTH * HEADS, RPB), "lam": a["diff_lambda_2"].reshape(-1),
        "gpost": np.stack([a["g_post_mix"][0], a["g_post_mlp"][0], a["g_post_mix"][1], a["g_post_mlp"][1],
                           a["post_mix_g_2"][0], a["post_ffn_g_2"][0]]),
        "pos": a["positions_2"], "consts": consts, "window": window, "masks2": masks2, "sel": sel,
        "stream": weight_stream(a),
    }
    nc = bacc.Bacc("TRN2", target_bir_lowering=False, num_devices=1)
    t = {}
    for name, v in arrays.items():
        arrays[name] = v = np.ascontiguousarray(v)
        t[name] = nc.dram_tensor(f"in_{name}", v.shape, mybir.dt.from_np(v.dtype), kind="ExternalInput").ap()
    t["rpb_rows"] = nc.dram_tensor("rpb_rows", (DEPTH * HEADS, GRID, RPB), f32, kind="Internal").ap()
    t["out"] = nc.dram_tensor("out", (1, SEQ, D), f32, kind="ExternalOutput").ap()
    build(nc, t)
    got = run_bass_kernel_spmd(nc, [{f"in_{name}": v for name, v in arrays.items()}], core_ids=[0])
    return got.results[0]["out"]
```

```python
import numpy as np
from contextlib import ExitStack

import concourse.bass as bass
from concourse import mybir

D = 1024
SEQ = 256
CTX = 256
NT_ALL = SEQ + CTX
DEPTH = 2
KT = D // 128
GRID = 64
RPB = 15 * 31
HEADS = 4
MLA_SCALE = 96 ** -0.5
NA_SCALE = 64 ** -0.5
CF_K = 31
EPS = 1e-6
MASKED = -1e30
FF2 = 2816
LAM_INIT = 0.2
CHUNK = 2048
HALF = CHUNK // 2
SLOTS = 4

MOD_WHOLE = [range(0, 10), range(2, 8)]

WIN = ["cf_a", "cf_g", "kv", "q", "nk", "nq", "nv", "sc_x", "sc_c", "sc_b"]
WIN_ALL_TOKENS = ("kv", "nk", "nv")
GROUPS1 = 4
GROUPS2 = [4, 4, 3]


def chunk_kinds():
    kinds, first = [], {}

    def add(key, names):
        first[key] = len(kinds)
        kinds.extend(names)

    for l in range(DEPTH):
        add(("mod", l), ["mod_whole" if j in MOD_WHOLE[l] else "mod" for j in range(24)])
        add(("win", l), WIN)
        add(("out", l), ["out"] * 4)
        add(("mlp", l), (["up"] * 4 + ["down"] * 4) * GROUPS1)
    add("proj2", ["qa", "qa", "ka", "ka", "va", "va"] + ["qb"] * 6 + ["kb"] * 6 + ["vb"] * 6)
    add("gates2", ["gate"] * 8)
    add("mix2", ["a_out"] * 2 + ["b_out"] * 2 + ["mix"] * 4)
    for g, steps in enumerate(GROUPS2):
        add(("ffn", g), ["up_gate", "up_val"] * steps + ["down2"] * 4)
    return kinds, first


KINDS, FIRST = chunk_kinds()
N_CHUNKS = len(KINDS)
ACT_READS = {"cf_a", "cf_g", "kv", "q", "nk", "nq", "nv", "sc_x", "sc_b", "out", "up", "va", "vb", "gate",
             "mix", "up_gate", "up_val"}
DVE_READS = {"mod", "mod_whole", "cf_a", "kv", "q", "nk", "nq", "nv", "sc_x", "sc_c", "sc_b", "out", "down", "qa", "ka",
             "va", "qb", "kb", "vb", "a_out", "b_out", "mix", "up_gate", "up_val", "down2"}


def running(of):
    total, out = 0, []
    for k in KINDS:
        total += k in of
        out.append(total)
    return out + [total] * 2


ACT_READ_COUNT = running(ACT_READS)
DVE_READ_COUNT = running(DVE_READS)
SPLIT_COUNT = running(set(KINDS) - {"mod_whole"})


class At:

    def __init__(self, first, per=0, i=0):
        self.first, self.per, self.i = first, per, i

    def __add__(self, n):
        return At(self.first + n, self.per, self.i)

    def value(self, count):
        if not self.per:
            return count(self.first)
        step = count(self.first + self.per + 2) - count(self.first + 2)
        return self.i * step + (count(self.first + self.per) - step)

    @property
    def slot(self):
        return self.first % SLOTS

    @property
    def pair(self):
        return self.first % 2


STATS_AT = [3, 5]
SECTIONS_AT = [8, 20]
NORM_AT = list(range(9, 9 + KT))


HEAD_A = 6


def head_steps(j):
    n = j - HEAD_A
    return [(head, step) for step, at in (("norm", 4), ("scores", 0), ("transposes", 2), ("values", 3))
            for head in range(HEADS) if n == 4 * head + at]


KEEP = {"cf_sq": (3, 2), "latent": (4, 3), "item": (2, 4)}


def feature_columns():
    cols, at = {}, 0

    def add(key, n):
        nonlocal at
        cols[key] = at
        at += n

    add("c", 16)
    for l in range(DEPTH):
        for key, n in (("g_pre_mix", 8), ("g_pre_mlp", 8), ("w_sc", 6), ("g_q", 2), ("g_kv", 1),
                       ("cf_w", 62), ("cf_b", 2), ("ln_g", 2), ("ln_b", 2)):
            add((key, l), n)
    for key, n in (("pre_mix2", 8), ("pre_ffn2", 8), ("conv_w2", 132), ("conv_b2", 44), ("head_g2", 1)):
        add(key, n)
    cols["n"] = at
    return cols


FC = feature_columns()
C_IDENT, C_ONES, C_SWAP, C_COS, C_SIN, C_INV, C_EPS, C_ZERO, C_SIGN = 0, 128, 256, 384, 640, 896, 898, 899, 900
C_N = 902

f32, f32r, i32 = mybir.dt.float32, mybir.dt.float32r, mybir.dt.int32
ALU, ACT, AX = mybir.AluOpType, mybir.ActivationFunctionType, mybir.AxisListType
SMALL_N = 2 * 384 + 512 + 512



FIRST_LAYER = {"b_mod_in": 16, "gpost_in": 32, "small_in": 16, "bias_in": 17 * 16, "mod_t": 2, "mod_feat": 2,
               "mod_gain": 2, "gate_in": 2, "gate_rows": 2, "gates": 2, "latent_sq": 2, "mla_mm": 3, "mla_in": 2, "cf_y": 2, "sc_y": 2, "hidden": 16, "squared": 16}
FIRST_LAYER.update({step: 16 for step in ("scores", "nmax", "exp", "p", "pt_mm", "pt_act", "pt_dve", "o_mm", "o_hi",
                                          "o_lo")})


class Core:

    def __init__(self, nc, stack):
        def sb(name, shape, dt=f32, to=stack):
            return to.enter_context(nc.sbuf_tensor(name, shape, dt))

        def sem(name):
            return stack.enter_context(nc.semaphore(name))

        self.nc = nc
        loaded = ExitStack()
        self.w = sb("w", [128, SLOTS, CHUNK], f32, loaded)
        loaded.close()
        self.w_lo = sb("w_lo", [128, SLOTS, CHUNK], f32r)
        self.w_hi = sb("w_hi", [128, SLOTS, CHUNK], f32r)
        self.X = sb("X", [128, 4, D])
        self.Y = sb("Y", [128, 4, D])
        self.h_hi = sb("h_hi", [128, KT * NT_ALL], f32r)
        self.h_lo = sb("h_lo", [128, KT * NT_ALL], f32r)
        self.GA = sb("GA", [128, 4, D])
        self.F = sb("F", [128, FC["n"]])
        self.C = sb("C", [128, C_N])
        self.SW = sb("SW", [128, SMALL_N])
        self.tiny = sb("tiny", [128, 128])
        self.cs_hi = sb("cs_hi", [128, 16], f32r)
        self.cs_lo = sb("cs_lo", [128, 16], f32r)
        self.mod_feat = sb("mod_feat", [128, 64])
        self.mod_gain = sb("mod_gain", [128, 32])
        attention = ExitStack()
        self.U = sb("U", [128, 12416], f32, attention)
        attention.close()
        self.g_hi = sb("g_hi", [128, KT * NT_ALL], f32r)
        self.g_lo = sb("g_lo", [128, KT * NT_ALL], f32r)
        self.R = sb("R", [128, 2, 1024])
        self.hf = sb("hf", [128, 2, 1024])
        self.ps = stack.enter_context(nc.psum_tensor("ps", [128, 8, 512], f32))

        self.w_loaded = [sem(f"w_loaded{r}") for r in range(SLOTS)]
        self.hi_done = sem("hi_done")
        self.lo_done = sem("lo_done")
        self.chunk_mm = sem("chunk_mm")
        self.act_read = sem("act_read")
        self.dve_read = sem("dve_read")
        self.act_order, self.dve_order, self.pool_order = sem("act_order"), sem("dve_order"), sem("pool_order")
        self.sems = {}
        self.make = sem

    def s(self, *name):
        name = "_".join(str(n) for n in name)
        if name not in self.sems:
            self.sems[name] = self.make(name)
        return self.sems[name]

    def wait(self, eng, name, l, value):
        eng.wait_ge(self.s(name), value + l * FIRST_LAYER.get(name, 1))

    def banks(self, b, n, at=0, parts=slice(0, 128)):
        flat = self.ps[:, :, :].rearrange("p b n -> p (b n)")
        return flat[parts, b * 512 + at:b * 512 + at + n]

    def two(self, c, n, parts=slice(0, 128)):
        return self.ps[parts, 2 * c.pair:2 * c.pair + 2, 0:n]


class Order:

    def __init__(self, eng, sem):
        self.eng, self.sem, self.n, self.base = eng, sem, 0, 0

    def then(self, ins):
        ins.then_inc(self.sem, 1)
        self.n += 1
        return self.n

    def wait(self, n=None):
        self.eng.wait_ge(self.sem, self.base + (self.n if n is None else n))

    def link(self, ins):
        self.wait(self.then(ins))

    def enter(self, i, per):
        self.base, self.per, self.start = i * per, per, self.n

    def leave(self, times):
        assert self.n - self.start == self.per, (self.n - self.start)
        self.n, self.base = self.start + self.per * times, 0


def run_loop(eng, times):
    return eng.Fori(0, times)


def feed_hi(k, act, c):
    if c.first >= N_CHUNKS or KINDS[c.first] == "mod_whole":
        return
    act.wait_ge(k.w_loaded[c.slot], c.value(lambda n: 16 * (n // SLOTS + 1)))
    for half in (slice(0, HALF), slice(HALF, CHUNK)):
        act.activation(k.w_hi[:, c.slot, half], k.w[:, c.slot, half], ACT.Copy).then_inc(k.hi_done, 1)


def feed_lo(k, dve, c):
    if c.first >= N_CHUNKS or KINDS[c.first] == "mod_whole":
        return
    for n_half, half in enumerate((slice(0, HALF), slice(HALF, CHUNK))):
        dve.wait_ge(k.hi_done, c.value(lambda n: 2 * SPLIT_COUNT[n] + n_half - 1))
        dve.tensor_tensor(k.w_lo[:, c.slot, half], k.w[:, c.slot, half], k.w_hi[:, c.slot, half].bitcast(f32),
                          ALU.subtract).then_inc(k.lo_done, 1)


def sync_program(k, sp, t):
    def load(c, c_dyn=None):
        src = t["stream"][bass.ds(c.value(lambda n: n), 1)].rearrange("o p n -> (o p) n")
        if c.first >= SLOTS:
            sp.wait_ge(k.chunk_mm, c.value(lambda n: n - SLOTS + 1))
        sp.dma_start(k.w[:, c.slot, :], src).then_inc(k.w_loaded[c.slot], 16)

    sp.dma_start(k.F[:, :], t["feats"]).then_inc(k.s("feats_in"), 16)
    for r in range(SLOTS):
        load(At(r))
    sp.dma_start(k.X[:, 0:2, :], t["x"].rearrange("o (t p) d -> p (o t) d", p=128)).then_inc(k.s("x_in"), 16)
    sp.dma_start(k.X[:, 2:4, :], t["ctx"].rearrange("o (t p) d -> p (o t) d", p=128)).then_inc(k.s("x_in"), 16)
    sp.dma_start(k.C[:, :], t["consts"]).then_inc(k.s("consts_in"), 16)
    whole = N_CHUNKS // SLOTS
    with sp.Fori(0, whole - 1) as i:
        for r in range(SLOTS):
            load(At(SLOTS + r, SLOTS, i))
    for n in range(whole * SLOTS, N_CHUNKS):
        load(At(n))
    out = t["out"].rearrange("o (t p) d -> p (o t) d", p=128)
    for tile in range(2):
        sp.wait_ge(k.s("res", "ffn"), tile + 1)
        sp.dma_start(out[:, tile, :], k.X[:, tile, :]).then_inc(k.s("out_done"), 16)
    sp.wait_ge(k.s("out_done"), 32)


def mixer_buffers(k):
    U, Yf = k.U, k.Y[:, :, :].rearrange("p t d -> p (t d)")
    b = {}
    for name, at, n in (("bias", 0, 2048), ("cf_a", 2048, 1024), ("cf_g", 3072, 1024), ("cf_in", 4096, 1144),
                        ("cf_acc", 5240, 1024), ("ckv", 6264, 512), ("ckv_sq", 6776, 512), ("kr", 7288, 512),
                        ("cq", 7800, 1024), ("sc_x", 8824, 1024), ("sc_in", 9848, 1032), ("sc_b", 10880, 1024),
                        ("qr", 11904, 512), ("sq", 2048, 1024), ("std", 3072, 1024), ("p", 2048, 2048),
                        ("pt", 4096, 2048), ("qn", 7800, 1024), ("kn", 6264, 1024), ("rope", 10880, 256),
                        ("window", 11904, 256)):
        b[name] = U[:, at:at + n]
    for name, at in (("na_q", 0), ("na_k", 1024), ("na_v", 2048), ("v", 3072)):
        b[name] = Yf[:, at:at + 1024]
    return b


def attention_items(l):
    items = [("mla", h, 0, 512, 2) for h in range(HEADS)] + [("na", h, 0, 512, 6) for h in range(HEADS)]
    if l == 0:
        items += [("mla", h, 256, 256, 2) for h in range(HEADS)] + [("na", h, 256, 256, 6) for h in range(HEADS)]
    return items


PASSES = (("hi", "hi"), ("hi", "lo"), ("lo", "hi"))


def chunk_waits(k, pe, c):
    for sem, count in ((k.act_read, ACT_READ_COUNT), (k.dve_read, DVE_READ_COUNT)):
        if c.first >= 2 and count[c.first - 2]:
            pe.wait_ge(sem, c.value(lambda n: count[n - 2]))


def half_wait(k, pe, c, half):
    pe.wait_ge(k.lo_done, c.value(lambda n: 2 * SPLIT_COUNT[n] + half - 1))


def to_features(k, pe, c, h, kts, width, tiles, n, stride, before_kt=None):
    chunk_waits(k, pe, c)
    w = {"hi": k.w_hi, "lo": k.w_lo}
    for j in range(tiles):
        for kt in range(kts):
            if j == 0 and kt * width in (0, HALF):
                half_wait(k, pe, c, kt * width // HALF)
            if j == 0 and before_kt:
                before_kt(kt)
            for p, (a, b) in enumerate(PASSES):
                at = kt * width + j * 128
                last = pe.matmul(k.banks(2 * c.pair, n, j * (512 if tiles == 2 else n)), w[a][:, c.slot, at:at + 128],
                                 h[b][:, kt * stride:kt * stride + n],
                                 start=kt == 0 and p == 0, stop=kt == kts - 1 and p == 2)
    last.then_inc(k.chunk_mm, 1)


def to_tokens(k, pe, c, h, kts, n_tiles, stride, m=128, late=None):
    chunk_waits(k, pe, c)
    w = {"hi": k.w_hi, "lo": k.w_lo}

    def products(t, kt0, kt1):
        for kt in range(kt0, kt1):
            if t == 0 and kt in (0, 4):
                half_wait(k, pe, c, kt // 4)
            for p, (a, b) in enumerate(PASSES):
                at = kt * stride + t * 128
                last = pe.matmul(k.banks(2 * c.pair, 256, t * (512 if n_tiles == 2 else 256), slice(0, m)),
                                 h[a][:, at:at + m], w[b][:, c.slot, kt * 256:kt * 256 + 256],
                                 start=kt == 0 and p == 0, stop=kt == kts - 1 and p == 2)
        return last

    if late:
        first = range(0, n_tiles, n_tiles // 2)
        for t in first:
            products(t, 0, late[0])
        late[1]()
        for t in first:
            last = products(t, late[0], kts)
        rest = [t for t in range(n_tiles) if t not in first]
    else:
        rest = range(n_tiles)
    for t in rest:
        last = products(t, 0, kts)
    last.then_inc(k.chunk_mm, 1)


def keep_clock(k, pe, bank, times, n=512):
    for _ in range(times):
        pe.matmul(k.banks(bank, n), k.C[:, C_IDENT:C_IDENT + 128], k.C[:, 0:n], start=True, stop=True)


def pe_transposed(k, pe, name, tiles, kt):
    if kt == 0:
        pe.wait_ge(k.s("xn", name), tiles)
    if kt >= 4:
        pe.wait_ge(k.s("hf", name), kt - 3)
    for t in range(tiles):
        last = pe.transpose(k.banks(4 + kt % 4, 128, t * 128), k.Y[:, t, kt * 128:kt * 128 + 128],
                            k.C[:, C_IDENT:C_IDENT + 128])
    last.then_inc(k.s("tp", name), 1)


def pe_norm(k, pe, name, tiles):
    for kt in range(KT):
        pe_transposed(k, pe, name, tiles, kt)


def pe_mod(k, pe, l):
    c0 = FIRST["mod", l]
    if l == 0:
        pe.wait_ge(k.s("cond"), 1)
    cs = {"hi": k.cs_hi, "lo": k.cs_lo}

    def transposed_sections(which):
        pe.wait_ge(k.dve_read, DVE_READ_COUNT[c0 + (7, 19)[which]])
        if l == 0 and which == 0:
            pe.wait_ge(k.s("consts_in"), 16)
        for n, sec in enumerate(((0, 1), (3, 4))[which]):
            for kt in range(KT):
                last = pe.transpose(k.banks(1 + 2 * which, 2, n * 16 + kt * 2),
                                    k.U[0:2, sec * D + kt * 128:sec * D + kt * 128 + 128], k.C[0:2, C_IDENT:C_IDENT + 2])
        last.then_inc(k.s("mod_t"), 1)

    for j in range(24):
        if j in MOD_WHOLE[l]:
            c = At(c0 + j)
            chunk_waits(k, pe, c)
            pe.wait_ge(k.w_loaded[c.slot], 16 * (c.first // SLOTS + 1))
            for kt in range(KT):
                last = pe.matmul(k.banks(2 * c.pair, 256, 0, slice(0, 2)), k.tiny[:, 96 + kt * 2:98 + kt * 2],
                                 k.w[:, c.slot, kt * 256:kt * 256 + 256], start=kt == 0, stop=kt == KT - 1)
            last.then_inc(k.chunk_mm, 1)
        else:
            to_tokens(k, pe, At(c0 + j), cs, KT, 1, 2, m=2)
        if j in SECTIONS_AT:
            transposed_sections(SECTIONS_AT.index(j))
        if j in NORM_AT:
            pe_transposed(k, pe, f"mix{l}", 4, NORM_AT.index(j))


def pe_gate_rows(k, pe, l, which, bank):
    k.wait(pe, "gate_in", l, which + 1)
    for v in range(2 if l == 0 else 1):
        pick = k.C[0:2, C_IDENT + v:C_IDENT + v + 1].broadcast_to([2, 128])
        for half in range(2):
            last = pe.matmul(k.banks(bank + 2 * v + half, 512), pick, k.GA[0:2, 2 * which, half * 512:half * 512 + 512],
                             start=True, stop=True)
    last.then_inc(k.s("gate_rows"), 1)


def pe_mixers(k, pe, l):
    b = mixer_buffers(k)
    nq = NT_ALL if l == 0 else SEQ
    ones, swap = k.C[:, C_ONES:C_ONES + 128], k.C[:, C_SWAP:C_SWAP + 128]
    h = {"hi": k.h_hi, "lo": k.h_lo}
    c0 = FIRST["win", l]
    for j, kind in enumerate(WIN):
        n = NT_ALL if kind in WIN_ALL_TOKENS else nq
        if kind == "nv":
            to_tokens(k, pe, At(c0 + j), h, KT, 4, NT_ALL)
        else:
            to_features(k, pe, At(c0 + j), h, KT, 256, 2, n, NT_ALL,
                        before_kt=None if j else lambda kt: pe.wait_ge(k.s("h", f"mix{l}"), kt + 1))
        if j == 0:
            pe_gate_rows(k, pe, l, 1, 4)

    k.wait(pe, "latent_sq", l, 2)
    k.wait(pe, "gates", l, 1)
    pe.matmul(k.banks(4, 512), ones, b["ckv_sq"], start=True, stop=True)
    for kt in range(2):
        last = pe.matmul(k.banks(5, nq), ones, b["sq"][:, kt * nq:kt * nq + nq], start=kt == 0, stop=kt == 1)
    last.then_inc(k.s("latent_ssq"), 1)
    k.wait(pe, "cf_conv", l, 1)
    for kt in range(2):
        last = pe.matmul(k.banks(6, nq), ones, b["cf_acc"][:, kt * nq:kt * nq + nq], start=kt == 0, stop=kt == 1)
    last.then_inc(k.s("cf_mean"), 1)
    pe.wait_ge(k.act_read, ACT_READ_COUNT[c0 + 9])
    pe.wait_ge(k.dve_read, DVE_READ_COUNT[c0 + 9])
    pe_gate_rows(k, pe, l, 0, 0)
    keep_clock(k, pe, 7, KEEP["cf_sq"][l])
    k.wait(pe, "cf_sq", l, 1)
    for kt in range(2):
        last = pe.matmul(k.banks(7, nq), ones, b["sq"][:, kt * nq:kt * nq + nq], start=kt == 0, stop=kt == 1)
    last.then_inc(k.s("cf_var"), 1)
    keep_clock(k, pe, 6, KEEP["latent"][l])
    k.wait(pe, "latent", l, 1)
    k.wait(pe, "small_in", l, 16)

    def query(j, to):
        for kt in range(2):
            last = pe.matmul(k.banks(to, nq), k.SW[:, kt * 384 + j * 128:kt * 384 + j * 128 + 128],
                             b["cq"][:, kt * nq:kt * nq + nq], start=kt == 0, stop=kt == 1)
        return last

    pe.matmul(k.banks(5, 256), swap, b["kr"][:, 0:256], start=True, stop=True)
    query(2, 4).then_inc(k.s("mla_mm"), 1)
    k.wait(pe, "cf_std", l, 1)
    for j in range(2):
        pe.matmul(k.banks(6 + j, 512), k.SW[:, 768 + j * 128:768 + j * 128 + 128], b["ckv"],
                  start=True, stop=True)
    k.wait(pe, "gates", l, 2)
    for t in range(4):
        last = pe.matmul(k.banks(2, 256, t * 256), b["ckv"][:, t * 128:t * 128 + 128], k.SW[:, 1024:1280],
                         start=True, stop=True)
    last.then_inc(k.s("mla_mm"), 1)
    query(0, 0)
    query(1, 1).then_inc(k.s("mla_mm"), 1)
    k.wait(pe, "qr", l, 1)
    k.wait(pe, "mla_in", l, 1)
    pe.matmul(k.banks(5, 256, 256), swap, b["qr"][:, 0:256], start=True, stop=True).then_inc(k.s("swap"), 1)
    k.wait(pe, "mla_kv", l, 1)
    k.wait(pe, "cf_act", l, 1)
    for j in range(2):
        for kt in range(2):
            last = pe.matmul(k.banks(6, nq, j * nq), k.SW[:, 1280 + kt * 256 + j * 128:1280 + kt * 256 + j * 128 + 128],
                             b["cf_acc"][:, kt * nq:kt * nq + nq], start=kt == 0, stop=kt == 1)
    last.then_inc(k.s("cf_mm"), 1)

    items = attention_items(l)
    ident = k.C[:, C_IDENT:C_IDENT + 128]
    k.wait(pe, "mla_in", l, 2)
    k.wait(pe, "mla_q", l, 1)

    def scores(i):
        kind, hd, q0, nk, _ = items[i]
        k0 = 0 if nk == 512 else 256
        rows = slice(64 * (hd % 2), 64 * (hd % 2) + 64)
        rot = slice(32 * hd, 32 * hd + 32)
        if i >= 2:
            k.wait(pe, "exp", l, i - 1)
        for qt in range(2):
            q = q0 + qt * 128
            to = k.banks(2 * (i % 2) + qt, nk)
            if kind == "mla":
                qa, ka = (hd // 2) * nq + q, (hd // 2) * 512 + k0
                pe.matmul(to, b["qn"][rows, qa:qa + 128], b["kn"][rows, ka:ka + nk], start=True, stop=False)
                last = pe.matmul(to, b["qr"][rot, q:q + 128], b["kr"][rot, k0:k0 + nk], start=False, stop=True)
            else:
                qa, ka = (hd // 2) * nq + q, (hd // 2) * 512 + k0
                last = pe.matmul(to, b["na_q"][rows, qa:qa + 128], b["na_k"][rows, ka:ka + nk], start=True, stop=True)
        last.then_inc(k.s("scores"), 1)

    def transposes(i):
        nk = items[i][3]
        if i >= 1:
            k.wait(pe, "pt_act", l, i)
            k.wait(pe, "pt_dve", l, i)
            keep_clock(k, pe, 4, KEEP["item"][nk // 512], 256)
        k.wait(pe, "p", l, i + 1)
        if i == 0:
            k.wait(pe, "cf_y", l, 2)
        for kt in range(nk // 128):
            for qt in range(2):
                at = qt * nk + kt * 128
                last = pe.transpose(k.banks(4 + kt // (nk // 256), 128, kt % (nk // 256) * 256 + qt * 128),
                                    b["p"][:, (i % 2) * 1024 + at:(i % 2) * 1024 + at + 128], ident)
        last.then_inc(k.s("pt_mm"), 1)

    def values(i):
        kind, hd, q0, nk, _ = items[i]
        v = b["v"] if kind == "mla" else b["na_v"]
        t0 = 0 if nk == 512 else 2
        k.wait(pe, "pt_act", l, i + 1)
        k.wait(pe, "pt_dve", l, i + 1)
        if i >= 2:
            k.wait(pe, "o_lo", l, i - 1)
        rows = slice(64 * (hd % 2), 64 * (hd % 2) + 64)
        for kt in range(nk // 128):
            at = (t0 + kt) * 256 + hd * 64
            last = pe.matmul(k.banks(6 + i % 2, 256, 0, rows), v[:, at:at + 64],
                             b["pt"][:, (i % 2) * 1024 + kt * 256:(i % 2) * 1024 + kt * 256 + 256],
                             start=kt == 0, stop=kt == nk // 128 - 1)
        last.then_inc(k.s("o_mm"), 1)

    scores(0)
    for i in range(len(items)):
        if i + 1 < len(items):
            scores(i + 1)
        transposes(i)
        values(i)

    k.wait(pe, "o_lo", l, len(items))
    k.wait(pe, "sc_y", l, 2)
    tiles = 4 if l == 0 else 2
    for j in range(4):
        to_tokens(k, pe, At(FIRST["out", l] + j), h, KT, tiles, NT_ALL)


def pe_mlp(k, pe, l):
    tiles = 4 if l == 0 else 2
    n = tiles * 128
    h, g = {"hi": k.h_hi, "lo": k.h_lo}, {"hi": k.g_hi, "lo": k.g_lo}
    pe_norm(k, pe, f"mlp{l}", tiles)
    c0 = FIRST["mlp", l]
    with run_loop(pe, GROUPS1) as i:
        for j in range(4):
            to_features(k, pe, At(c0 + j, 8, i), h, KT, 256, 2, n, NT_ALL,
                        before_kt=None if j else lambda kt: pe.wait_ge(k.s("h", f"mlp{l}"), kt + 1))
        k.wait(pe, "hidden", l, i * 4 + 3)
        for j in range(4):
            to_tokens(k, pe, At(c0 + 4 + j, 8, i), g, KT, tiles, n,
                      late=(6, lambda: k.wait(pe, "hidden", l, i * 4 + 4)) if j == 0 else None)


def pe_second(k, pe):
    h, g = {"hi": k.h_hi, "lo": k.h_lo}, {"hi": k.g_hi, "lo": k.g_lo}
    b = second_buffers(k)
    ones, ident = k.C[:, C_ONES:C_ONES + 128], k.C[:, C_IDENT:C_IDENT + 128]
    pe_norm(k, pe, "mix2", 2)
    c0 = FIRST["proj2"]

    def step_a(hd, step):
        if step == "scores":
            if hd == 0:
                pe.wait_ge(k.s("rope2"), 4)
            else:
                pe.wait_ge(k.s("exp_a"), hd)
            for cmp in range(2):
                rows = slice(64 * cmp, 64 * cmp + 64)
                for qt in range(2):
                    last = pe.matmul(k.banks(4, 256, (cmp * 2 + qt) * 256),
                                     b["qa"][rows, hd * 256 + qt * 128:hd * 256 + qt * 128 + 128],
                                     b["ka"][rows, hd * 256:hd * 256 + 256], start=True, stop=True)
            last.then_inc(k.s("scores_a"), 1)
        elif step == "transposes":
            pe.wait_ge(k.s("p_a"), hd + 1)
            if hd:
                pe.wait_ge(k.s("pt_a"), hd)
            for kt in range(2):
                for qt in range(2):
                    at = (hd % 2) * 1024 + qt * 256 + kt * 128
                    last = pe.transpose(k.banks(6, 128, kt * 256 + qt * 128), b["pa"][:, at:at + 128], ident)
            last.then_inc(k.s("pt_a_mm"), 1)
        elif step == "values":
            if hd == 0:
                pe.wait_ge(k.act_read, ACT_READ_COUNT[c0 + 5])
                pe.wait_ge(k.dve_read, DVE_READ_COUNT[c0 + 5])
            pe.wait_ge(k.s("pt_a"), hd + 1)
            if hd:
                pe.wait_ge(k.s("oa"), hd)
            for kt in range(2):
                last = pe.matmul(k.banks(7, 256), b["va"][:, kt * 512 + hd * 128:kt * 512 + hd * 128 + 128],
                                 b["pta"][:, (hd % 2) * 512 + kt * 256:(hd % 2) * 512 + kt * 256 + 256],
                                 start=kt == 0, stop=kt == 1)
            last.then_inc(k.s("oa_mm"), 1)
        else:
            pe.wait_ge(k.s("oa_sq"), hd + 1)
            pe.matmul(k.banks(7, 256, 256), ones, b["oa_sq"], start=True, stop=True).then_inc(k.s("oa_ssq"), 1)

    for j in range(24):
        c = At(c0 + j)
        if KINDS[c.first] in ("va", "vb"):
            to_tokens(k, pe, c, h, KT, 2, SEQ)
        else:
            to_features(k, pe, c, h, KT, 256, 2, SEQ, SEQ,
                        before_kt=None if j else lambda kt: pe.wait_ge(k.s("h", "mix2"), kt + 1))
        for hd, step in head_steps(j):
            step_a(hd, step)

    def scores_b(hd):
        if hd:
            pe.wait_ge(k.s("pt_b_act"), hd)
            pe.wait_ge(k.s("pt_b_dve"), hd)
        for qt in range(2):
            for grp in range(3):
                at = (grp * 4 + hd) * 256
                last = pe.matmul(k.banks(4, 256, qt * 768 + grp * 256), b["qb"][:, at + qt * 128:at + qt * 128 + 128],
                                 b["kb"][:, at:at + 256], start=True, stop=True)
        last.then_inc(k.s("scores_b"), 1)

    def values_b(hd):
        pe.wait_ge(k.s("pt_b_act"), hd + 1)
        pe.wait_ge(k.s("pt_b_dve"), hd + 1)
        if hd:
            pe.wait_ge(k.s("ob"), hd)
        for n in range(6):
            grp, kt = n // 2, n % 2
            at = kt * 1536 + (grp * 4 + hd) * 128
            last = pe.matmul(k.banks(7, 256), b["vb"][:, at:at + 128], b["ptb"][:, n * 256:n * 256 + 256],
                             start=n == 0, stop=n == 5)
        last.then_inc(k.s("ob_mm"), 1)

    def gate(j):
        to_features(k, pe, At(FIRST["gates2"] + j), h, KT, 256, 2, SEQ, SEQ)

    pe.wait_ge(k.act_read, ACT_READ_COUNT[c0 + 23])
    pe.wait_ge(k.dve_read, DVE_READ_COUNT[c0 + 23])
    pe.wait_ge(k.s("rope2"), 16)
    pe.wait_ge(k.s("oa"), HEADS)
    scores_b(0)
    for hd in range(HEADS):
        gate(2 * hd)
        pe.wait_ge(k.s("p_b"), hd + 1)
        for grp in range(3):
            for kt in range(2):
                for qt in range(2):
                    at = qt * 768 + grp * 256 + kt * 128
                    last = pe.transpose(k.banks(4, 128, (grp * 2 + kt) * 256 + qt * 128), b["pb"][:, at:at + 128],
                                        ident)
        last.then_inc(k.s("pt_b_mm"), 1)
        gate(2 * hd + 1)
        if hd + 1 < HEADS:
            scores_b(hd + 1)
        values_b(hd)

    pe.wait_ge(k.s("ob"), HEADS)
    for j in range(4):
        o = {p: h[p][:, 2048 + (j // 2) * 1024:2048 + (j // 2) * 1024 + 1024] for p in h}
        to_features(k, pe, At(FIRST["mix2"] + j), o, 4, 512, 4, SEQ, SEQ)
    pe.wait_ge(k.s("z"), 1)
    for j in range(4):
        to_tokens(k, pe, At(FIRST["mix2"] + 4 + j), h, KT, 2, SEQ,
                  late=None if j else (4, lambda: pe.wait_ge(k.s("z"), 2)))

    pe_norm(k, pe, "ffn", 2)

    def group(i, g0, steps):
        c0 = FIRST["ffn", g0]
        per = 12 if steps == 4 else 0
        for j in range(2 * steps):
            to_features(k, pe, At(c0 + j, per, i), h, KT, 256, 2, SEQ, SEQ,
                        before_kt=None if j else lambda kt: pe.wait_ge(k.s("h", "ffn"), kt + 1))
        n = i * 4 + steps if per else 4 * g0 + steps
        pe.wait_ge(k.s("hidden2"), n - 1)
        for j in range(4):
            to_tokens(k, pe, At(c0 + 2 * steps + j, per, i), g, 2 * steps, 2, SEQ,
                      late=(2 * steps - 2, lambda: pe.wait_ge(k.s("hidden2"), n)) if j == 0 else None)

    with run_loop(pe, 2) as i:
        group(i, 0, 4)
    group(0, 2, 3)


def tensor_program(k, pe):
    for l in range(DEPTH):
        pe_mod(k, pe, l)
        pe_mixers(k, pe, l)
        pe_mlp(k, pe, l)
    pe_second(k, pe)


def second_buffers(k):
    Yf, T = k.Y[:, :, :].rearrange("p t d -> p (t d)"), k.GA[:, 2, :]
    b = {}
    for name, at, n in (("qa", 0, 1024), ("ka", 1024, 1024), ("va", 2048, 1024), ("qb", 3072, 3072),
                        ("kb", 6144, 3072), ("vb", 9216, 3072), ("gate", 0, 3072), ("z", 4096, 2048),
                        ("zb", 6144, 2048)):
        b[name] = k.U[:, at:at + n]
    for name, at, n in (("pa", 0, 2048), ("pta", 2048, 1024), ("pb", 0, 1536), ("ptb", 1536, 1536),
                        ("swapped", 3072, 1024), ("gate_end", 3072, 1024)):
        b[name] = Yf[:, at:at + n]
    for name, at, n in (("oa_sq", 0, 256), ("oa_std", 256, 256), ("oa_f", 512, 256)):
        b[name] = T[:, at:at + n]
    for n, name in enumerate(("lam", "pos", "t0", "t1")):
        b[name] = k.GA[:, 1, n * 256:n * 256 + 256]
    for n, name in enumerate(("cos_a", "sin_a", "cos_b", "sin_b")):
        b[name] = k.GA[:, 3, n * 256:n * 256 + 256]
    b["mask_a"] = k.X[:, 2, 0:512]
    b["mask_b"] = k.X[:, 2:4, :].rearrange("p t d -> p (t d)")[:, 512:2048]
    return b


def gate_columns(b, at, n):
    return b["gate"][:, at:at + n] if at < 3072 else b["gate_end"][:, at - 3072:at - 3072 + n]


def col(k, at, n=1):
    return k.F[:, at:at + n]


def act_stats(k, act, o, name, tiles, x_ready):
    for t in range(tiles):
        x_ready(t)
        o.then(act.activation(k.Y[:, t, :], k.X[:, t, :], ACT.Square, accum_out=k.tiny[:, t:t + 1]))
    o.wait()
    act.activation(k.tiny[:, 4:4 + tiles], k.tiny[:, 0:tiles], ACT.Sqrt, bias=k.C[:, C_EPS:C_EPS + 1],
                   scale=1.0 / D).then_inc(k.s("std", name), 1)


def act_features(k, act, name, n, kt, gain, shift, hi=False):
    act.wait_ge(k.s("tp", name), kt + 1)
    if kt >= 2:
        act.wait_ge(k.s("h", name), kt - 1)
    for part in range(n // 256):
        outs = [k.hf[:, kt % 2, part * 256:part * 256 + 256]]
        if hi:
            outs.append(k.h_hi[:, kt * n + part * 256:kt * n + part * 256 + 256])
        for out in outs:
            last = act.activation(out, k.banks(4 + kt % 4, 256, part * 256), ACT.Identity,
                                  bias=shift(kt, part), scale=gain(kt, part))
    last.then_inc(k.s("hf", name), 1)


def act_norm(k, act, o, name, tiles, n, x_ready, gain, shift):
    act_stats(k, act, o, name, tiles, x_ready)
    for kt in range(KT):
        act_features(k, act, name, n, kt, gain, shift)


def act_mod(k, act, o, l):
    c0 = FIRST["mod", l]

    def x_ready(t):
        if l == 0 and t == 0:
            act.wait_ge(k.s("x_in"), 32)
            act.wait_ge(k.s("consts_in"), 16)
        if l:
            act.wait_ge(k.s("res", "mlp0"), t + 1)

    if l:
        act_residual(k, act, o, "mlp0", 4, c0 - 1)
    for j in range(24):
        feed_hi(k, act, At(c0 + j + 2))
        if j == STATS_AT[l]:
            act_stats(k, act, o, f"mix{l}", 4, x_ready)
        if j == NORM_AT[0]:
            k.wait(act, "mod_gain", l, 1)
        if j in NORM_AT:
            act_features(k, act, f"mix{l}", NT_ALL, NORM_AT.index(j),
                         lambda kt, v: k.mod_gain[:, v * 8 + kt:v * 8 + kt + 1],
                         lambda kt, v: k.mod_feat[:, kt * 2 + v:kt * 2 + v + 1], hi=True)


def act_gates(k, act, l, which, bank):
    k.wait(act, "gate_rows", l, 2 - which)
    for v in range(2 if l == 0 else 1):
        last = act.activation(k.GA[:, 2 * which + v, :], k.banks(bank + 2 * v, 1024), ACT.Copy)
    last.then_inc(k.s("gates"), 1)


def act_residual(k, act, o, name, tiles, last_chunk):
    act.wait_ge(k.act_read, ACT_READ_COUNT[last_chunk])
    act.wait_ge(k.dve_read, DVE_READ_COUNT[last_chunk])
    for t in range(tiles):
        if t >= 2:
            act.wait_ge(k.s("y_squared", name), t - 1)
        act.activation(k.hf[:, t % 2, :], k.Y[:, t, :], ACT.Square,
                       accum_out=k.tiny[:, t:t + 1]).then_inc(k.s("y_squared", name), 1)
    act.wait_ge(k.s("y_squared", name), tiles)
    act.activation(k.tiny[:, 4:4 + tiles], k.tiny[:, 0:tiles], ACT.Sqrt, bias=k.C[:, C_EPS:C_EPS + 1],
                   scale=1.0 / D).then_inc(k.s("rstd", name), 1)


def act_take(k, act, c, out, width, at, func=None, scale=1.0):
    act.wait_ge(k.chunk_mm, c.value(lambda n: n + 1))
    return act.activation(out, k.banks(2 * c.pair, width, at), func or ACT.Copy, scale=scale)


def act_mixers(k, act, o, l):
    b = mixer_buffers(k)
    nq = NT_ALL if l == 0 else SEQ
    c0 = FIRST["win", l]
    eps = k.C[:, C_EPS:C_EPS + 1]
    for j, kind in enumerate(WIN):
        c = At(c0 + j)
        feed_hi(k, act, c + 2)
        n = NT_ALL if kind in WIN_ALL_TOKENS else nq
        last = None
        if kind in ("cf_a", "sc_x", "sc_b"):
            last = act_take(k, act, c, b[kind][:, 0:n], n, 0)
        elif kind == "cf_g":
            act.wait_ge(k.chunk_mm, c.first + 1)
            last = act.activation(b["cf_g"][:, 0:2 * n].rearrange("p (t n) -> p t n", t=2), k.two(c, n), ACT.Sigmoid)
        elif kind == "kv":
            last = act_take(k, act, c, b["kr"], 512, 512)
        elif kind == "q":
            last = act_take(k, act, c, b["cq"][:, 0:n], n, 0)
        elif kind == "nk":
            last = act_take(k, act, c, b["na_k"][:, 0:n], n, 0)
        elif kind == "nq":
            last = act_take(k, act, c, b["na_q"][:, 0:n], n, 0, scale=NA_SCALE)
        elif kind == "nv":
            last = act_take(k, act, c, b["na_v"][:, 0:512], 512, 0)
        if last is not None:
            last.then_inc(k.act_read, 1)
        if j == 0:
            act_gates(k, act, l, 1, 4)
        if kind == "q":
            act.wait_ge(k.dve_read, DVE_READ_COUNT[c0 + 2])
            act.activation(b["ckv_sq"], b["ckv"], ACT.Square).then_inc(k.s("latent_sq"), 1)
        if kind == "nk":
            act.wait_ge(k.act_read, ACT_READ_COUNT[c0 + 3])
            act.wait_ge(k.dve_read, DVE_READ_COUNT[c0 + 3])
            act.activation(b["sq"][:, 0:2 * nq], b["cq"][:, 0:2 * nq], ACT.Square).then_inc(k.s("latent_sq"), 1)

    hk = k.h_hi[:, :].rearrange("p (k n) -> p k n", k=KT)
    k.wait(act, "latent_ssq", l, 1)
    act.activation(b["std"][:, 0:512], k.banks(4, 512), ACT.Sqrt, bias=eps, scale=1.0 / 128)
    act.activation(b["std"][:, 512:512 + nq], k.banks(5, nq), ACT.Sqrt, bias=eps,
                   scale=1.0 / 256).then_inc(k.s("latent_std"), 1)
    k.wait(act, "sc_done", l, 1)
    act.activation(hk[:, 0:2, 0:nq], b["sc_x"][:, 0:2 * nq].rearrange("p (k n) -> p k n", k=2),
                   ACT.Copy).then_inc(k.s("sc_y"), 1)
    k.wait(act, "cf_cent", l, 1)
    act.activation(b["sq"][:, 0:2 * nq], b["cf_acc"][:, 0:2 * nq], ACT.Square).then_inc(k.s("cf_sq"), 1)
    act_gates(k, act, l, 0, 0)
    k.wait(act, "cf_var", l, 1)
    k.wait(act, "latent", l, 1)
    act.activation(b["std"][:, 0:nq], k.banks(7, nq), ACT.Sqrt, bias=eps, scale=1.0 / 256).then_inc(k.s("cf_std"), 1)
    k.wait(act, "cf_norm", l, 1)
    for j in range(2):
        last = act.activation(b["cf_acc"][:, j * nq:j * nq + nq], b["cf_acc"][:, j * nq:j * nq + nq], ACT.Silu,
                              bias=col(k, FC["ln_b", l] + j))
    last.then_inc(k.s("cf_act"), 1)
    k.wait(act, "mla_mm", l, 2)
    act.activation(b["kn"], k.banks(6, 1024), ACT.Copy).then_inc(k.s("mla_kv"), 1)
    k.wait(act, "mla_mm", l, 3)
    for j in range(2):
        last = act.activation(b["qn"][:, j * nq:j * nq + nq], k.banks(j, nq), ACT.Copy, scale=MLA_SCALE)
    last.then_inc(k.s("mla_q"), 1)
    k.wait(act, "cf_mm", l, 1)
    act.activation(hk[:, 4:6, 0:nq], k.banks(6, 2 * nq).rearrange("p (k n) -> p k n", k=2),
                   ACT.Copy).then_inc(k.s("cf_y"), 1)

    items = attention_items(l)

    def exps(i):
        nk = items[i][3]
        k.wait(act, "nmax", l, i + 1)
        if i >= 2:
            k.wait(act, "pt_mm", l, i - 1)
        for qt in range(2):
            at = (i % 2) * 1024 + qt * nk
            last = act.activation(b["p"][:, at:at + nk], k.banks(2 * (i % 2) + qt, nk), ACT.Exp,
                                  bias=k.tiny[:, 16 + 2 * (i % 2) + qt:17 + 2 * (i % 2) + qt],
                                  accum_out=k.tiny[:, 20 + 2 * (i % 2) + qt:21 + 2 * (i % 2) + qt])
        last.then_inc(k.s("exp"), 1)

    exps(0)
    for i, (kind, hd, q0, nk, kt0) in enumerate(items):
        if i + 1 < len(items):
            exps(i + 1)
        k.wait(act, "pt_mm", l, i + 1)
        if i >= 2:
            k.wait(act, "o_mm", l, i - 1)
        act.activation(b["pt"][:, (i % 2) * 1024:(i % 2) * 1024 + nk], k.banks(4, nk),
                       ACT.Copy).then_inc(k.s("pt_act"), 1)
        k.wait(act, "o_mm", l, i + 1)
        rows, at = slice(64 * (hd % 2), 64 * (hd % 2) + 64), (kt0 + hd // 2) * NT_ALL + q0
        act.activation(k.h_hi[rows, at:at + 256], k.banks(6 + i % 2, 256, 0, rows),
                       ACT.Copy).then_inc(k.s("o_hi"), 1)

    half = 512 if l == 0 else 256
    for j in range(4):
        c = At(FIRST["out", l] + j)
        feed_hi(k, act, c + 2)
        out = k.Y[:, 0:half // 256, j * 256:j * 256 + 256]
        act.wait_ge(k.chunk_mm, c.first + 1)
        act.activation(out, k.banks(2 * c.pair, half).rearrange("p (t n) -> p t n", n=256),
                       ACT.Copy).then_inc(k.act_read, 1)


def act_mlp(k, act, o, l):
    tiles = 4 if l == 0 else 2
    n = tiles * 128
    act_residual(k, act, o, f"mix{l}", tiles, FIRST["out", l] + 3)
    act_norm(k, act, o, f"mlp{l}", tiles, n, lambda t: act.wait_ge(k.s("res", f"mix{l}"), t + 1),
             lambda kt, v: k.mod_gain[:, 16 + v * 8 + kt:17 + v * 8 + kt],
             lambda kt, v: k.mod_feat[:, 32 + kt * 2 + v:33 + kt * 2 + v])
    if l == DEPTH - 1:
        act.wait_ge(k.s("angles"), 1)
        act.activation(k.GA[:, 3, :], k.GA[:, 3, :], ACT.Sin).then_inc(k.s("tables"), 1)
        act.wait_ge(k.s("lam_sums"), 1)
        act.activation(k.tiny[:, 66:68], k.tiny[:, 64:66], ACT.Exp).then_inc(k.s("lam_exp"), 1)
    c0 = FIRST["mlp", l]
    with run_loop(act, GROUPS1) as i:
        for j in range(8):
            c = At(c0 + j, 8, i)
            feed_hi(k, act, c + 2)
            if j >= 4:
                continue
            act.wait_ge(k.chunk_mm, c.value(lambda m: m + 1))
            if j >= 2:
                k.wait(act, "hidden", l, i * 4 + (j - 1))
            act.activation(k.R[:, j % 2, 0:2 * n].rearrange("p (t n) -> p t n", t=2), k.two(c, n),
                           ACT.Relu).then_inc(k.act_read, 1)
            act.wait_ge(k.act_read, c.value(lambda m: ACT_READ_COUNT[m]))
            act.activation(k.R[:, j % 2, 0:2 * n], k.R[:, j % 2, 0:2 * n],
                           ACT.Square).then_inc(k.s("squared"), 1)
    if l == DEPTH - 1:
        act_residual(k, act, o, f"mlp{l}", tiles, c0 + 31)


def act_second(k, act, o):
    b = second_buffers(k)
    eps = k.C[:, C_EPS:C_EPS + 1]
    act_norm(k, act, o, "mix2", 2, SEQ, lambda t: act.wait_ge(k.s("res", "mlp1"), t + 1),
             lambda kt, v: col(k, FC["pre_mix2"] + kt), lambda kt, v: k.C[:, C_ZERO:C_ZERO + 1])
    c0 = FIRST["proj2"]

    def step_a(hd, step):
        if step == "scores":
            act.wait_ge(k.s("nmax_a"), hd + 1)
            if hd >= 2:
                act.wait_ge(k.s("pt_a_mm"), hd - 1)
            for m in range(4):
                at = (hd % 2) * 1024 + m * 256
                last = act.activation(b["pa"][:, at:at + 256], k.banks(4, 256, m * 256), ACT.Exp,
                                      bias=k.tiny[:, 40 + 4 * (hd % 2) + m:41 + 4 * (hd % 2) + m], scale=0.125,
                                      accum_out=k.tiny[:, 48 + 4 * (hd % 2) + m:49 + 4 * (hd % 2) + m])
            last.then_inc(k.s("exp_a"), 1)
        elif step == "transposes":
            act.wait_ge(k.s("pt_a_mm"), hd + 1)
            if hd >= 2:
                act.wait_ge(k.s("oa_mm"), hd - 1)
            act.activation(b["pta"][:, (hd % 2) * 512:(hd % 2) * 512 + 512], k.banks(6, 512),
                           ACT.Copy).then_inc(k.s("pt_a"), 1)
        elif step == "values":
            act.wait_ge(k.s("oa_mm"), hd + 1)
            if hd:
                act.wait_ge(k.s("oa"), hd)
            act.activation(b["oa_sq"], k.banks(7, 256), ACT.Square).then_inc(k.s("oa_sq"), 1)
        else:
            act.wait_ge(k.s("oa_ssq"), hd + 1)
            act.activation(b["oa_std"], k.banks(7, 256, 256), ACT.Sqrt, bias=eps,
                           scale=1.0 / 128).then_inc(k.s("oa_std"), 1)

    act.wait_ge(k.s("lam_exp"), 1)
    for j in range(24):
        c = At(c0 + j)
        feed_hi(k, act, c + 2)
        kind = KINDS[c.first]
        if kind in ("va", "vb"):
            at = (j - 4) * 256 if kind == "va" else (j - 18) * 256
            act_take(k, act, c, b[kind][:, at:at + 256], 256, 0).then_inc(k.act_read, 1)
        for hd, step in head_steps(j):
            step_a(hd, step)

    def exps_b(hd):
        act.wait_ge(k.s("nmax_b"), hd + 1)
        if hd:
            act.wait_ge(k.s("pt_b_mm"), hd)
        for qt in range(2):
            last = act.activation(b["pb"][:, qt * 768:qt * 768 + 768], k.banks(4, 768, qt * 768), ACT.Exp,
                                  bias=k.tiny[:, 74 + qt:75 + qt], scale=128 ** -0.5,
                                  accum_out=k.tiny[:, 76 + qt:77 + qt])
        last.then_inc(k.s("exp_b"), 1)

    def gate(j):
        c = At(FIRST["gates2"] + j)
        feed_hi(k, act, c + 2)
        act.wait_ge(k.chunk_mm, c.first + 1)
        act.activation(gate_columns(b, j * 512, 512).rearrange("p (t n) -> p t n", t=2), k.two(c, 256),
                       ACT.Sigmoid).then_inc(k.act_read, 1)

    exps_b(0)
    for hd in range(HEADS):
        gate(2 * hd)
        act.wait_ge(k.s("pt_b_mm"), hd + 1)
        if hd:
            act.wait_ge(k.s("ob_mm"), hd)
        act.activation(b["ptb"][:, 0:1024], k.banks(4, 1024), ACT.Copy).then_inc(k.s("pt_b_act"), 1)
        gate(2 * hd + 1)
        act.wait_ge(k.s("ob_mm"), hd + 1)
        at = 3072 + hd * 256
        act.activation(k.h_hi[:, at:at + 256], k.banks(7, 256), ACT.Copy).then_inc(k.s("ob_hi"), 1)
        if hd + 1 < HEADS:
            exps_b(hd + 1)

    for j in range(4):
        feed_hi(k, act, At(FIRST["mix2"] + j + 2))
        if j >= 2:
            act.wait_ge(k.s("z_f"), j - 1)
            at = slice((j - 2) * 1024, (j - 1) * 1024)
            act.activation(k.h_hi[:, at], b["z"][:, at], ACT.Copy).then_inc(k.s("z_hi"), 1)
    for j in range(4):
        c = At(FIRST["mix2"] + 4 + j)
        feed_hi(k, act, c + 2)
        act_take(k, act, c, k.Y[:, 0, j * 256:j * 256 + 256], 256, 0).then_inc(k.act_read, 1)
    act_residual(k, act, o, "mix2", 2, FIRST["mix2"] + 7)
    act_norm(k, act, o, "ffn", 2, SEQ, lambda t: act.wait_ge(k.s("res", "mix2"), t + 1),
             lambda kt, v: col(k, FC["pre_ffn2"] + kt), lambda kt, v: k.C[:, C_ZERO:C_ZERO + 1])

    def group(i, g0, steps):
        per = 12 if steps == 4 else 0
        for st in range(steps):
            for kind in range(2):
                c = At(FIRST["ffn", g0] + 2 * st + kind, per, i)
                feed_hi(k, act, c + 2)
                act.wait_ge(k.chunk_mm, c.value(lambda m: m + 1))
                if st >= 2 and kind == 0:
                    act.wait_ge(k.s("hidden2"), i * 4 + (st - 1) if per else 4 * g0 + st - 1)
                for t in range(2):
                    tile = kind * 22 + (g0 * 4 + st) * 2 + t
                    w = FC["conv_w2"] + 2 * 44 + tile
                    bb = FC["conv_b2"] + tile
                    if per:
                        w, bb = i * 8 + w, i * 8 + bb
                    last = act.activation(k.R[:, st % 2, kind * 512 + t * 256:kind * 512 + t * 256 + 256],
                                          k.banks(2 * c.pair, 256, t * 512), ACT.Identity,
                                          bias=k.F[:, bass.ds(bb, 1)], scale=k.F[:, bass.ds(w, 1)])
                last.then_inc(k.act_read, 1)
            act.wait_ge(k.dve_read, At(FIRST["ffn", g0] + 2 * st, per, i).value(lambda m: DVE_READ_COUNT[m]))
            act.activation(k.R[:, st % 2, 0:512], k.R[:, st % 2, 0:512],
                           ACT.Gelu_apprx_tanh).then_inc(k.s("gelu"), 1)
        for j in range(4):
            feed_hi(k, act, At(FIRST["ffn", g0] + 2 * steps + j + 2, per, i))

    with run_loop(act, 2) as i:
        group(i, 0, 4)
    group(0, 2, 3)
    act_residual(k, act, o, "ffn", 2, N_CHUNKS - 1)


def scalar_program(k, act):
    o = Order(act, k.act_order)
    act.wait_ge(k.s("feats_in"), 16)
    o.link(act.activation(k.tiny[:, 96:112], k.F[:, 0:16], ACT.Silu))
    act.activation(k.cs_hi[:, :], k.tiny[:, 96:112], ACT.Copy).then_inc(k.s("cond_hi"), 1)
    feed_hi(k, act, At(0))
    feed_hi(k, act, At(1))
    for l in range(DEPTH):
        act_mod(k, act, o, l)
        act_mixers(k, act, o, l)
        act_mlp(k, act, o, l)
    act_second(k, act, o)


def dve_tokens(k, dve, o, name, tiles):
    dve.wait_ge(k.s("std", name), 1)
    o.link(dve.reciprocal(k.tiny[:, 8:8 + tiles], k.tiny[:, 4:4 + tiles]))
    for t in range(tiles):
        dve.tensor_scalar(k.Y[:, t, :], k.X[:, t, :], k.tiny[:, 8 + t:9 + t], None,
                          ALU.mult).then_inc(k.s("xn", name), 1)


def dve_features(k, dve, o, name, n, stride, kt, hi_there=False):
    dve.wait_ge(k.s("hf", name), kt + 1)
    hi, lo = k.h_hi[:, kt * stride:kt * stride + n], k.h_lo[:, kt * stride:kt * stride + n]
    if not hi_there:
        o.link(dve.tensor_copy(hi, k.hf[:, kt % 2, 0:n]))
    dve.tensor_tensor(lo, k.hf[:, kt % 2, 0:n], hi.bitcast(f32), ALU.subtract).then_inc(k.s("h", name), 1)


def dve_norm(k, dve, o, name, tiles, n, stride):
    dve_tokens(k, dve, o, name, tiles)
    for kt in range(KT):
        dve_features(k, dve, o, name, n, stride, kt)


def dve_residual(k, dve, o, name, tiles, ga):
    for t in range(tiles):
        dve.wait_ge(k.s("y_squared", name), t + 1)
        o.then(dve.tensor_tensor(k.Y[:, t, :], k.Y[:, t, :], k.GA[:, ga(t), :], ALU.mult))
    dve.wait_ge(k.s("rstd", name), 1)
    o.link(dve.reciprocal(k.tiny[:, 8:8 + tiles], k.tiny[:, 4:4 + tiles]))
    for t in range(tiles):
        dve.scalar_tensor_tensor(k.X[:, t, :], k.Y[:, t, :], k.tiny[:, 8 + t:9 + t], k.X[:, t, :],
                                 ALU.mult, ALU.add).then_inc(k.s("res", name), 1)


def dve_take(k, dve, c, out, width, at, scale=None):
    dve.wait_ge(k.chunk_mm, c.value(lambda n: n + 1))
    if scale is None:
        return dve.tensor_copy(out, k.banks(2 * c.pair, width, at))
    return dve.tensor_scalar(out, k.banks(2 * c.pair, width, at), scale, None, ALU.mult)


def dve_mod(k, dve, o, l):
    c0 = FIRST["mod", l]
    k.wait(dve, "b_mod_in", l, 16)

    def sections(which):
        k.wait(dve, "mod_t", l, which + 1)
        dve.tensor_copy(k.mod_feat[:, 32 * which:32 * which + 32], k.banks(1 + 2 * which, 32)).then_inc(k.s("mod_feat"), 1)
        k.wait(dve, "mod_feat", l, which + 1)
        mf = k.mod_feat[:, 32 * which:32 * which + 32].rearrange("p (s k v) -> p s v k", s=2, v=2)
        for v in range(2):
            at = (2 * which + v) * 8
            last = dve.scalar_tensor_tensor(k.mod_gain[:, at:at + 8], mf[:, 1, v, :], 1.0,
                                            col(k, FC[("g_pre_mix", "g_pre_mlp")[which], l], 8), ALU.add, ALU.mult)
        last.then_inc(k.s("mod_gain"), 1)

    for j in range(24):
        c = At(c0 + j)
        dve.wait_ge(k.chunk_mm, c.first + 1)
        row = k.U[0:2, j * 256:j * 256 + 256]
        dve.tensor_tensor(row, k.banks(2 * c.pair, 256, 0, slice(0, 2)), row, ALU.add).then_inc(k.dve_read, 1)
        feed_lo(k, dve, c + 2)
        if l and j == 1:
            dve_residual(k, dve, o, "mlp0", 4, lambda t: 2 + t // 2)
        if j == STATS_AT[l]:
            dve_tokens(k, dve, o, f"mix{l}", 4)
        if j in SECTIONS_AT:
            sections(SECTIONS_AT.index(j))
        if j in NORM_AT:
            dve_features(k, dve, o, f"mix{l}", NT_ALL, NT_ALL, NORM_AT.index(j), hi_there=True)
        if j in (11, 23):
            k.wait(dve, "gpost_in", l, 32)
            dve.wait_ge(k.dve_read, DVE_READ_COUNT[c.first])
            gain, sec = k.GA[0:2, 0 if j == 11 else 2, :], j // 4
            dve.tensor_tensor(gain, gain, k.U[0:2, sec * D:sec * D + D], ALU.mult).then_inc(k.s("gate_in"), 1)


def dve_mixers(k, dve, o, l):
    b = mixer_buffers(k)
    nq = NT_ALL if l == 0 else SEQ
    seg = nq // 256
    c0 = FIRST["win", l]
    cf_in = b["cf_in"].rearrange("p (k s n) -> p k s n", k=2, s=2)
    sc_in = b["sc_in"].rearrange("p (k s n) -> p k s n", k=2, s=2)
    acc = b["cf_acc"][:, 0:2 * nq].rearrange("p (k s n) -> p k s n", k=2, s=seg)
    scx = b["sc_x"][:, 0:2 * nq].rearrange("p (k s n) -> p k s n", k=2, s=seg)
    k.wait(dve, "gate_in", l, 2)
    o.then(dve.memset(b["cf_in"], 0.0))
    o.link(dve.memset(b["sc_in"], 0.0))

    done = {}
    taps = [(tap, kt) for tap in range(CF_K) for kt in range(2)]

    def conv_taps(n):
        for tap, kt in taps[:n]:
            src, w = cf_in[:, kt, 0:seg, tap:tap + 256], col(k, FC["cf_w", l] + kt * CF_K + tap)
            if tap == 0:
                ins = dve.tensor_scalar(acc[:, kt], src, w, col(k, FC["cf_b", l] + kt), ALU.mult, ALU.add)
            else:
                o.wait(done[kt])
                ins = dve.scalar_tensor_tensor(acc[:, kt], src, w, acc[:, kt], ALU.mult, ALU.add)
            if (tap, kt) == (CF_K - 1, 1):
                ins.then_inc(k.s("cf_conv"), 1)
            else:
                done[kt] = o.then(ins)
        del taps[:n]

    for j, kind in enumerate(WIN):
        c = At(c0 + j)
        feed_lo(k, dve, c + 2)
        n = NT_ALL if kind in WIN_ALL_TOKENS else nq
        if kind in ("cf_a", "sc_x", "sc_b"):
            dve_take(k, dve, c, b[kind][:, n:2 * n], n, 512).then_inc(k.dve_read, 1)
        elif kind == "cf_g":
            dve.wait_ge(k.act_read, ACT_READ_COUNT[c.first])
            dve.wait_ge(k.dve_read, DVE_READ_COUNT[c.first - 1])
            o.link(dve.tensor_tensor(cf_in[:, :, 0:seg, 15:271],
                                     b["cf_a"][:, 0:2 * n].rearrange("p (k s n) -> p k s n", k=2, s=seg),
                                     b["cf_g"][:, 0:2 * n].rearrange("p (k s n) -> p k s n", k=2, s=seg), ALU.mult))
        elif kind == "kv":
            dve_take(k, dve, c, b["ckv"], 512, 0).then_inc(k.dve_read, 1)
        elif kind == "q":
            dve_take(k, dve, c, b["cq"][:, n:2 * n], n, 512).then_inc(k.dve_read, 1)
        elif kind == "nk":
            dve_take(k, dve, c, b["na_k"][:, n:2 * n], n, 512).then_inc(k.dve_read, 1)
        elif kind == "nq":
            dve_take(k, dve, c, b["na_q"][:, n:2 * n], n, 512, NA_SCALE).then_inc(k.dve_read, 1)
        elif kind == "nv":
            dve_take(k, dve, c, b["na_v"][:, 512:1024], 512, 512).then_inc(k.dve_read, 1)
        elif kind == "sc_c":
            dve.wait_ge(k.chunk_mm, c.first + 1)
            dve.wait_ge(k.act_read, ACT_READ_COUNT[c.first])
            dve.wait_ge(k.dve_read, DVE_READ_COUNT[c.first - 1])
            dve.tensor_tensor(sc_in[:, :, 0:seg, 1:257],
                              k.two(c, n).rearrange("p k (s n) -> p k s n", s=seg), scx,
                              ALU.mult).then_inc(k.dve_read, 1)
        if j >= 2:
            conv_taps(8)
    dve.wait_ge(k.dve_read, DVE_READ_COUNT[c0 + 9])
    dve.wait_ge(k.act_read, ACT_READ_COUNT[c0 + 9])
    for kt in range(2):
        w = FC["w_sc", l] + kt * 3
        done[kt] = o.then(dve.tensor_scalar(scx[:, kt], sc_in[:, kt, 0:seg, 0:256], col(k, w), None, ALU.mult))
    for tap in (1, 2):
        for kt in range(2):
            o.wait(done[kt])
            done[kt] = o.then(dve.scalar_tensor_tensor(scx[:, kt], sc_in[:, kt, 0:seg, tap:tap + 256],
                                                       col(k, FC["w_sc", l] + kt * 3 + tap), scx[:, kt],
                                                       ALU.mult, ALU.add))
    o.wait()
    sc = b["sc_x"][:, 0:2 * nq]
    dve.tensor_tensor(sc, sc, b["sc_b"][:, 0:2 * nq], ALU.mult).then_inc(k.s("sc_done"), 1)

    k.wait(dve, "cf_mean", l, 1)
    cf = [b["cf_acc"][:, kt * nq:kt * nq + nq] for kt in range(2)]
    for kt in range(2):
        last = dve.scalar_tensor_tensor(cf[kt], k.banks(6, nq), -1.0 / 256, cf[kt], ALU.mult, ALU.add)
    last.then_inc(k.s("cf_cent"), 1)
    k.wait(dve, "latent_std", l, 1)
    o.link(dve.reciprocal(b["std"][:, 0:512 + nq], b["std"][:, 0:512 + nq]))
    dve.scalar_tensor_tensor(b["ckv"], b["ckv"], col(k, FC["g_kv", l]), b["std"][:, 0:512], ALU.mult, ALU.mult)
    for kt in range(2):
        cq = b["cq"][:, kt * nq:kt * nq + nq]
        last = dve.scalar_tensor_tensor(cq, cq, col(k, FC["g_q", l] + kt), b["std"][:, 512:512 + nq],
                                        ALU.mult, ALU.mult)
    last.then_inc(k.s("latent"), 1)
    hk, lk = (h[:, :].rearrange("p (k n) -> p k n", k=KT) for h in (k.h_hi, k.h_lo))
    k.wait(dve, "sc_y", l, 1)
    dve.tensor_tensor(lk[:, 0:2, 0:nq], sc.rearrange("p (k n) -> p k n", k=2), hk[:, 0:2, 0:nq].bitcast(f32),
                      ALU.subtract).then_inc(k.s("sc_y"), 1)
    k.wait(dve, "cf_std", l, 1)
    o.link(dve.reciprocal(b["std"][:, 0:nq], b["std"][:, 0:nq]))
    for kt in range(2):
        last = dve.scalar_tensor_tensor(cf[kt], cf[kt], col(k, FC["ln_g", l] + kt), b["std"][:, 0:nq],
                                        ALU.mult, ALU.mult)
    last.then_inc(k.s("cf_norm"), 1)
    k.wait(dve, "mla_mm", l, 1)
    k.wait(dve, "bias", l, 1)
    dve.tensor_scalar(b["qr"][:, 0:nq], k.banks(4, nq), MLA_SCALE, None, ALU.mult).then_inc(k.s("qr"), 1)
    cos, sin = k.C[:, C_COS:C_COS + 256], k.C[:, C_SIN:C_SIN + 256]

    def rotate(x, swapped):
        o.then(dve.tensor_tensor(b["rope"], swapped, sin, ALU.mult))
        o.link(dve.tensor_tensor(x, x, cos, ALU.mult))
        ins = dve.tensor_tensor(x, x, b["rope"], ALU.add)
        ins.then_inc(k.s("mla_in"), 1)

    rotate(b["kr"][:, 0:256], k.banks(5, 256))
    k.wait(dve, "mla_mm", l, 3)
    o.then(dve.tensor_copy(b["v"], k.banks(2, 1024)))
    k.wait(dve, "swap", l, 1)
    k.wait(dve, "mla_in", l, 1)
    k.wait(dve, "qr", l, 1)
    rotate(b["qr"][:, 0:256], k.banks(5, 256, 256))
    k.wait(dve, "cf_y", l, 1)
    dve.tensor_tensor(lk[:, 4:6, 0:nq], k.banks(6, 2 * nq).rearrange("p (k n) -> p k n", k=2),
                      hk[:, 4:6, 0:nq].bitcast(f32), ALU.subtract).then_inc(k.s("cf_y"), 1)

    items = attention_items(l)

    def maxima(i):
        kind, hd, q0, nk, _ = items[i]
        k.wait(dve, "scores", l, i + 1)
        sc2 = k.ps[:, 2 * (i % 2):2 * (i % 2) + 2, :]
        if kind == "na" and q0 == 0:
            bias = b["bias"][:, hd * 512:hd * 512 + 512].rearrange("p (q n) -> p q n", q=2)
            o.link(dve.tensor_tensor(sc2[:, :, 0:256], sc2[:, :, 0:256], bias, ALU.add))
        dve.tensor_reduce(k.tiny[:, 16 + 2 * (i % 2):18 + 2 * (i % 2)], sc2[:, :, 0:nk], AX.X, ALU.max,
                          negate=True).then_inc(k.s("nmax"), 1)

    maxima(0)
    for i, (kind, hd, q0, nk, kt0) in enumerate(items):
        k.wait(dve, "exp", l, i + 1)
        rc = k.tiny[:, 24 + 2 * (i % 2):26 + 2 * (i % 2)]
        o.link(dve.reciprocal(rc, k.tiny[:, 20 + 2 * (i % 2):22 + 2 * (i % 2)]))
        for qt in range(2):
            at = (i % 2) * 1024 + qt * nk
            last = dve.tensor_scalar(b["p"][:, at:at + nk], b["p"][:, at:at + nk], rc[:, qt:qt + 1], None, ALU.mult)
        last.then_inc(k.s("p"), 1)
        if i + 1 < len(items):
            maxima(i + 1)
        k.wait(dve, "pt_mm", l, i + 1)
        if i >= 2:
            k.wait(dve, "o_mm", l, i - 1)
        at = (i % 2) * 1024 + nk
        dve.tensor_copy(b["pt"][:, at:at + nk], k.banks(5, nk)).then_inc(k.s("pt_dve"), 1)
        k.wait(dve, "o_hi", l, i + 1)
        rows, at = slice(64 * (hd % 2), 64 * (hd % 2) + 64), (kt0 + hd // 2) * NT_ALL + q0
        dve.tensor_tensor(k.h_lo[rows, at:at + 256], k.banks(6 + i % 2, 256, 0, rows),
                          k.h_hi[rows, at:at + 256].bitcast(f32), ALU.subtract).then_inc(k.s("o_lo"), 1)

    half = 512 if l == 0 else 256
    for j in range(4):
        c = At(FIRST["out", l] + j)
        feed_lo(k, dve, c + 2)
        dve.wait_ge(k.chunk_mm, c.first + 1)
        t0 = half // 256
        dve.tensor_copy(k.Y[:, t0:2 * t0, j * 256:j * 256 + 256],
                        k.banks(2 * c.pair, half, 512).rearrange("p (t n) -> p t n", n=256)).then_inc(k.dve_read, 1)


def dve_down(k, dve, c, tiles, j):
    feed_lo(k, dve, c + 2)
    dve.wait_ge(k.chunk_mm, c.value(lambda n: n + 1))
    dve.wait_ge(k.dve_read, c.value(lambda n: DVE_READ_COUNT[n - 1]))
    y = k.Y[:, 0:tiles, j * 256:j * 256 + 256]
    products = k.two(c, 256) if tiles == 2 else k.banks(2 * c.pair, 1024).rearrange("p (t n) -> p t n", n=256)
    dve.tensor_tensor(y, products, y,
                      ALU.add).then_inc(k.dve_read, 1)


def dve_mlp(k, dve, o, l):
    tiles = 4 if l == 0 else 2
    n = tiles * 128
    dve_residual(k, dve, o, f"mix{l}", tiles, lambda t: t // 2)
    dve_norm(k, dve, o, f"mlp{l}", tiles, n, NT_ALL)
    dve.wait_ge(k.s("y0", f"mlp{l}"), 1)
    if l == DEPTH - 1:
        dve.wait_ge(k.s("angles"), 1)
        dve.tensor_reduce(k.tiny[:, 64:66], second_buffers(k)["t1"][:, 0:128].rearrange("p (a n) -> p a n", a=2), AX.X,
                          ALU.add).then_inc(k.s("lam_sums"), 1)
    c0 = FIRST["mlp", l]
    with run_loop(dve, GROUPS1) as i:
        o.enter(i, 4)
        for j in range(4):
            feed_lo(k, dve, At(c0 + j + 2, 8, i))
            k.wait(dve, "squared", l, i * 4 + (j + 1))
            r, at = k.R[:, j % 2, 0:2 * n], 2 * j * n
            o.link(dve.tensor_copy(k.g_hi[:, at:at + 2 * n], r))
            dve.tensor_tensor(k.g_lo[:, at:at + 2 * n], r, k.g_hi[:, at:at + 2 * n].bitcast(f32),
                              ALU.subtract).then_inc(k.s("hidden"), 1)
        for j in range(4):
            dve_down(k, dve, At(c0 + 4 + j, 8, i), tiles, j)
    o.leave(GROUPS1)
    if l == DEPTH - 1:
        dve_residual(k, dve, o, f"mlp{l}", tiles, lambda t: 2 + t // 2)


TWO_PI = 2 * np.pi
C1 = 6.28125
C2 = float(np.float32(np.round((TWO_PI - C1) * 2 ** 20) / 2 ** 20))
C3 = float(np.float32(TWO_PI - C1 - C2))
ROUND = 1.5 * 2 ** 23
PI_IN = 3.1415925


def dve_second(k, dve, o):
    b = second_buffers(k)
    dve_norm(k, dve, o, "mix2", 2, SEQ, SEQ)
    c0 = FIRST["proj2"]
    dve.wait_ge(k.s("lam_exp"), 1)
    o.link(dve.tensor_tensor(k.tiny[:, 68:69], k.tiny[:, 67:68], k.tiny[:, 66:67], ALU.subtract))
    o.link(dve.tensor_scalar(k.tiny[:, 69:70], k.tiny[:, 68:69], -LAM_INIT, None, ALU.add))
    o.link(dve.tensor_scalar(k.tiny[:, 70:71], col(k, FC["head_g2"]), 1.0 - LAM_INIT, None, ALU.mult))
    dve.wait_ge(k.s("tables"), 1)

    def values(c, j):
        at, width = ((j - 4) * 256, 512) if KINDS[c.first] == "va" else ((j - 18) * 256, 1536)
        dve_take(k, dve, c, b[KINDS[c.first]][:, width + at:width + at + 256], 256, 512).then_inc(k.dve_read, 1)

    def rotated(c, j):
        kind = KINDS[c.first]
        turned = j if j < 4 else j - 2
        at = {"qa": j, "ka": j - 2, "qb": j - 6, "kb": j - 12}[kind] * 512
        if turned >= 2:
            dve.wait_ge(k.s("rope2"), turned - 1)
        dve.wait_ge(k.chunk_mm, c.first + 1)
        two = lambda ap: ap.rearrange("p (t n) -> p t n", t=2)
        wide = 32 if kind in ("qa", "ka") else 64
        cos, sin = (b["cos_a"], b["sin_a"]) if wide == 32 else (b["cos_b"], b["sin_b"])
        for q in range(128 // wide):
            src, dst = slice(q * wide, q * wide + wide), slice((q ^ 1) * wide, (q ^ 1) * wide + wide)
            m = b["swapped"][dst, (turned % 2) * 512:(turned % 2) * 512 + 512]
            dve.tensor_tensor(two(m), k.two(c, 256, src),
                              sin[src].unsqueeze(1).broadcast_to([wide, 2, 256]), ALU.mult)
        dve.tensor_tensor(two(b[kind][:, at:at + 512]), k.two(c, 256),
                          cos.unsqueeze(1).broadcast_to([128, 2, 256]), ALU.mult).then_inc(k.dve_read, 1)

    def chunk(j):
        c = At(c0 + j)
        feed_lo(k, dve, c + 2)
        if KINDS[c.first] in ("va", "vb"):
            values(c, j)
        else:
            rotated(c, j)
        for hd, step in head_steps(j):
            step_a(hd, step)
        if j > HEAD_A and (j - HEAD_A) % 4 == 1 and (j - HEAD_A) // 4 < HEADS:
            probs_a((j - HEAD_A) // 4)

    def maxima_a(hd):
        dve.wait_ge(k.s("scores_a"), hd + 1)
        if hd == 0:
            dve.wait_ge(k.s("masks_in"), 16)
        sc = k.banks(4, 1024).rearrange("p (c n) -> p c n", c=2)
        o.link(dve.tensor_tensor(sc, sc, b["mask_a"].unsqueeze(1).broadcast_to([128, 2, 512]), ALU.add))
        nm = k.tiny[:, 32 + 4 * (hd % 2):36 + 4 * (hd % 2)]
        o.link(dve.tensor_reduce(nm, k.banks(4, 1024).rearrange("p (m n) -> p m n", m=4), AX.X, ALU.max,
                                 negate=True))
        dve.tensor_scalar(k.tiny[:, 40 + 4 * (hd % 2):44 + 4 * (hd % 2)], nm, 0.125, None,
                          ALU.mult).then_inc(k.s("nmax_a"), 1)

    def probs_a(hd):
        dve.wait_ge(k.s("exp_a"), hd + 1)
        rc = k.tiny[:, 56 + 4 * (hd % 2):60 + 4 * (hd % 2)]
        o.link(dve.reciprocal(rc, k.tiny[:, 48 + 4 * (hd % 2):52 + 4 * (hd % 2)]))
        o.link(dve.tensor_scalar(rc[:, 2:4], rc[:, 2:4], k.tiny[:, 69:70], None, ALU.mult))
        p = b["pa"][:, (hd % 2) * 1024:(hd % 2) * 1024 + 1024]
        for qt in range(2):
            o.then(dve.tensor_scalar(p[:, qt * 256:qt * 256 + 256], p[:, qt * 256:qt * 256 + 256],
                                     rc[:, qt:qt + 1], None, ALU.mult))
        o.wait()
        for qt in range(2):
            last = dve.scalar_tensor_tensor(p[:, qt * 256:qt * 256 + 256], p[:, 512 + qt * 256:768 + qt * 256],
                                            rc[:, 2 + qt:3 + qt], p[:, qt * 256:qt * 256 + 256], ALU.mult, ALU.add)
        last.then_inc(k.s("p_a"), 1)

    def step_a(hd, step):
        if step == "scores":
            maxima_a(hd)
        elif step == "norm":
            dve.wait_ge(k.s("oa_std"), hd + 1)
            o.link(dve.reciprocal(b["oa_std"], b["oa_std"]))
            o.link(dve.scalar_tensor_tensor(b["oa_f"], k.banks(7, 256), k.tiny[:, 70:71], b["oa_std"],
                                            ALU.mult, ALU.mult))
            at = 2048 + hd * 256
            o.link(dve.tensor_copy(k.h_hi[:, at:at + 256], b["oa_f"]))
            dve.tensor_tensor(k.h_lo[:, at:at + 256], b["oa_f"], k.h_hi[:, at:at + 256].bitcast(f32),
                              ALU.subtract).then_inc(k.s("oa"), 1)

    for j in range(24):
        chunk(j)

    def maxima_b(hd):
        dve.wait_ge(k.s("scores_b"), hd + 1)
        sc = k.banks(4, 1536)
        o.link(dve.tensor_tensor(sc, sc, b["mask_b"], ALU.add))
        o.link(dve.tensor_reduce(k.tiny[:, 72:74], sc.rearrange("p (q n) -> p q n", q=2), AX.X, ALU.max, negate=True))
        dve.tensor_scalar(k.tiny[:, 74:76], k.tiny[:, 72:74], 128 ** -0.5, None, ALU.mult).then_inc(k.s("nmax_b"), 1)

    maxima_b(0)
    for hd in range(HEADS):
        dve.wait_ge(k.s("exp_b"), hd + 1)
        o.link(dve.reciprocal(k.tiny[:, 78:80], k.tiny[:, 76:78]))
        for qt in range(2):
            p = b["pb"][:, qt * 768:qt * 768 + 768]
            last = dve.tensor_scalar(p, p, k.tiny[:, 78 + qt:79 + qt], None, ALU.mult)
        last.then_inc(k.s("p_b"), 1)
        feed_lo(k, dve, At(FIRST["gates2"] + 2 * hd + 2))
        dve.wait_ge(k.s("pt_b_mm"), hd + 1)
        if hd:
            dve.wait_ge(k.s("ob_mm"), hd)
        dve.tensor_copy(b["ptb"][:, 1024:1536], k.banks(6, 512)).then_inc(k.s("pt_b_dve"), 1)
        feed_lo(k, dve, At(FIRST["gates2"] + 2 * hd + 3))
        if hd + 1 < HEADS:
            maxima_b(hd + 1)
        dve.wait_ge(k.s("ob_hi"), hd + 1)
        at = 3072 + hd * 256
        dve.tensor_tensor(k.h_lo[:, at:at + 256], k.banks(7, 256), k.h_hi[:, at:at + 256].bitcast(f32),
                          ALU.subtract).then_inc(k.s("ob"), 1)

    dve.wait_ge(k.act_read, ACT_READ_COUNT[FIRST["gates2"] + 7])
    for j in range(4):
        c = At(FIRST["mix2"] + j)
        feed_lo(k, dve, c + 2)
        dve.wait_ge(k.chunk_mm, c.first + 1)
        to = b[("z", "zb")[j // 2]][:, (j % 2) * 1024:(j % 2) * 1024 + 1024]
        dve.tensor_tensor(to, k.banks(2 * c.pair, 1024), gate_columns(b, j * 1024, 1024),
                          ALU.mult).then_inc(k.dve_read, 1)
        if j >= 2:
            dve.wait_ge(k.dve_read, DVE_READ_COUNT[c.first])
            z, at = b["z"][:, (j - 2) * 1024:(j - 1) * 1024], slice((j - 2) * 1024, (j - 1) * 1024)
            dve.tensor_tensor(z, z, b["zb"][:, at], ALU.add).then_inc(k.s("z_f"), 1)
            dve.wait_ge(k.s("z_hi"), j - 1)
            dve.tensor_tensor(k.h_lo[:, at], z, k.h_hi[:, at].bitcast(f32), ALU.subtract).then_inc(k.s("z"), 1)
    for j in range(4):
        c = At(FIRST["mix2"] + 4 + j)
        feed_lo(k, dve, c + 2)
        dve_take(k, dve, c, k.Y[:, 1, j * 256:j * 256 + 256], 256, 512).then_inc(k.dve_read, 1)
    dve.wait_ge(k.s("post_in"), 32)
    dve_residual(k, dve, o, "mix2", 2, lambda t: 1)
    dve_norm(k, dve, o, "ffn", 2, SEQ, SEQ)
    dve.wait_ge(k.s("y0", "ffn"), 1)

    def group(i, g0, steps):
        per = 12 if steps == 4 else 0
        for st in range(steps):
            for kind in range(2):
                c = At(FIRST["ffn", g0] + 2 * st + kind, per, i)
                feed_lo(k, dve, c + 2)
                dve.wait_ge(k.act_read, c.value(lambda m: ACT_READ_COUNT[m]))
                for tap in (0, 1):
                    for t in range(2):
                        tile = FC["conv_w2"] + tap * 44 + kind * 22 + (g0 * 4 + st) * 2 + t
                        if per:
                            tile = i * 8 + tile
                        r = k.R[:, st % 2, kind * 512 + t * 256 + 2 - tap:kind * 512 + t * 256 + 256]
                        if tap:
                            o.wait(first[t])
                        ins = dve.scalar_tensor_tensor(r, k.banks(2 * c.pair, 254 + tap, t * 512),
                                                       k.F[:, bass.ds(tile, 1)], r, ALU.mult, ALU.add)
                        if tap == 0:
                            first = {} if t == 0 else first
                            first[t] = o.then(ins)
                ins.then_inc(k.dve_read, 1)
            dve.wait_ge(k.s("gelu"), i * 4 + (st + 1) if per else 4 * g0 + st + 1)
            dve.wait_ge(k.dve_read, At(FIRST["ffn", g0] + 2 * st + 1, per, i).value(lambda m: DVE_READ_COUNT[m]))
            r = k.R[:, st % 2, 0:512]
            o.link(dve.tensor_tensor(r, r, k.R[:, st % 2, 512:1024], ALU.mult))
            o.link(dve.tensor_copy(k.g_hi[:, st * 512:st * 512 + 512], r))
            dve.tensor_tensor(k.g_lo[:, st * 512:st * 512 + 512], r, k.g_hi[:, st * 512:st * 512 + 512].bitcast(f32),
                              ALU.subtract).then_inc(k.s("hidden2"), 1)
        for j in range(4):
            dve_down(k, dve, At(FIRST["ffn", g0] + 2 * steps + j, per, i), 2, j)

    with run_loop(dve, 2) as i:
        o.enter(i, 4 * 6)
        group(i, 0, 4)
    o.leave(2)
    group(0, 2, 3)
    dve_residual(k, dve, o, "ffn", 2, lambda t: 0)


def vector_program(k, dve):
    o = Order(dve, k.dve_order)
    dve.wait_ge(k.s("cond_hi"), 1)
    dve.tensor_tensor(k.cs_lo[:, :], k.tiny[:, 96:112], k.cs_hi[:, :].bitcast(f32),
                      ALU.subtract).then_inc(k.s("cond"), 1)
    feed_lo(k, dve, At(0))
    feed_lo(k, dve, At(1))
    for l in range(DEPTH):
        dve_mod(k, dve, o, l)
        dve_mixers(k, dve, o, l)
        dve_mlp(k, dve, o, l)
    dve_second(k, dve, o)


def pool_tables(k, pool, o):
    b = second_buffers(k)
    pool.wait_ge(k.s("second_in"), 32)
    o.link(pool.tensor_copy(b["t0"], b["pos"].bitcast(i32)))
    for n, (cs, sn) in enumerate((("cos_a", "sin_a"), ("cos_b", "sin_b"))):
        a, turns, cs = b[sn], b["t1"], b[cs]
        o.link(pool.tensor_scalar(a, b["t0"], k.C[:, C_INV + n:C_INV + n + 1], None, ALU.mult))
        o.link(pool.tensor_scalar(turns, a, 1.0 / TWO_PI, ROUND, ALU.mult, ALU.add))
        o.link(pool.tensor_scalar(turns, turns, -ROUND, None, ALU.add))
        for part in (C1, C2, C3):
            o.link(pool.tensor_scalar(b["pos"], turns, -part, None, ALU.mult))
            o.link(pool.tensor_tensor(a, a, b["pos"], ALU.add))
        o.link(pool.tensor_scalar(cs, a, np.pi / 2, None, ALU.add))
        o.link(pool.tensor_scalar(turns, cs, PI_IN, -TWO_PI, ALU.is_gt, ALU.mult))
        o.link(pool.tensor_tensor(cs, cs, turns, ALU.add))
        o.link(pool.tensor_scalar(cs, cs, PI_IN, -PI_IN, ALU.min, ALU.max))
        o.link(pool.tensor_scalar(a, a, PI_IN, -PI_IN, ALU.min, ALU.max))
        o.link(pool.tensor_scalar(a, a, k.C[:, C_SIGN + n:C_SIGN + n + 1], None, ALU.mult))
    lam = b["lam"].rearrange("p (a b n) -> p a b n", a=2, b=2)
    pool.tensor_tensor(b["t1"][:, 0:128].rearrange("p (a n) -> p a n", a=2), lam[:, :, 0, :], lam[:, :, 1, :],
                       ALU.mult).then_inc(k.s("angles"), 1)


def pool_program(k, pool, t):
    b2 = second_buffers(k)
    o = Order(pool, k.pool_order)

    def rows(ap, parts):
        return bass.AP(ap.tensor, ap.offset, [[0, parts]] + [list(x) for x in ap.ap])

    for l in range(DEPTH):
        b = mixer_buffers(k)
        if l:
            pool.wait_ge(k.chunk_mm, FIRST["mod", l])
        pool.dma_start(k.U[0:2, 0:6144], rows(t["b_mod"][l], 2)).then_inc(k.s("b_mod_in"), 16)
        if l:
            pool.wait_ge(k.s("res", f"mlp{l - 1}"), 4)
        for which in range(2):
            pool.dma_start(k.GA[0:2, 2 * which, :], rows(t["gpost"][2 * l + which], 2)).then_inc(k.s("gpost_in"), 16)
        k.wait(pool, "mod_t", l, 2)
        if l == 0:
            for hd in range(DEPTH * HEADS):
                pool.dma_start(t["rpb_rows"][hd], rows(t["rpb"][hd], GRID)).then_inc(k.s("rpb_out"), 16)
        pool.dma_start(k.SW[:, :], t["small"][l]).then_inc(k.s("small_in"), 16)
        pool.wait_ge(k.s("rpb_out"), 16 * DEPTH * HEADS)
        if l:
            pool.dma_start(b2["lam"], rows(t["lam"], 128)).then_inc(k.s("second_in"), 16)
            pool.dma_start(b2["pos"].bitcast(i32), rows(t["pos"][0], 128)).then_inc(k.s("second_in"), 16)
        pool.wait_ge(k.s("h", f"mix{l}"), KT)
        for hd in range(HEADS):
            for r in range(4):
                at = ((l * HEADS + hd) * GRID) * RPB + (7 - r) * 31 + 15
                src = bass.AP(t["rpb_rows"].tensor, at, [[RPB - 1, GRID], [31, 4], [1, GRID]])
                dst = b["bias"][64 * (r % 2):64 * (r % 2) + 64, hd * 512 + (r // 2) * 256:hd * 512 + (r // 2) * 256 + 256]
                pool.dma_start(dst.rearrange("p (i n) -> p i n", i=4), src).then_inc(k.s("bias_in"), 16)
        pool.dma_start(b["window"], t["window"]).then_inc(k.s("bias_in"), 16)
        k.wait(pool, "bias_in", l, 17 * 16)
        bias = b["bias"].rearrange("p (m n) -> p m n", m=8)
        pool.tensor_tensor(bias, bias, b["window"].unsqueeze(1).broadcast_to([128, 8, 256]),
                           ALU.add).then_inc(k.s("bias"), 1)
        if l:
            pool.dma_start(k.X[:, 2:4, :].rearrange("p t d -> p (t d)"), t["masks2"]).then_inc(k.s("masks_in"), 16)
            pool_tables(k, pool, o)
        pool.wait_ge(k.s("tp", f"mlp{l}"), KT)
        pool.memset(k.Y[:, :, :], 0.0).then_inc(k.s("y0", f"mlp{l}"), 1)
    pool.wait_ge(k.s("lam_sums"), 1)
    pool.dma_start(k.GA[:, 1, :], rows(t["gpost"][4], 128)).then_inc(k.s("post_in"), 16)
    pool.dma_start(k.GA[:, 0, :], rows(t["gpost"][5], 128)).then_inc(k.s("post_in"), 16)
    turned = 0
    for j in range(24):
        n = FIRST["proj2"] + j
        kind = KINDS[n]
        if kind in ("va", "vb"):
            continue
        at = {"qa": j, "ka": j - 2, "qb": j - 6, "kb": j - 12}[kind] * 512
        pool.wait_ge(k.dve_read, DVE_READ_COUNT[n])
        to = b2[kind][:, at:at + 512]
        pool.tensor_tensor(to, to, b2["swapped"][:, (turned % 2) * 512:(turned % 2) * 512 + 512],
                           ALU.add).then_inc(k.s("rope2"), 1)
        turned += 1
    pool.wait_ge(k.s("tp", "ffn"), KT)
    pool.memset(k.Y[:, 0:2, :], 0.0).then_inc(k.s("y0", "ffn"), 1)


def build(nc, t):
    with ExitStack() as stack:
        k = Core(nc, stack)
        block = stack.enter_context(nc.Block())

        @block.sync
        def _(sp):
            sync_program(k, sp, t)

        @block.gpsimd
        def _(pool):
            pool_program(k, pool, t)

        @block.tensor
        def _(pe):
            tensor_program(k, pe)

        @block.scalar
        def _(act):
            scalar_program(k, act)

        @block.vector
        def _(dve):
            vector_program(k, dve)


def chunked(w, rows, cols):
    kt, n = rows // 128, w.shape[1] // cols
    return w.reshape(kt, 128, n, cols).transpose(2, 1, 0, 3).reshape(n, 128, kt * cols)


def padded(chunks):
    out = np.zeros((chunks.shape[0], 128, CHUNK), np.float32)
    out[:, :, :chunks.shape[2]] = chunks
    return out


def weight_stream(a):
    parts = []
    for l in range(DEPTH):
        parts.append(chunked(a["w_mod"][l], D, 256))
        w = a["w_in"][l]
        kv = np.concatenate([w[:, 1024:1152]] + [w[:, 1152:1184]] * 4, axis=1)
        cols = {"sc_x": w[:, 0:256], "sc_b": w[:, 256:512], "sc_c": w[:, 512:768], "q": w[:, 768:1024], "kv": kv,
                "cf_a": w[:, 1184:1440], "cf_g": w[:, 1440:1696], "nq": w[:, 1696:1952], "nk": w[:, 1952:2208],
                "nv": w[:, 2208:2464]}
        parts.append(chunked(np.concatenate([cols[n] for n in WIN], axis=1), D, 256))
        parts.append(chunked(a["w_out"][l], D, 256))
        up = chunked(a["w_mlp1"][l], D, 256)
        for g in range(GROUPS1):
            parts += [up[4 * g:4 * g + 4], chunked(a["w_mlp2"][l][g * D:g * D + D], D, 256)]
    w = a["w_in_2"][0]
    cols = [w[:, 0:1536]] + [w[:, 1536:6144]] + [w[:, 6144:8192]]
    parts.append(chunked(np.concatenate(cols, axis=1), D, 256))
    parts += [chunked(a["w_a_out_2"][0], 512, 512), chunked(a["w_b_out_2"][0], 512, 512),
              chunked(a["w_mix_out_2"][0], D, 256)]
    up, step = chunked(a["w_up_2"][0], D, 256), 0
    for steps in GROUPS2:
        for s in range(step, step + steps):
            parts += [up[s:s + 1], up[11 + s:12 + s]]
        parts.append(padded(chunked(a["w_down_2"][0][step * 256:(step + steps) * 256], steps * 256, 256)))
        step += steps
    out = np.concatenate(parts)
    assert out.shape == (N_CHUNKS, 128, CHUNK), (out.shape, N_CHUNKS)
    return out


def features(v):
    v = v.reshape(-1, v.shape[-1] // 128, 128)
    return v.transpose(2, 0, 1).reshape(128, -1)


def feature_vectors(a):
    cond = np.stack([a["c"][0], a["c_ctx"]])
    out = {"c": features(cond).reshape(128, 2, 8).transpose(0, 2, 1).reshape(128, 16)}
    by_channel = lambda w: features(w).reshape(128, w.shape[0], -1).transpose(0, 2, 1).reshape(128, -1)
    for l in range(DEPTH):
        out["g_pre_mix", l], out["g_pre_mlp", l] = features(a["g_pre_mix"][l]), features(a["g_pre_mlp"][l])
        out["w_sc", l], out["cf_w", l] = by_channel(a["w_sc"][l]), by_channel(a["cf_w_dw"][l])
        out["g_q", l], out["g_kv", l] = features(a["g_q"][l]), features(a["g_kv"][l])
        out["cf_b", l] = features(a["cf_b_dw"][l])
        out["ln_g", l], out["ln_b", l] = features(a["cf_ln_g"][l]), features(a["cf_ln_b"][l])
    out["pre_mix2"], out["pre_ffn2"] = features(a["pre_mix_g_2"][0]), features(a["pre_ffn_g_2"][0])
    out["conv_w2"], out["conv_b2"] = features(a["conv_w_2"][0]), features(a["conv_b_2"][0])
    out["head_g2"] = features(a["diff_head_g_2"][0])
    return np.concatenate([out[key] for key in FC if key != "n"], axis=1)


def small_weights(a):
    out = []
    for l in range(DEPTH):
        uq = a["w_uq"][l].reshape(256, HEADS, 96)
        uq = np.concatenate([uq[:, :, :64].reshape(256, 256), uq[:, :, 64:].reshape(256, 128)], axis=1)
        ukv = a["w_ukv"][l].reshape(128, HEADS, 2, 64).transpose(0, 2, 1, 3).reshape(128, 512)
        out.append(np.concatenate([chunked(uq, 256, 384)[0], ukv, chunked(a["cf_w_pw"][l], 256, 256)[0]], axis=1))
    return np.stack(out)


def shape_constants():
    c = np.zeros((128, C_N), np.float32)
    p = np.arange(128)
    c[:, C_IDENT:C_IDENT + 128] = np.eye(128)
    c[:, C_ONES:C_ONES + 128] = 1
    c[p ^ 8, C_SWAP + p] = 1
    inv = np.float32(10000.0) ** (-np.arange(8, dtype=np.float32) / np.float32(8))
    tok = np.arange(SEQ)
    grid = np.stack([tok // GRID, tok % GRID]).astype(np.float32)
    ang = grid[(p % 32) // 16] * inv[p % 8][:, None]
    c[:, C_COS:C_COS + 256] = np.cos(ang)
    c[:, C_SIN:C_SIN + 256] = np.sin(ang) * np.where(p % 16 < 8, -1, 1)[:, None]
    inv = lambda dim: np.float32(10000.0) ** (-np.arange(0, dim, 2, dtype=np.float32) / np.float32(dim))
    c[:, C_INV], c[:, C_INV + 1] = inv(64)[p % 32], inv(128)[p % 64]
    c[:, C_EPS] = EPS
    c[:, C_SIGN], c[:, C_SIGN + 1] = np.where(p // 32 % 2, -1, 1), np.where(p // 64, -1, 1)
    qc, kc = p % GRID, np.arange(256) % GRID
    start = np.clip(qc - 8, 0, GRID - 16)[:, None]
    window = np.where((kc >= start) & (kc < start + 16), 0, MASKED).astype(np.float32)
    q = (p[:, None] + np.array([0, 128]))[:, :, None, None]
    rel = q - np.arange(256)
    masks = [rel >= 0, (rel >= 0) & (rel <= 128), (rel >= 0) & (rel % 4 == 0), (rel >= 0) & (rel % 16 == 0)]
    masks = np.where(np.concatenate(masks, axis=2), 0, MASKED).astype(np.float32)
    masks2 = np.concatenate([masks[:, :, 0].reshape(128, 512), masks[:, :, 1:].reshape(128, 1536)], axis=1)
    return c, window, masks2


def kernel(**inputs):
    import concourse.bacc as bacc
    from concourse.bass_utils import run_bass_kernel_spmd

    a = {name: np.asarray(v) for name, v in inputs.items()}
    consts, window, masks2 = shape_constants()
    arrays = {
        "x": a["x"], "ctx": a["ctx"], "feats": feature_vectors(a), "small": small_weights(a),
        "b_mod": a["b_mod"], "rpb": a["na_rpb"].reshape(DEPTH * HEADS, RPB), "lam": a["diff_lambda_2"].reshape(-1),
        "gpost": np.stack([a["g_post_mix"][0], a["g_post_mlp"][0], a["g_post_mix"][1], a["g_post_mlp"][1],
                           a["post_mix_g_2"][0], a["post_ffn_g_2"][0]]),
        "pos": a["positions_2"], "consts": consts, "window": window, "masks2": masks2,
        "stream": weight_stream(a),
    }
    nc = bacc.Bacc("TRN2", target_bir_lowering=False, num_devices=1)
    t = {}
    for name, v in arrays.items():
        arrays[name] = v = np.ascontiguousarray(v)
        t[name] = nc.dram_tensor(f"in_{name}", v.shape, mybir.dt.from_np(v.dtype), kind="ExternalInput").ap()
    t["rpb_rows"] = nc.dram_tensor("rpb_rows", (DEPTH * HEADS, GRID, RPB), f32, kind="Internal").ap()
    t["out"] = nc.dram_tensor("out", (1, SEQ, D), f32, kind="ExternalOutput").ap()
    build(nc, t)
    got = run_bass_kernel_spmd(nc, [{f"in_{name}": v for name, v in arrays.items()}], core_ids=[0])
    return got.results[0]["out"]
```
